# Optimizing a Trainium2 kernel written in Bass

```python
import math
import jax, jax.numpy as jnp
from jax import lax
import numpy as np

D_MODEL = 1024
BATCH = 1
SEQ = 512
DEPTH = 1

CHUNK = 64
HEAD_DIM = 64
N_HEADS_FOX = 8
N_HEADS_CHUNK = 8
WIDTH_FOX = N_HEADS_FOX * HEAD_DIM
WIDTH_CHUNK = N_HEADS_CHUNK * HEAD_DIM
LEFT_CHUNKS = 8
BAND_CHUNKS = LEFT_CHUNKS + 1
REL_CLIP = 128
Q_BLOCK = 128
D_FF = 2816
CONV_WIDTH = 3
LN_EPS = 1e-5
N_MOD = 6
PROJ_SIZES = (WIDTH_FOX, WIDTH_FOX, WIDTH_FOX, N_HEADS_FOX,
              WIDTH_CHUNK, WIDTH_CHUNK, WIDTH_CHUNK, D_MODEL, D_MODEL)
PROJ_COLS = sum(PROJ_SIZES)


def _layer_norm(x, gain=None, bias=None):
    xf = x.astype(jnp.float32)
    mu = jnp.mean(xf, axis=-1, keepdims=True)
    var = jnp.mean(jnp.square(xf - mu), axis=-1, keepdims=True)
    y = (xf - mu) * lax.rsqrt(var + LN_EPS)
    if gain is not None:
        y = y * gain.astype(jnp.float32) + bias.astype(jnp.float32)
    return y.astype(x.dtype)

def _forgetting_attention(q, k, v, f_logit):
    b, s, h, dh = q.shape
    n_blk = s // Q_BLOCK
    log_f = jax.nn.log_sigmoid(f_logit.astype(jnp.float32))
    cum = jnp.cumsum(log_f, axis=1).transpose(0, 2, 1)
    scale = 1.0 / math.sqrt(dh)
    k_pos = jnp.arange(s)
    q_blocks = q.reshape(b, n_blk, Q_BLOCK, h, dh).transpose(1, 0, 2, 3, 4)
    cum_blocks = cum.reshape(b, h, n_blk, Q_BLOCK).transpose(2, 0, 1, 3)
    neg = jnp.finfo(jnp.float32).min

    def block(args):
        qb, cq, i = args
        q_pos = i * Q_BLOCK + jnp.arange(Q_BLOCK)
        logits = jnp.einsum('bqhd,bkhd->bhqk', qb, k).astype(jnp.float32) * scale
        logits = logits + cq[:, :, :, None] - cum[:, :, None, :]
        mask = k_pos[None, :] <= q_pos[:, None]
        logits = jnp.where(mask[None, None], logits, neg)
        p = jax.nn.softmax(logits, axis=-1).astype(v.dtype)
        return jnp.einsum('bhqk,bkhd->bqhd', p, v)

    out = lax.map(block, (q_blocks, cum_blocks, jnp.arange(n_blk)))
    return out.transpose(1, 0, 2, 3, 4).reshape(b, s, h * dh)

def _chunk_band_attention(q, k, v, rel_table):
    b, s, h, dh = q.shape
    n_c = s // CHUNK
    band = BAND_CHUNKS * CHUNK
    qc = q.reshape(b, n_c, CHUNK, h, dh)
    pad = ((0, 0), (LEFT_CHUNKS, 0), (0, 0), (0, 0), (0, 0))
    kp = jnp.pad(k.reshape(b, n_c, CHUNK, h, dh), pad)
    vp = jnp.pad(v.reshape(b, n_c, CHUNK, h, dh), pad)
    band_idx = jnp.arange(n_c)[:, None] + jnp.arange(BAND_CHUNKS)[None, :]
    kb = kp[:, band_idx].reshape(b, n_c, band, h, dh)
    vb = vp[:, band_idx].reshape(b, n_c, band, h, dh)
    valid = jnp.repeat(band_idx >= LEFT_CHUNKS, CHUNK, axis=1)
    q_off = LEFT_CHUNKS * CHUNK + np.arange(CHUNK)
    rel = np.clip(q_off[:, None] - np.arange(band)[None, :], -REL_CLIP, REL_CLIP) + REL_CLIP
    bias = rel_table[:, rel].astype(jnp.float32)
    scale = 1.0 / math.sqrt(dh)
    logits = jnp.einsum('bcqhd,bckhd->bchqk', qc, kb).astype(jnp.float32) * scale
    logits = logits + bias[None, None]
    logits = jnp.where(valid[None, :, None, None, :], logits, jnp.finfo(jnp.float32).min)
    p = jax.nn.softmax(logits, axis=-1).astype(v.dtype)
    out = jnp.einsum('bchqk,bckhd->bcqhd', p, vb)
    return out.reshape(b, s, h * dh)

def _causal_depthwise_conv(u, w, bias):
    s = u.shape[1]
    up = jnp.pad(u, ((0, 0), (CONV_WIDTH - 1, 0), (0, 0)))
    y = bias
    for j in range(CONV_WIDTH):
        y = y + w[j] * up[:, j:j + s]
    return y

def first_inputs(seed: int = 0) -> dict:
    key = jax.random.key(seed)
    ks = jax.random.split(key, 20)
    beta = (8.0 * DEPTH) ** -0.25
    f32 = jnp.float32
    nrm = lambda k, shape: jax.random.normal(k, shape, f32)
    col_scale = np.concatenate([
        np.ones(2 * WIDTH_FOX), beta * np.ones(WIDTH_FOX), 0.5 * np.ones(N_HEADS_FOX),
        np.ones(2 * WIDTH_CHUNK), beta * np.ones(WIDTH_CHUNK), np.ones(2 * D_MODEL)]).astype(np.float32)
    w_in = nrm(ks[2], (DEPTH, D_MODEL, PROJ_COLS)) * (D_MODEL ** -0.5) * jnp.asarray(col_scale)
    b_f = jnp.linspace(1.0, 5.0, N_HEADS_FOX, dtype=f32)[None, :] + 0.1 * nrm(ks[3], (DEPTH, N_HEADS_FOX))
    rel_bias = 0.5 * nrm(ks[4], (DEPTH, N_HEADS_CHUNK, 2 * REL_CLIP + 1))
    w_br_fox = nrm(ks[5], (DEPTH, WIDTH_FOX, D_MODEL)) * WIDTH_FOX ** -0.5
    w_br_chunk = nrm(ks[6], (DEPTH, WIDTH_CHUNK, D_MODEL)) * WIDTH_CHUNK ** -0.5
    w_out = nrm(ks[7], (DEPTH, D_MODEL, D_MODEL)) * (D_MODEL ** -0.5) * beta
    w_up = nrm(ks[8], (DEPTH, D_MODEL, 2 * D_FF)) * D_MODEL ** -0.5
    conv_w = 0.3 * nrm(ks[9], (DEPTH, CONV_WIDTH, 2 * D_FF)) + jnp.array([0.0, 0.0, 1.0], f32)[None, :, None]
    conv_b = 0.01 * nrm(ks[10], (DEPTH, 2 * D_FF))
    w_down = nrm(ks[11], (DEPTH, D_FF, D_MODEL)) * (D_FF ** -0.5) * beta
    w_ada = 0.2 * nrm(ks[12], (DEPTH, D_MODEL, N_MOD * D_MODEL)) * D_MODEL ** -0.5
    b_ada = 0.01 * nrm(ks[13], (DEPTH, N_MOD * D_MODEL))
    ln1_g = 1.0 + 0.05 * nrm(ks[14], (DEPTH, D_MODEL))
    ln1_b = 0.01 * nrm(ks[15], (DEPTH, D_MODEL))
    ln2_g = 1.0 + 0.05 * nrm(ks[16], (DEPTH, D_MODEL))
    ln2_b = 0.01 * nrm(ks[17], (DEPTH, D_MODEL))
    x = nrm(ks[0], (BATCH, SEQ, D_MODEL))
    c = nrm(ks[1], (BATCH, D_MODEL))
    return {"x": x, "c": c, "w_in": w_in, "b_f": b_f, "rel_bias": rel_bias,
            "w_br_fox": w_br_fox, "w_br_chunk": w_br_chunk, "w_out": w_out,
            "w_up": w_up, "conv_w": conv_w, "conv_b": conv_b, "w_down": w_down,
            "w_ada": w_ada, "b_ada": b_ada, "ln1_g": ln1_g, "ln1_b": ln1_b,
            "ln2_g": ln2_g, "ln2_b": ln2_b}

def first_block(x, c, w_in, b_f, rel_bias, w_br_fox, w_br_chunk, w_out, w_up, conv_w,
              conv_b, w_down, w_ada, b_ada, ln1_g, ln1_b, ln2_g, ln2_b):
    alpha = (2.0 * DEPTH) ** 0.25
    b, s, _ = x.shape
    split_points = list(np.cumsum(PROJ_SIZES)[:-1])
    cond = jax.nn.silu(c)
    for l in range(DEPTH):
        mod = cond @ w_ada[l] + b_ada[l]
        sh1, sc1, g1, sh2, sc2, g2 = jnp.split(mod[:, None, :], N_MOD, axis=-1)

        h = _layer_norm(x) * (1.0 + sc1) + sh1
        proj = h @ w_in[l]
        q_a, k_a, v_a, f_a, q_c, k_c, v_c, gate_a, gate_c = jnp.split(proj, split_points, axis=-1)
        heads_a = lambda t: t.reshape(b, s, N_HEADS_FOX, HEAD_DIM)
        heads_c = lambda t: t.reshape(b, s, N_HEADS_CHUNK, HEAD_DIM)
        o_a = _forgetting_attention(heads_a(q_a), heads_a(k_a), heads_a(v_a), f_a + b_f[l])
        o_c = _chunk_band_attention(heads_c(q_c), heads_c(k_c), heads_c(v_c), rel_bias[l])
        merged = (jax.nn.sigmoid(gate_a) * (o_a @ w_br_fox[l])
                  + jax.nn.sigmoid(gate_c) * (o_c @ w_br_chunk[l]))
        mix = merged @ w_out[l]
        x = _layer_norm(alpha * x + (1.0 + g1) * mix, ln1_g[l], ln1_b[l])

        h = _layer_norm(x) * (1.0 + sc2) + sh2
        u = _causal_depthwise_conv(h @ w_up[l], conv_w[l], conv_b[l])
        a, val = jnp.split(u, 2, axis=-1)
        y = (jax.nn.silu(a) * val) @ w_down[l]
        x = _layer_norm(alpha * x + (1.0 + g2) * y, ln2_g[l], ln2_b[l])
    return x


DEPTH_2 = 2

N_MIXERS = 2
N_META = 16
N_HEADS = 16
QK_NOPE_DIM = 64
QK_ROPE_DIM = 32
QK_HEAD_DIM = QK_NOPE_DIM + QK_ROPE_DIM
V_HEAD_DIM = 64
Q_LORA_RANK = 384
KV_LORA_RANK = 256
ROPE_THETA = 10000.0
POOL_WINDOWS = (2, 4, 8, 16)
N_POOL_GROUPS = len(POOL_WINDOWS)
POOL_GROUP_DIM = D_MODEL // N_POOL_GROUPS
NORM_EPS = 1e-6
N_MLA_LAYERS = len(range(0, DEPTH_2, N_MIXERS))
N_POOL_LAYERS = DEPTH_2 - N_MLA_LAYERS


def rmsnorm(x, g):
    xf = x.astype(jnp.float32)
    y = xf * lax.rsqrt(jnp.mean(xf * xf, axis=-1, keepdims=True) + NORM_EPS)
    return (y * g.astype(jnp.float32)).astype(x.dtype)

def rope_tables(length):
    inv = 1.0 / (ROPE_THETA ** (jnp.arange(0, QK_ROPE_DIM, 2, dtype=jnp.float32) / QK_ROPE_DIM))
    ang = jnp.arange(length, dtype=jnp.float32)[:, None] * inv[None, :]
    return jnp.cos(ang), jnp.sin(ang)

def apply_rope(x, cos, sin):
    xf = x.astype(jnp.float32)
    x1, x2 = jnp.split(xf, 2, axis=-1)
    c = cos[None, :, None, :]
    s = sin[None, :, None, :]
    return jnp.concatenate([x1 * c - x2 * s, x2 * c + x1 * s], axis=-1).astype(x.dtype)

def mla_mixer(h, w_dqkv, q_norm, w_uq, kv_norm, w_ukv, w_o, cos, sin):
    B, L, _ = h.shape
    a = h @ w_dqkv
    c_q, c_kv, k_rope = jnp.split(a, [Q_LORA_RANK, Q_LORA_RANK + KV_LORA_RANK], axis=-1)
    c_q = rmsnorm(c_q, q_norm)
    c_kv = rmsnorm(c_kv, kv_norm)
    q = (c_q @ w_uq).reshape(B, L, N_HEADS, QK_HEAD_DIM)
    q = jnp.concatenate([q[..., :QK_NOPE_DIM], apply_rope(q[..., QK_NOPE_DIM:], cos, sin)], axis=-1)
    kv = (c_kv @ w_ukv).reshape(B, L, N_HEADS, QK_NOPE_DIM + V_HEAD_DIM)
    k_nope, v = jnp.split(kv, [QK_NOPE_DIM], axis=-1)
    k_rope = apply_rope(k_rope[:, :, None, :], cos, sin)
    k = jnp.concatenate([k_nope, jnp.broadcast_to(k_rope, (B, L, N_HEADS, QK_ROPE_DIM))], axis=-1)
    scale = QK_HEAD_DIM ** -0.5
    outs = []
    for start in range(0, L, Q_BLOCK):
        end = start + Q_BLOCK
        qb = q[:, start:end]
        kb = k[:, :end]
        vb = v[:, :end]
        s = jnp.einsum('bqhd,bkhd->bhqk', qb, kb).astype(jnp.float32) * scale
        mask = jnp.arange(start, end)[:, None] >= jnp.arange(end)[None, :]
        s = jnp.where(mask[None, None], s, -jnp.inf)
        p = jax.nn.softmax(s, axis=-1).astype(vb.dtype)
        outs.append(jnp.einsum('bhqk,bkhd->bqhd', p, vb))
    o = jnp.concatenate(outs, axis=1).reshape(B, L, N_HEADS * V_HEAD_DIM)
    return o @ w_o

def pool_mixer(h, w_group, scale):
    B, L, D = h.shape
    hf = h.astype(jnp.float32).reshape(B, L, N_POOL_GROUPS, POOL_GROUP_DIM)
    csum = jnp.cumsum(hf, axis=1)
    t = jnp.arange(1, L + 1, dtype=jnp.float32)
    means = []
    for g, w in enumerate(POOL_WINDOWS):
        cg = csum[:, :, g, :]
        prev = jnp.pad(cg[:, :L - w], ((0, 0), (w, 0), (0, 0)))
        cnt = jnp.minimum(t, float(w))[None, :, None]
        means.append((cg - prev) / cnt)
    pooled = jnp.stack(means, axis=2)
    mixed = (pooled - hf).astype(h.dtype)
    y = jnp.einsum('blgc,gcd->blgd', mixed, w_group).reshape(B, L, D)
    return y * scale

def conv_ffn(h, w_up, conv_w, conv_b, w_down):
    L = h.shape[1]
    u = h @ w_up
    up = jnp.pad(u, ((0, 0), (CONV_WIDTH - 1, 0), (0, 0)))
    u = conv_b + sum(conv_w[j] * up[:, j:j + L] for j in range(CONV_WIDTH))
    gate, val = jnp.split(u, 2, axis=-1)
    return (jax.nn.silu(gate) * val) @ w_down

def second_inputs(seed: int = 0) -> dict:
    key = jax.random.key(seed)
    ks = jax.random.split(key, 24)
    f32 = jnp.float32

    def nrm(k, shape, fan_in):
        return jax.random.normal(k, shape, f32) * (fan_in ** -0.5)

    def gain(k, shape, s=0.05):
        return 1.0 + s * jax.random.normal(k, shape, f32)

    return {
        "x": jax.random.normal(ks[0], (BATCH, SEQ, D_MODEL), f32),
        "meta_tokens": jax.random.normal(ks[1], (N_META, D_MODEL), f32),
        "norm_mix_pre": gain(ks[2], (DEPTH_2, D_MODEL)),
        "norm_mix_post": gain(ks[3], (DEPTH_2, D_MODEL)),
        "norm_ffn_pre": gain(ks[4], (DEPTH_2, D_MODEL)),
        "norm_ffn_post": gain(ks[5], (DEPTH_2, D_MODEL)),
        "mla_w_dqkv": nrm(ks[6], (N_MLA_LAYERS, D_MODEL, Q_LORA_RANK + KV_LORA_RANK + QK_ROPE_DIM), D_MODEL),
        "mla_q_norm": gain(ks[7], (N_MLA_LAYERS, Q_LORA_RANK)),
        "mla_w_uq": nrm(ks[8], (N_MLA_LAYERS, Q_LORA_RANK, N_HEADS * QK_HEAD_DIM), Q_LORA_RANK),
        "mla_kv_norm": gain(ks[9], (N_MLA_LAYERS, KV_LORA_RANK)),
        "mla_w_ukv": nrm(ks[10], (N_MLA_LAYERS, KV_LORA_RANK, N_HEADS * (QK_NOPE_DIM + V_HEAD_DIM)), KV_LORA_RANK),
        "mla_w_o": nrm(ks[11], (N_MLA_LAYERS, N_HEADS * V_HEAD_DIM, D_MODEL), N_HEADS * V_HEAD_DIM),
        "pool_w_group": nrm(ks[12], (N_POOL_LAYERS, N_POOL_GROUPS, POOL_GROUP_DIM, POOL_GROUP_DIM), POOL_GROUP_DIM),
        "pool_scale": gain(ks[13], (N_POOL_LAYERS, D_MODEL), 0.1),
        "ffn_w_up": nrm(ks[14], (DEPTH_2, D_MODEL, 2 * D_FF), D_MODEL),
        "ffn_conv_w": nrm(ks[15], (DEPTH_2, CONV_WIDTH, 2 * D_FF), CONV_WIDTH),
        "ffn_conv_b": 0.01 * jax.random.normal(ks[16], (DEPTH_2, 2 * D_FF), f32),
        "ffn_w_down": nrm(ks[17], (DEPTH_2, D_FF, D_MODEL), D_FF),
    }

def second_block(x, meta_tokens, norm_mix_pre, norm_mix_post, norm_ffn_pre, norm_ffn_post,
              mla_w_dqkv, mla_q_norm, mla_w_uq, mla_kv_norm, mla_w_ukv, mla_w_o,
              pool_w_group, pool_scale, ffn_w_up, ffn_conv_w, ffn_conv_b, ffn_w_down):
    B, S, D = x.shape
    L = N_META + S
    L_pad = -(-L // Q_BLOCK) * Q_BLOCK
    meta = jnp.broadcast_to(meta_tokens.astype(x.dtype)[None], (B, N_META, D))
    h = jnp.concatenate([meta, x, jnp.zeros((B, L_pad - L, D), x.dtype)], axis=1)
    cos, sin = rope_tables(L_pad)
    for i in range(DEPTH_2):
        j = i // N_MIXERS
        a = rmsnorm(h, norm_mix_pre[i])
        if i % N_MIXERS == 0:
            m = mla_mixer(a, mla_w_dqkv[j], mla_q_norm[j], mla_w_uq[j], mla_kv_norm[j],
                          mla_w_ukv[j], mla_w_o[j], cos, sin)
        else:
            m = pool_mixer(a, pool_w_group[j], pool_scale[j])
        h = h + rmsnorm(m, norm_mix_post[i])
        f = conv_ffn(rmsnorm(h, norm_ffn_pre[i]), ffn_w_up[i], ffn_conv_w[i], ffn_conv_b[i], ffn_w_down[i])
        h = h + rmsnorm(f, norm_ffn_post[i])
    return h[:, N_META:L]


def setup_inputs(seed=0):
    out = dict(first_inputs(seed))
    for name, value in second_inputs(seed + 1).items():
        if name != "x":
            out[name + "_2"] = value
    return out


def reference(
    x, c, w_in, b_f, rel_bias, w_br_fox, w_br_chunk, w_out, w_up, conv_w, conv_b, w_down, w_ada,
    b_ada, ln1_g, ln1_b, ln2_g, ln2_b, meta_tokens_2, norm_mix_pre_2, norm_mix_post_2,
    norm_ffn_pre_2, norm_ffn_post_2, mla_w_dqkv_2, mla_q_norm_2, mla_w_uq_2, mla_kv_norm_2,
    mla_w_ukv_2, mla_w_o_2, pool_w_group_2, pool_scale_2, ffn_w_up_2, ffn_conv_w_2,
    ffn_conv_b_2, ffn_w_down_2,
):
    x = first_block(
        x, c, w_in, b_f, rel_bias, w_br_fox, w_br_chunk, w_out, w_up, conv_w, conv_b, w_down,
        w_ada, b_ada, ln1_g, ln1_b, ln2_g, ln2_b,
    )
    return second_block(
        x, meta_tokens_2, norm_mix_pre_2, norm_mix_post_2, norm_ffn_pre_2, norm_ffn_post_2,
        mla_w_dqkv_2, mla_q_norm_2, mla_w_uq_2, mla_kv_norm_2, mla_w_ukv_2, mla_w_o_2,
        pool_w_group_2, pool_scale_2, ffn_w_up_2, ffn_conv_w_2, ffn_conv_b_2, ffn_w_down_2,
    )


_drawn_inputs = setup_inputs


def setup_inputs(seed=0):
    import zlib

    import numpy as np

    out = dict(_drawn_inputs(seed))
    spreads = {}
    factors = {'rel_bias': 2.98, 'conv_b': 5.038, 'b_ada': 2.886, 'ffn_conv_b_2': 5.217}
    for name, (base, spread) in spreads.items():
        noise = np.random.default_rng([zlib.crc32(name.encode()), seed]).standard_normal(out[name].shape)
        drawn = base * np.exp(spread * noise) if base else spread * noise
        out[name] = __import__('jax').numpy.asarray(drawn.astype(out[name].dtype))
    for name, factor in factors.items():
        out[name] = (out[name] * factor).astype(out[name].dtype)
    return out
```

```python
from contextlib import ExitStack

import concourse.bass as bass
from concourse import mybir

P = 128
D = 1024
KD = D // P
S1 = 512
META = 16
S2 = S1 + META
H1 = 8
H2 = 16
FF = 2816
KF = FF // P
QB = 128
RQ, RKV = 384, 256
NOPE, ROPE = 64, 32
POOLS = (2, 4, 8, 16)
ALPHA = 2.0 ** 0.25
LN_EPS, RMS_EPS = 1e-5, 1e-6

BLK = 1024
C_PAD = P - META
SHIFT = 16
RING = 4

F32 = mybir.dt.float32
F32R = mybir.dt.float32r
BF16 = mybir.dt.bfloat16
ALU = mybir.AluOpType
ACT = mybir.ActivationFunctionType
AX = mybir.AxisListType
ds = bass.ds

STAGES = [
    ("forget", 1, 1), ("qk", 4, 4), ("v", 4, 2), ("merge", 12, 2), ("out", 4, 2),
    ("up_a", 4, 11), ("down_a", 12, 2),
    ("dqkv", 6, 1), ("uq", 4, 2), ("uk", 2, 1), ("uv", 2, 1), ("wo", 4, 2),
    ("up_b", 4, 11), ("down_b", 12, 2), ("pool", 2, 1), ("up_c", 4, 11), ("down_c", 12, 2),
]
DOWN_ROWS = (2,) * (KF - 12) + (1,) * (24 - KF)
BLK0, _n = {}, 0
for _name, _b, _t in STAGES:
    BLK0[_name] = _n
    _n += _b * _t
NBLK = _n
NSTREAM = NBLK + RING

BATCH = {
    "forget": [(1, 0, 0)], "qk": [(4, 3, 0)], "v": [(4, 3, 0)],
    "merge": [(4, 3, 0), (4, 5, 0), (4, 9, 0), (4, 11, 0)],
    "out": [(4, 3, 0)], "up_a": [(4, 3, 0)], "down_a": [(4, 11, 0)], "dqkv": [(4, 3, 0), (2, 5, 0)],
    "uq": [(2, 0, 0), (2, 1, 2), (2, 2, 0), (2, 3, 2)], "uk": [(4, 0, 0), (4, 1, 0)],
    "uv": [(5, 0, 0), (5, 1, 0)], "wo": [(4, 3, 0)],
    "up_b": [(4, 3, 0)], "down_b": [(4, 11, 0)], "pool": [(4, 0, 0), (4, 1, 0)], "up_c": [(4, 3, 0)],
    "down_c": [(4, 11, 0)],
}
NB = {name: b for name, b, _ in STAGES}
FULL0, FREE0, _f, _u = {}, {}, 0, [0, 0, 0, 0]


def tiles_in(name, k, before=None):
    return sum(1 for n, _, p in BATCH[name][:before] for j in range(n) if (p + j) % 4 == k)


for _name, _b, _t in STAGES:
    FULL0[_name], FREE0[_name] = _f, list(_u)
    _f += sum(n - 1 for n, _, _ in BATCH[_name]) * _t
    for _k in range(4):
        _u[_k] += tiles_in(_name, _k) * _t
FREE_END = list(_u)


def free_before(name, batch, i, g=0):
    k = (BATCH[name][batch][2] + i) % 4
    return g * tiles_in(name, k) + (FREE0[name][k] + tiles_in(name, k, batch) + i // 4)


TILES1 = [(i * QB, QB, (i + 1) * QB) for i in range(S1 // QB)]
TILES2 = TILES1[:3] + [(384, 72, 512), (456, 72, S2)]
KEYS1 = [(i * QB, QB) for i in range(S1 // QB)]
KEYS2 = KEYS1 + [(S1, META)]
ATT = {
    "fox": (TILES1, KEYS1, S1, H1 // 2, 0, 0, 0),
    "chunk": (TILES1, KEYS1, S1, H1 // 2, 0, 32, 4),
    "mla": (TILES2, KEYS2, S2, H2 // 2, 256, 64, 8),
}
STG_ACT = {"fox": 4, "chunk": 5, "mla": 6}
STG_POOL = {"fox": 4, "chunk": 5, "mla": 6}
STG_ACT0 = {"fox": 0, "chunk": 16, "mla": 36}
STG_POOL0 = {"fox": 0, "chunk": 16, "mla": 36}
COL2 = 248
HALF2 = S2 // 2

VEC, _v = {}, 0
for _name, _w in [("c", 8), ("b_ada", 48), ("ln1_g", 8), ("ln1_b", 8), ("ln2_g", 8), ("ln2_b", 8),
                  ("b_f", 1), ("qk_scale", 4), ("rel_far", 8), ("sel", 8),
                  ("mix_pre", 16), ("mix_post", 16), ("ffn_pre", 16), ("ffn_post", 16),
                  ("q_norm", 3), ("kv_norm", 2), ("pool_scale", 8), ("eps", 2),
                  ("cnt", 64), ("conv", 3 * 4 * 2 * KF)]:
    VEC[_name] = _v
    _v += _w
NVEC = _v
SET_UP = 14
ADA_ORDER = (1, 0, 2, 3, 4, 5)


def program(nc, xT, meta, stream, ada, vecs, consts, rel, rope, yT):
    with ExitStack() as ctx:
        def sb(name, cols, dt=F32):
            return ctx.enter_context(nc.sbuf_tensor(name, [P, cols], dt))

        def region(*tensors):
            with ExitStack() as over:
                return [over.enter_context(nc.sbuf_tensor(n, [P, c], dt)) for n, c, dt in tensors]

        def sem(name):
            return ctx.enter_context(nc.semaphore(name))

        X = sb("X", KD * S2)
        w_raw = sb("w_raw", RING * BLK)
        w_hi = sb("w_hi", RING * BLK, F32R)
        w_lo = sb("w_lo", RING * BLK, F32R)
        (work_r,) = region(("work_r", 4 * S2, F32R))
        work = sb("work", 4 * S2)
        RS = sb("RS", S2)
        vec = sb("vec", NVEC)
        mod = sb("mod", 48)
        modp = sb("modp", 48)
        ident = sb("ident", P)
        ones = sb("ones", P)
        ident_bf = sb("ident_bf", P, BF16)
        causal_bf = sb("causal_bf", P, BF16)
        chunk_bf = sb("chunk_bf", P, BF16)
        ident_r = sb("ident_r", P, F32R)
        cond = sb("cond", 8)
        small = sb("small", 8)
        (m_out,) = region(("m_out", KD * S2, F32))
        (v_raw2,) = region(("v_raw2", 5 * D, F32))
        H_hi = sb("H_hi", KD * S2, F32R)
        H_lo = sb("H_lo", KD * S2, F32R)
        (_, QK, XC, ada_w, ada_acc) = region(
            ("shift", SHIFT, F32),             ("QK", 16 * S1, F32), ("XC", KD * S2, F32), ("ada_w", 4 * D, F32), ("ada_acc", D, F32))
        (_, QK_, v_raw, q_hi, q_lo, k_hi, k_lo, v_hi, v_lo, db, PT_hi, PT_lo, rel_raw, rel_hi, rel_lo,
         sel_bf, F_bf, F_tmp) = region(
            ("shift_", SHIFT, F32), ("QK_", 16 * S1, F32), ("v_raw", 4 * D, F32), ("q_hi", S1, F32R), ("q_lo", S1, F32R),
            ("k_hi", S1, F32R), ("k_lo", S1, F32R), ("v_hi", 2 * 4 * P, F32R), ("v_lo", 2 * 4 * P, F32R),
            ("db", 2 * P, F32), ("PT_hi", 4 * S1, F32R), ("PT_lo", 4 * S1, F32R),
            ("rel_raw", 2 * 256, F32), ("rel_hi", 2 * 256, F32R), ("rel_lo", 2 * 256, F32R),
            ("sel_bf", 8 * P, BF16), ("F_bf", S1, BF16), ("F_tmp", S1, BF16))
        (O_split, mg_hi, mg_lo, gate, acc) = region(
            ("O_split", SHIFT + 16 * S1, F32R), ("mg_hi", KD * S1, F32R), ("mg_lo", KD * S1, F32R),
            ("gate", 4 * S1, F32), ("acc", 4 * S1, F32))
        mid_hi, mid_lo = region(("mid_hi", KF * S2, F32R), ("mid_lo", KF * S2, F32R))
        (Q2, K2, c_hi, c_lo, cos_t, sin_t, kr) = region(
            ("Q2", H2 * S2, F32), ("K2", KD * S2, F32), ("c_hi", 5 * S2 + C_PAD, F32R),
            ("c_lo", 5 * S2 + C_PAD, F32R),
            ("cos_t", S2, F32), ("sin_t", S2, F32), ("kr", S2, F32))
        (Q2_, K2_, q2_hi, q2_lo, k2_hi, k2_lo, v2_hi, v2_lo, db2, PT2_hi, PT2_lo) = region(
            ("Q2_", H2 * S2, F32), ("K2_", KD * S2, F32), ("q2_hi", 2 * S2, F32R), ("q2_lo", 2 * S2, F32R),
            ("k2_hi", 2 * S2, F32R), ("k2_lo", 2 * S2, F32R), ("v2_hi", 2 * 5 * P, F32R),
            ("v2_lo", 2 * 5 * P, F32R), ("db2", 2 * P, F32), ("PT2_hi", 4 * S2, F32R), ("PT2_lo", 4 * S2, F32R))
        (OQ_lo, OK_hi) = region(("OQ_lo", H2 * S2 - SHIFT, F32R), ("OK_hi", SHIFT + KD * S2, F32R))
        (pool_a, pool_s, pool_c) = region(
            ("pool_a", 2 * S2, F32), ("pool_s", 2 * S2, F32), ("pool_c", 4 * P, F32))
        PS = ctx.enter_context(nc.psum_tensor("PS", [P, 4, 2 * 512], F32))

        w_in = [sem(f"w_in{i}") for i in range(RING)]
        w_hi_ok, w_lo_ok, w_used = sem("w_hi_ok"), sem("w_lo_ok"), sem("w_used")
        full = sem("full")
        free = [sem(f"free{i}") for i in range(4)]
        x_in, cst_in, set_up = sem("x_in"), sem("cst_in"), sem("set_up")
        ada_in = [sem(f"ada_in{i}") for i in range(4)]
        ada_used, ada_mm, cond_ok = sem("ada_used"), sem("ada_mm"), sem("cond_ok")
        n_mean, n_xc, n_sq, n_sq_used, n_sum, n_r0, n_rs = (
            sem(s) for s in ("n_mean", "n_xc", "n_sq", "n_sq_used", "n_sum", "n_r0", "n_rs"))
        t_ok, t_hi, h_ok = sem("t_ok"), sem("t_hi"), sem("h_ok")
        x_ok = sem("x_ok")
        dve, act, pool = sem("dve_step"), sem("act_step"), sem("pool_step")
        f_z, f_e, f_ln, f_ok = sem("f_z"), sem("f_e"), sem("f_ln"), sem("f_ok")
        q_ok, v_ok = sem("q_ok"), sem("v_ok")
        tab_in, zero_ok, kr_ok, rope_hi = sem("tab_in"), sem("zero_ok"), sem("kr_ok"), sem("rope_hi")
        stg_hi, stg_lo, rel_in, rel_ok = sem("stg_hi"), sem("stg_lo"), sem("rel_in"), sem("rel_ok")
        s_full, nmax_ok, p_ok, d_ok = sem("s_full"), sem("nmax_ok"), sem("p_ok"), sem("d_ok")
        pt_full, pt_hi, pt_lo, pv_done = sem("pt_full"), sem("pt_hi"), sem("pt_lo"), sem("pv_done")
        o_hi, o_lo = sem("o_hi"), sem("o_lo")
        g_ok, a_ok, m_ok, mh_ok, ml_ok = sem("g_ok"), sem("a_ok"), sem("m_ok"), sem("mh_ok"), sem("ml_ok")
        y_ok, c_ok, s_ok, mid_ok, midh_ok, midl_ok = (
            sem(s) for s in ("y_ok", "c_ok", "s_ok", "mid_ok", "midh_ok", "midl_ok"))
        out_done = sem("out_done")

        def x1(k):
            return X[:, k * S2 + META:(k + 1) * S2]

        def ht(t, k, n=S1):
            return t[:, k * S2:k * S2 + n]

        def v1(name, i):
            c = VEC[name]
            if isinstance(i, int):
                return vec[:, c + i:c + i + 1]
            return vec[:, ds(i + c, 1)]

        def v1w(name, w):
            return vec[:, VEC[name]:VEC[name] + w]

        def wtile(t, slot, kk, m, cols=4):
            o = slot * BLK + (kk * cols + m) * P
            return t[:, o:o + P]

        def psum1(k):
            return PS[:, k, 0:S1]

        def psum2(k):
            return PS[:, k, COL2:COL2 + S2]

        def psumT(k, T):
            return psum1(k) if T == S1 else psum2(k)

        def wait_tile(eng, name, bi, i, g=0):
            n, end, _ = BATCH[name][bi]
            if i == n - 1:
                eng.wait_ge(w_used, g * NB[name] + (BLK0[name] + end + 1 + RING))
            else:
                per = sum(x[0] - 1 for x in BATCH[name])
                own = sum(x[0] - 1 for x in BATCH[name][:bi])
                eng.wait_ge(full, g * per + (FULL0[name] + own + i + 1))

        def wait_out(eng, name, bi, i, g=0):
            eng.wait_ge(free[(BATCH[name][bi][2] + i) % 4], free_before(name, bi, i, g) + 2)

        def out_sem(name, bi, i):
            return free[(BATCH[name][bi][2] + i) % 4]

        class Chain:

            def __init__(self, eng, s):
                self.eng, self.s, self.base, self.k, self.g, self.per = eng, s, 0, 0, None, 0

            def done(self, ins):
                ins.then_inc(self.s, 1)
                self.k += 1

            def wait(self):
                n = self.base + self.k
                self.eng.wait_ge(self.s, n if self.g is None else self.g * self.per + n)

            def turn(self, g, per):
                self.base, self.k, self.g, self.per = self.base + self.k, 0, g, per

            def end(self, turns):
                assert self.k == self.per, (self.k, self.per)
                self.base, self.k, self.g = self.base + turns * self.per, 0, None

        block = ctx.enter_context(nc.Block())

        @block.sync
        def _(sp):
            sp.dma_start(vec[:, :], vecs).then_inc(cst_in, 16)
            sp.dma_start(ident[:, :], consts[:, 0:P]).then_inc(cst_in, 16)
            sp.dma_start(work[:, 0:2 * P], consts[:, P:]).then_inc(cst_in, 16)
            sp.dma_start(X[:, :].rearrange("p (k t) -> p k t", k=KD)[:, :, META:S2],
                         xT.rearrange("k p t -> p k t")).then_inc(x_in, 16)
            sp.dma_start(X[:, :].rearrange("p (k t) -> p k t", k=KD)[:, :, 0:META],
                         meta.rearrange("k p t -> p k t")).then_inc(x_in, 16)

            def load_w(n, slot):
                sp.wait_ge(w_lo_ok, n + 1)
                sp.dma_start(w_raw[:, slot * BLK:(slot + 1) * BLK],
                             stream[ds(n, 1)].rearrange("a p c -> p (a c)")).then_inc(w_in[slot], 16)

            def load_ada(n, slot):
                sp.wait_ge(ada_used, n + 1)
                sp.dma_start(ada_w[:, slot * D:(slot + 1) * D],
                             ada[ds(n, 1)].rearrange("a p c -> p (a c)")).then_inc(ada_in[slot], 16)

            for n in range(12):
                load_ada(n, n % 4)
            for n in range(4):
                load_w(n, n)
            for n in range(12, 16):
                load_ada(n, n % 4)
            for n in range(4, 8):
                load_w(n, n % 4)
            with sp.Fori(0, 4) as g:
                for j in range(4):
                    load_w(g * 4 + (8 + j), j)
                for j in range(8):
                    load_ada(g * 8 + (16 + j), j % 4)
            with sp.Fori(0, (NSTREAM - 24) // 4) as g:
                for j in range(4):
                    load_w(g * 4 + (24 + j), j)
            for n in range(NSTREAM - NSTREAM % 4, NSTREAM):
                load_w(n, n % 4)

            for k in range(KD):
                sp.wait_ge(x_ok, 7 * KD + k + 1)
            sp.dma_start(yT.rearrange("k p t -> p k t"),
                         X[:, :].rearrange("p (k t) -> p k t", k=KD)[:, :, META:S2]).then_inc(out_done, 16)
            sp.wait_ge(out_done, 16)

        @block.tensor
        def _(pe):
            cnt_ = {"sq": 0, "norm": 0}
            pe.sem_inc(w_used, RING)
            pe.sem_inc(pt_full, 2)
            pe.sem_inc(pv_done, 1)

            def spans(T):
                return [(0, S1, 0)] if T == S1 else [(0, HALF2, COL2), (HALF2, S2, COL2)]

            def mm3(out, w_h, w_l, x_h, x_l, cuts, start, stop):
                last = None
                for i, (w, x) in enumerate(((w_l, x_h), (w_h, x_l), (w_h, x_h))):
                    for a, b, c0 in cuts:
                        last = pe.matmul(out[:, c0 + a:c0 + b], w, x[:, a:b], start=start and i == 0,
                                         stop=stop and i == 2)
                return last

            def begin(name, batch, i, g):
                pe.wait_ge(free[(BATCH[name][batch][2] + i) % 4], free_before(name, batch, i, g) + 1)

            def batch(name, bi, g, n, blocks, tiles, kks, cols, x, T, h_ready=None, w_tile=None):
                done = 0
                for bi_, b in enumerate(blocks):
                    slot = (BLK0[name] + b) % RING
                    kk = kks[bi_] if isinstance(kks, tuple) else kks
                    pe.wait_ge(w_lo_ok, n + (b + 1 + RING))
                    for m in range(tiles):
                        if bi_ == 0:
                            begin(name, bi, m, g)
                        for k in range(kk):
                            kt = done + k
                            if m == 0 and h_ready is not None:
                                pe.wait_ge(h_ok, h_ready + kt + 1)
                            xh, xl = x(kt)
                            last = mm3(PS[:, m, :], wtile(w_hi, slot, k, m, cols), wtile(w_lo, slot, k, m, cols),
                                       xh, xl, spans(T), bi_ == 0 and k == 0,
                                       bi_ == len(blocks) - 1 and k == kk - 1)
                        if bi_ == len(blocks) - 1 and m < tiles - 1:
                            last.then_inc(full, 1)
                    last.then_inc(w_used, 1)
                    done += kk

            def norm(n, T, ready, mean, src):
                if mean:
                    for k in range(n):
                        if ready is not None:
                            pe.wait_ge(ready[0], ready[1] + k + 1)
                        for a, b, c0 in spans(T):
                            last = pe.matmul(PS[:, 1, c0 + a:c0 + b], ones[:, :], src(k)[:, a:b],
                                             start=k == 0, stop=k == n - 1)
                    last.then_inc(n_mean, 1)
                if cnt_["norm"]:
                    pe.wait_ge(n_rs, cnt_["norm"])
                cnt_["norm"] += 1
                for k in range(n):
                    cnt_["sq"] += 1
                    pe.wait_ge(n_sq, cnt_["sq"])
                    for a, b, c0 in spans(T):
                        last = pe.matmul(PS[:, 0, c0 + a:c0 + b], ones[:, :], ht(work, k % 2, T)[:, a:b],
                                         start=k == 0, stop=k == n - 1)
                    last.then_inc(n_sq_used, 1)

            def hx(T):
                return lambda k: (ht(H_hi, k, T), ht(H_lo, k, T))

            def attention(kind):
                tiles, keys, T, pairs, c0, u0, p0 = ATT[kind]
                nq = len(tiles)
                U = 2 * nq
                mla = kind == "mla"
                qh, ql, kh, kl = (q2_hi, q2_lo, k2_hi, k2_lo) if mla else (q_hi, q_lo, k_hi, k_lo)
                vh, vl = (v2_hi, v2_lo) if mla else (v_hi, v_lo)
                dbuf = db2 if mla else db
                with pe.Fori(0, pairs) as p:
                    for t in range(U + 3):
                        if t < U:
                            par, i = divmod(t, nq)
                            q0, qn, ke = tiles[i]
                            if t == 0:
                                pe.wait_ge(stg_lo, p * STG_POOL[kind] + (STG_POOL0[kind] + STG_POOL[kind]))
                            pe.wait_ge(p_ok, p * U + (u0 + t + 1))
                            if mla:
                                rows = slice(0, P)
                                o = par * S2
                                cuts = [(0, 256)] + ([(256, max(ke, 512))] if ke > 256 else [])
                            else:
                                rows = slice(64 * par, 64 * par + 64)
                                o = 0
                                cuts = [(0, max(ke, 256))]
                            out = PS[:, t % 2, :]
                            for a, b in cuts:
                                for j, (l, r) in enumerate(((ql, kh), (qh, kl), (qh, kh))):
                                    last = pe.matmul(out[0:qn, c0 + a:c0 + b], l[rows, o + q0:o + q0 + qn],
                                                     r[rows, o + a:o + b], start=j == 0, stop=False,
                                                     skip_group_check=True)
                            if kind == "fox":
                                b = cuts[0][1]
                                pe.matmul(out[:, 0:b], sel_bf[:, ds(p * (2 * P) + par * P, P)], F_bf[:, 0:b],
                                          start=False, stop=False, skip_group_check=True)
                            if kind == "chunk":
                                lo = 0 if q0 else P
                                for r in (rel_lo, rel_hi):
                                    pe.matmul(out[:, q0 - P + lo:q0 + P], ident_r[:, :],
                                              r[:, par * 256 + lo:par * 256 + 256], start=False, stop=False,
                                              skip_group_check=True)
                            mask = chunk_bf if kind == "chunk" else causal_bf
                            last = pe.matmul(out[0:qn, c0 + q0:c0 + ke], ident_bf[:, 0:qn], mask[:, 0:ke - q0],
                                             start=False, stop=True, skip_group_check=True)
                            last.then_inc(s_full, 1)
                        if 1 <= t <= U:
                            w = t - 1
                            par, i = divmod(w, nq)
                            q0, qn, _ = tiles[i]
                            pe.wait_ge(d_ok, p * U + (u0 + w + 1))
                            pe.wait_ge(pt_lo, p * U + (u0 + w + 1))
                            pb, d = ht(work, w % 2, S2), dbuf[:, (w % 2) * P:(w % 2) * P + P]
                            for j in range(i + 1):
                                k0, kn = keys[j]
                                o = 512 * (w % 2) + j * qn
                                last = pe.matmul(PS[0:kn, 2, o:o + qn], pb[0:qn, k0:k0 + kn], d[0:qn, 0:qn],
                                                 start=True, stop=True, skip_group_check=True)
                            last.then_inc(pt_full, 1)
                        if t - 3 in (nq - 1, U - 1):
                            par = 0 if t - 3 == nq - 1 else 1
                            pe.wait_ge(pt_lo, p * U + (u0 + t - 3 + 1 + 2))
                            if par == 0:
                                pe.wait_ge(o_lo, p + (p0 + 1))
                            for j, (k0, kn) in enumerate(keys):
                                if mla:
                                    cuts = (((0, 256), (256, S2)), ((0, 256), (256, S2)),
                                            ((256, S2),), ((272, S2),), ((456, S2),))[j]
                                    if j == nq - 1:
                                        sh, sl, so = work_r[:, 2 * S2:3 * S2], work_r[:, 3 * S2:4 * S2], 0
                                    else:
                                        sh, sl, so = PT2_hi, PT2_lo, j * S2
                                else:
                                    cuts = ((min(k0, 256), T),)
                                    sh, sl, so = PT_hi, PT_lo, j * S1
                                vo = (par * nq + j) * P
                                for n_, (l, r) in enumerate(((vl, sh), (vh, sl), (vh, sh))):
                                    for a, b in cuts:
                                        end = j == nq - 1 or (mla and j == 1 and b == 256)
                                        last = pe.matmul(
                                            PS[:, 3, c0 + a:c0 + b], l[0:kn, vo:vo + P], r[0:kn, so + a:so + b],
                                            start=par == 0 and j == 0 and n_ == 0,
                                            stop=par == 1 and end and n_ == 2, skip_group_check=True)
                            last.then_inc(pv_done, 1)

            pe.wait_ge(set_up, SET_UP)
            pe.wait_ge(x_in, 32)
            norm(KD, S1, None, True, x1)
            def ada_turn(c):
                pe.wait_ge(ada_used, c * KD + (KD + 4))
                for m in range(KD):
                    last = pe.matmul(PS[:, 3, 512 + m:513 + m], ada_acc[:, m * P:(m + 1) * P], ones[:, 0:1],
                                     start=True, stop=True, skip_group_check=True)
                last.then_inc(ada_mm, 1)

            ada_turn(0)
            ada_turn(1)
            batch("forget", 0, 0, BLK0["forget"], [0], 1, 8, 1, hx(S1), S1, 0)
            with pe.Fori(0, 4) as g:
                batch("qk", 0, g, g * 4 + BLK0["qk"], range(4), 4, 2, 4, hx(S1), S1, 0)
                ada_turn(g + 2)
            with pe.Fori(0, 2) as g:
                for b in range(4):
                    slot = (BLK0["v"] + b) % RING
                    pe.wait_ge(w_lo_ok, g * 4 + (BLK0["v"] + b + 1 + RING))
                    for t in range(4):
                        if b == 0:
                            begin("v", 0, t, g)
                        for k in range(2):
                            kt = b * 2 + k
                            wr = slice(slot * BLK + k * 512, slot * BLK + k * 512 + 512)
                            hs = slice(kt * S2 + t * P, kt * S2 + t * P + P)
                            for j, (l, r) in enumerate(((H_lo, w_hi), (H_hi, w_lo), (H_hi, w_hi))):
                                last = pe.matmul(PS[:, t, 0:512], l[:, hs], r[:, wr],
                                                 start=kt == 0 and j == 0, stop=kt == 7 and j == 2)
                        if b == 3 and t < 3:
                            last.then_inc(full, 1)
                    last.then_inc(w_used, 1)
            for k in range(4):
                pe.wait_ge(free[k], FREE0["merge"][k] + 1)
            pe.wait_ge(f_ok, 1)
            attention("fox")
            attention("chunk")
            pe.wait_ge(o_lo, 8 + 1)

            def ox(kind):
                o = SHIFT + (0 if kind == "fox" else 8) * S1
                return lambda k: (O_split[:, o + k * S1:o + (k + 1) * S1],
                                  O_split[:, o + (4 + k) * S1:o + (5 + k) * S1])

            with pe.Fori(0, 2) as g:
                n = g * 12 + BLK0["merge"]
                batch("merge", 0, g, n, range(0, 4), 4, 2, 4, hx(S1), S1)
                batch("merge", 1, g, n, range(4, 6), 4, 2, 4, ox("fox"), S1)
                batch("merge", 2, g, n, range(6, 10), 4, 2, 4, hx(S1), S1)
                batch("merge", 3, g, n, range(10, 12), 4, 2, 4, ox("chunk"), S1)
            pe.wait_ge(ml_ok, 12)
            with pe.Fori(0, 2) as g:
                batch("out", 0, g, g * 4 + BLK0["out"], range(4), 4, 2, 4,
                      lambda k: (mg_hi[:, k * S1:(k + 1) * S1], mg_lo[:, k * S1:(k + 1) * S1]), S1)

            def ffn(up, down, T, h0, mid0):
                with pe.Fori(0, 11) as g:
                    batch(up, 0, g, g * 4 + BLK0[up], range(4), 4, 2, 4, hx(T), T, h0)
                pe.wait_ge(midl_ok, mid0 + KF + 1)
                with pe.Fori(0, 2) as g:
                    batch(down, 0, g, g * 12 + BLK0[down], range(12), 4, DOWN_ROWS, 4,
                          lambda k: (ht(mid_hi, k, T), ht(mid_lo, k, T)), T)

            def norm_after(nxt, n, T, ready, mean, src):
                for k in (0, 1):
                    pe.wait_ge(free[k], FREE0[nxt][k] + 1)
                norm(n, T, ready, mean, src)

            norm_after("up_a", KD, S1, (x_ok, 0), True, x1)
            norm_after("up_a", KD, S1, (x_ok, 8), True, x1)
            ffn("up_a", "down_a", S1, 8, 0)
            norm_after("dqkv", KD, S1, (x_ok, 16), True, x1)

            norm(KD, S2, None, False, None)
            batch("dqkv", 0, 0, BLK0["dqkv"], range(4), 4, 2, 4, hx(S2), S2, 16)
            batch("dqkv", 1, 0, BLK0["dqkv"], range(4, 6), 2, 4, 2, hx(S2), S2)
            norm_after("uq", 3, S2, None, False, None)
            norm(2, S2, None, False, None)
            pe.wait_ge(n_rs, cnt_["norm"])
            cx = lambda o: (lambda k: (ht(c_hi, o + k, S2), ht(c_lo, o + k, S2)))
            with pe.Fori(0, 2) as g:
                for b in range(4):
                    slot = (BLK0["uq"] + b) % RING
                    pe.wait_ge(w_lo_ok, g * 4 + (BLK0["uq"] + b + 1 + RING))
                    for j in range(2):
                        m = (2 * b + j) % 4
                        begin("uq", b, j, g)
                        for k in range(3):
                            pe.wait_ge(h_ok, 24 + k + 1)
                            xh, xl = cx(0)(k)
                            last = mm3(PS[:, m, :], wtile(w_hi, slot, k, j, 2), wtile(w_lo, slot, k, j, 2),
                                       xh, xl, spans(S2), k == 0, k == 2)
                        last.then_inc(full if j == 0 else w_used, 1)
            pe.wait_ge(h_ok, 29)
            for b in range(2):
                slot = (BLK0["uk"] + b) % RING
                pe.wait_ge(w_lo_ok, BLK0["uk"] + b + 1 + RING)
                for m in range(4):
                    begin("uk", b, m, 0)
                    for k in range(2):
                        xh, xl = cx(3)(k)
                        last = mm3(PS[:, m, :], wtile(w_hi, slot, k, m), wtile(w_lo, slot, k, m),
                                   xh, xl, spans(S2), k == 0, k == 1)
                    if m < 3:
                        last.then_inc(full, 1)
                last.then_inc(w_used, 1)
            for b in range(2):
                slot = (BLK0["uv"] + b) % RING
                pe.wait_ge(w_lo_ok, BLK0["uv"] + b + 1 + RING)
                for t in range(5):
                    begin("uv", b, t, 0)
                    t0 = KEYS2[t][0]
                    for k in range(2):
                        wr = slice(slot * BLK + k * 512, slot * BLK + k * 512 + 512)
                        cs = slice((3 + k) * S2 + t0, (3 + k) * S2 + t0 + P)
                        for j, (l, r) in enumerate(((c_lo, w_hi), (c_hi, w_lo), (c_hi, w_hi))):
                            last = pe.matmul(PS[:, t % 4, 0:512], l[:, cs], r[:, wr],
                                             start=k == 0 and j == 0, stop=k == 1 and j == 2)
                    if t < 4:
                        last.then_inc(full, 1)
                last.then_inc(w_used, 1)
            for k in range(4):
                pe.wait_ge(free[k], FREE0["wo"][k] + 1)
            attention("mla")
            pe.wait_ge(o_lo, 16 + 1)
            with pe.Fori(0, 2) as g:
                batch("wo", 0, g, g * 4 + BLK0["wo"], range(4), 4, 2, 4,
                      lambda k: (OK_hi[:, SHIFT + k * S2:SHIFT + (k + 1) * S2], ht(OQ_lo, 2 * k, S2)), S2)
            norm_after("up_b", KD, S2, None, False, None)
            norm(KD, S2, None, False, None)
            ffn("up_b", "down_b", S2, 29, KF)
            norm_after("pool", KD, S2, None, False, None)
            norm(KD, S2, None, False, None)
            for b in range(2):
                slot = (BLK0["pool"] + b) % RING
                pe.wait_ge(w_lo_ok, BLK0["pool"] + b + 1 + RING)
                for m in range(4):
                    begin("pool", b, m, 0)
                    grp = m // 2
                    for k in range(2):
                        kt = (2 * b + grp) * 2 + k
                        pe.wait_ge(h_ok, 37 + kt + 1)
                        xh, xl = hx(S2)(kt)
                        last = mm3(PS[:, m, :], wtile(w_hi, slot, grp * 2 + k, m % 2, 2),
                                   wtile(w_lo, slot, grp * 2 + k, m % 2, 2), xh, xl, spans(S2), k == 0, k == 1)
                    if m < 3:
                        last.then_inc(full, 1)
                last.then_inc(w_used, 1)
            norm_after("up_c", KD, S2, None, False, None)
            norm(KD, S2, None, False, None)
            ffn("up_c", "down_c", S2, 45, 2 * KF)
            for k in (0, 1):
                pe.wait_ge(free[k], FREE_END[k] + 1)
            norm(KD, S2, None, False, None)

        @block.gpsimd
        def _(gp):
            gp.sem_inc(w_lo_ok, RING)

            def lower(n, slot):
                gp.wait_ge(w_hi_ok, n + 1)
                o = slice(slot * BLK, (slot + 1) * BLK)
                gp.tensor_tensor(w_lo[:, o], w_raw[:, o], w_hi[:, o].bitcast(F32), ALU.subtract)\
                  .then_inc(w_lo_ok, 1)

            def lower_blocks(a, b):
                while a % RING and a < b:
                    lower(a, a % RING)
                    a += 1
                turns = (b - a) // RING
                if turns:
                    with gp.Fori(0, turns) as g:
                        for j in range(RING):
                            lower(g * RING + (a + j), j)
                for n in range(a + turns * RING, b):
                    lower(n, n % RING)

            def staged(kind, p, j, out, a, hi):
                gp.wait_ge(stg_hi, p * STG_ACT[kind] + (STG_ACT0[kind] + j + 1))
                if kind == "mla" and j >= 3:
                    gp.wait_ge(stg_lo, p * STG_POOL[kind] + (STG_POOL0[kind] + j))
                gp.tensor_tensor(out, a, hi.bitcast(F32), ALU.subtract).then_inc(stg_lo, 1)

            lower_blocks(0, BLK0["merge"] + RING)
            gp.wait_ge(ada_used, 6 * KD + 4)
            gp.memset(v_hi[:, :].bitcast(F32), 0.0).then_inc(zero_ok, 1)
            gp.memset(v_lo[:, :].bitcast(F32), 0.0).then_inc(zero_ok, 1)
            gp.memset(PT_hi[:, :].bitcast(F32), 0.0).then_inc(zero_ok, 1)
            gp.memset(PT_lo[:, :].bitcast(F32), 0.0).then_inc(zero_ok, 1)
            gp.wait_ge(zero_ok, 4)
            for kind, o in (("fox", 0), ("chunk", 8)):
                with gp.Fori(0, 4) as p:
                    staged(kind, p, 0, q_lo[:, :], QK[:, ds(p * S1 + o * S1, S1)], q_hi[:, :])
                    staged(kind, p, 1, k_lo[:, :], QK[:, ds(p * S1 + (o + 4) * S1, S1)], k_hi[:, :])
                    for par in range(2):
                        raw = v_raw[:, :].rearrange("p (t c) -> p t c", t=4)[:, :, ds(p * P + (o * 64 + par * 64), 64)]
                        hv, lv = (t[:, par * 512:(par + 1) * 512].rearrange("p (t c) -> p t c", t=4)
                                  [:, :, par * 64:par * 64 + 64] for t in (v_hi, v_lo))
                        staged(kind, p, 2 + par, lv, raw, hv)
                    if kind == "chunk":
                        staged(kind, p, 4, rel_lo[:, :], rel_raw[:, :], rel_hi[:, :])
            lower_blocks(BLK0["merge"] + RING, BLK0["wo"] + RING)
            gp.wait_ge(w_used, BLK0["wo"] + RING)
            gp.memset(k2_hi[:, :].bitcast(F32), 0.0).then_inc(zero_ok, 1)
            gp.memset(k2_lo[:, :].bitcast(F32), 0.0).then_inc(zero_ok, 1)
            for par, r in ((0, slice(64, 96)), (1, slice(32, 64))):
                gp.wait_ge(rope_hi, par + 1)
                gp.tensor_tensor(k2_lo[r, par * S2:(par + 1) * S2], kr[r, :],
                                 k2_hi[r, par * S2:(par + 1) * S2].bitcast(F32), ALU.subtract)\
                  .then_inc(zero_ok, 1)
            gp.wait_ge(zero_ok, 8)
            gp.memset(v2_hi[:, :].bitcast(F32), 0.0).then_inc(zero_ok, 1)
            gp.memset(v2_lo[:, :].bitcast(F32), 0.0).then_inc(zero_ok, 1)
            gp.memset(PT2_hi[:, :].bitcast(F32), 0.0).then_inc(zero_ok, 1)
            gp.memset(PT2_lo[:, :].bitcast(F32), 0.0).then_inc(zero_ok, 1)
            gp.wait_ge(zero_ok, 12)
            with gp.Fori(0, 8) as p:
                for par in range(2):
                    o = slice(par * S2, (par + 1) * S2)
                    staged("mla", p, par, q2_lo[:, o], Q2[:, ds(p * (2 * S2) + par * S2, S2)], q2_hi[:, o])
                for par in range(2):
                    o = slice(par * S2, (par + 1) * S2)
                    r = slice(64 * par, 64 * par + 64)
                    staged("mla", p, 2 + par, k2_lo[r, o], K2[r, ds(p * S2, S2)], k2_hi[r, o])
                for par in range(2):
                    raw = v_raw2[:, :].rearrange("p (t c) -> p t c", t=5)[:, :, ds(p * P + par * 64, 64)]
                    hv, lv = (t[:, par * 640:(par + 1) * 640].rearrange("p (t c) -> p t c", t=5)
                              [:, :, par * 64:par * 64 + 64] for t in (v2_hi, v2_lo))
                    staged("mla", p, 4 + par, lv, raw, hv)
            lower_blocks(BLK0["wo"] + RING, NBLK)

        @block.scalar
        def _(act_):
            cnt_ = {"sq": 0, "xc": 0, "r0": 0, "t": 0}
            chain = Chain(act_, act)
            act_.sem_inc(p_ok, 2)

            def copy(out, in_, scale=1.0):
                return act_.activation(out, in_, ACT.Copy, scale=scale)

            def upper(name, b, g=0):
                n = BLK0[name] + b
                slot = n % RING
                per = NB[name] if not isinstance(g, int) else 0
                g = g if per else 0
                act_.wait_ge(w_in[slot], g * (16 * per // RING) + 16 * (n // RING + 1))
                act_.wait_ge(w_used, g * per + (n + 1))
                o = slice(slot * BLK, (slot + 1) * BLK)
                copy(w_hi[:, o], w_raw[:, o]).then_inc(w_hi_ok, 1)

            def stage(name, g=0, take=None):
                b = RING
                for bi, (_, end, _) in enumerate(BATCH[name]):
                    while b < end + RING:
                        upper(name, b, g)
                        b += 1
                    if take is not None:
                        take(bi)
                while b < NB[name] + RING:
                    upper(name, b, g)
                    b += 1

            def loop(name, turns, take=None, per=0):
                with act_.Fori(0, turns) as g:
                    chain.turn(g, per)
                    stage(name, g, None if take is None else lambda bi: take(g, bi))
                chain.end(turns)

            def norm(n, T, eps, src, ready, mean=False):
                if cnt_["t"]:
                    act_.wait_ge(h_ok, cnt_["t"])
                for k in range(n):
                    if mean:
                        cnt_["xc"] += 1
                        act_.wait_ge(n_xc, cnt_["xc"])
                    else:
                        ready(k)
                    if k >= 2:
                        act_.wait_ge(n_sq_used, cnt_["sq"] - 1)
                    act_.activation(ht(work, k % 2, T), src(k), ACT.Square).then_inc(n_sq, 1)
                    cnt_["sq"] += 1
                act_.wait_ge(n_sq_used, cnt_["sq"])
                chain.done(act_.activation(ht(work, 2, T), psumT(0, T), ACT.Ln, bias=v1("eps", eps),
                                           scale=1.0 / (n * P)))
                chain.wait()
                act_.activation(ht(work, 3, T), ht(work, 2, T), ACT.Exp, scale=-0.5).then_inc(n_r0, 1)

            def split(n, T, hi):
                for k in range(n):
                    cnt_["t"] += 1
                    act_.wait_ge(t_ok, cnt_["t"])
                    copy(hi(k), ht(work, k % 2, T)).then_inc(t_hi, 1)

            def attention(kind):
                tiles, keys, T, pairs, c0, u0, p0 = ATT[kind]
                nq = len(tiles)
                U = 2 * nq
                mla = kind == "mla"
                na, s0 = STG_ACT[kind], STG_ACT0[kind]
                with act_.Fori(0, pairs) as p:
                    chain.turn(p, 2 if mla else 0)
                    act_.wait_ge(pv_done, p * 2 + (2 * p0 + 1))
                    if kind == "chunk":
                        act_.wait_ge(stg_lo, p * STG_POOL[kind] + STG_POOL0[kind])
                        act_.dma_start(rel_raw[:, :].rearrange("p (h c) -> p h c", h=2),
                                       rel[ds(p * 2, 2)].rearrange("h p c -> p h c")).then_inc(rel_in, 16)
                    if not mla:
                        o = 8 if kind == "chunk" else 0
                        copy(q_hi[:, :], QK[:, ds(p * S1 + o * S1, S1)]).then_inc(stg_hi, 1)
                        copy(k_hi[:, :], QK[:, ds(p * S1 + (o + 4) * S1, S1)]).then_inc(stg_hi, 1)
                        for par in range(2):
                            raw = v_raw[:, :].rearrange("p (t c) -> p t c", t=4)[:, :, ds(p * P + (o * 64 + par * 64), 64)]
                            copy(v_hi[:, par * 512:(par + 1) * 512].rearrange("p (t c) -> p t c", t=4)
                                 [:, :, par * 64:par * 64 + 64], raw).then_inc(stg_hi, 1)
                        if kind == "chunk":
                            act_.wait_ge(rel_ok, p * 2 + 2)
                            copy(rel_hi[:, :], rel_raw[:, :]).then_inc(stg_hi, 1)
                    else:
                        for par in range(2):
                            copy(q2_hi[:, par * S2:(par + 1) * S2], Q2[:, ds(p * (2 * S2) + par * S2, S2)])\
                                .then_inc(stg_hi, 1)
                        for par in range(2):
                            r = slice(64 * par, 64 * par + 64)
                            copy(k2_hi[r, par * S2:(par + 1) * S2], K2[r, ds(p * S2, S2)]).then_inc(stg_hi, 1)
                        for par in range(2):
                            raw = v_raw2[:, :].rearrange("p (t c) -> p t c", t=5)[:, :, ds(p * P + par * 64, 64)]
                            copy(v2_hi[:, par * 640:(par + 1) * 640].rearrange("p (t c) -> p t c", t=5)
                                 [:, :, par * 64:par * 64 + 64], raw).then_inc(stg_hi, 1)
                    for t in range(U + 2):
                        if t >= 2:
                            w = t - 2
                            par, i = divmod(w, nq)
                            q0, qn, _ = tiles[i]
                            act_.wait_ge(pt_full, p * U + (u0 + w + 3))
                            if i == 0:
                                act_.wait_ge(pv_done, p * 2 + (2 * p0 + par + 1))
                            nj = min(i + 1, 4)
                            po = 512 * (w % 2)
                            if i == 4:
                                chain.done(copy(work_r[0:META, 2 * S2 + q0:2 * S2 + q0 + qn],
                                                PS[0:META, 2, po + 4 * qn:po + 5 * qn]))
                            dst = PT2_hi if mla else PT_hi
                            h = copy(dst[:, :].rearrange("p (j t) -> p j t", t=T)[:, 0:nj, q0:q0 + qn],
                                     PS[:, 2, po:po + nj * qn].rearrange("p (j t) -> p j t", t=qn))
                            h.then_inc(pt_hi, 1)
                        if t < U:
                            par, i = divmod(t, nq)
                            q0, qn, ke = tiles[i]
                            act_.wait_ge(nmax_ok, p * U + (u0 + t + 1))
                            act_.wait_ge(pt_full, p * U + (u0 + t + 1))
                            act_.activation(ht(work, t % 2, S2)[0:qn, 0:ke], PS[0:qn, t % 2, c0:c0 + ke],
                                            ACT.Exp, bias=small[0:qn, t % 2:t % 2 + 1],
                                            accum_out=small[0:qn, 2 + t % 2:3 + t % 2]).then_inc(p_ok, 1)
                    act_.wait_ge(pv_done, p * 2 + (2 * p0 + 3))
                    if mla:
                        copy(OK_hi[:, ds(p * S2 + SHIFT, S2)], PS[:, 3, c0:c0 + S2]).then_inc(o_hi, 1)
                    else:
                        copy(O_split[:, ds(p * S1 + (o * S1 + SHIFT), S1)], PS[:, 3, 0:S1]).then_inc(o_hi, 1)
                chain.end(pairs)

            def ffn(up, down, T, layer, mid0, y0, down_take=None, down_per=0):
                def take(g, _):
                    act_.wait_ge(midl_ok, g * 2 + (mid0 + 1))
                    for m in range(4):
                        wait_tile(act_, up, 0, m, g)
                        c = layer * 8 * KF + 4 * m
                        act_.activation(ht(work, m, T), psumT(m, T), ACT.Identity,
                                        bias=v1("conv", g * 16 + (c + 3)), scale=v1("conv", g * 16 + (c + 2)))\
                            .then_inc(y_ok, 1)
                    for j in range(2):
                        wait_out(act_, up, 0, 2 * j, g)
                        act_.activation(ht(work, 2 * j, T), ht(work, 2 * j, T), ACT.Silu).then_inc(s_ok, 1)
                    for j in range(2):
                        act_.wait_ge(mid_ok, g * 2 + (mid0 + j + 1))
                        copy(mid_hi[:, ds((g * 2 + j) * S2, T)], ht(work, 2 * j + 1, T)).then_inc(midh_ok, 1)
                loop(up, 11, take)
                loop(down, 2, down_take, down_per)

            act_.wait_ge(cst_in, 48)
            act_.activation(cond[:, :], v1w("c", 8), ACT.Silu).then_inc(cond_ok, 1)
            norm(KD, S1, 0, lambda k: ht(XC, k), None, True)
            for b in range(RING):
                upper("forget", b)
            split(KD, S1, lambda k: ht(H_hi, k))

            def take_forget(_):
                act_.wait_ge(f_z, 1)
                chain.done(act_.activation(work[0:8, 3 * S2:3 * S2 + S1], work[0:8, 3 * S2:3 * S2 + S1],
                                           ACT.Exp, scale=-1.0))
                chain.wait()
                act_.activation(work[0:8, 3 * S2:3 * S2 + S1], work[0:8, 3 * S2:3 * S2 + S1],
                                ACT.Ln, bias=1.0).then_inc(f_ln, 1)
            stage("forget", 0, take_forget)
            loop("qk", 4)
            loop("v", 2)
            act_.wait_ge(zero_ok, 4)
            for k in range(4):
                act_.wait_ge(free[k], FREE0["merge"][k] + 1)
            attention("fox")
            attention("chunk")

            def take_merge(g, bi):
                for m in range(4):
                    if bi in (0, 2):
                        if bi == 2:
                            wait_out(act_, "merge", 1, m, g)
                        else:
                            act_.wait_ge(a_ok, g * 4 + (m + 1))
                        wait_tile(act_, "merge", bi, m, g)
                        act_.activation(gate[:, m * S1:(m + 1) * S1], psum1(m), ACT.Sigmoid)\
                            .then_inc(out_sem("merge", bi, m), 1)
                    if bi == 3:
                        act_.wait_ge(a_ok, g * 4 + (4 + m + 1))
                        copy(mg_hi[:, ds((g * 4 + m) * S1, S1)], acc[:, m * S1:(m + 1) * S1]).then_inc(mh_ok, 1)
            loop("merge", 2, take_merge)
            loop("out", 2)
            norm(KD, S1, 0, x1, None, True)
            norm(KD, S1, 0, lambda k: ht(XC, k), None, True)
            split(KD, S1, lambda k: ht(H_hi, k))
            ffn("up_a", "down_a", S1, 0, 0, 0)
            norm(KD, S1, 0, x1, None, True)

            act_.wait_ge(w_used, BLK0["dqkv"] + RING)
            act_.dma_start(cos_t[:, :], rope[0]).then_inc(tab_in, 16)
            act_.dma_start(sin_t[:, :], rope[1]).then_inc(tab_in, 16)
            act_.wait_ge(x_in, 32)
            x2 = lambda k: ht(X, k, S2)
            x_new = lambda base: (lambda k: act_.wait_ge(x_ok, base + k + 1))
            norm(KD, S2, 1, x2, x_new(24))
            split(KD, S2, lambda k: ht(H_hi, k, S2))
            stage("dqkv")
            norm(3, S2, 1, lambda k: ht(Q2, k, S2), lambda k: wait_out(act_, "dqkv", 0, k))
            split(3, S2, lambda k: ht(c_hi, k, S2))
            norm(2, S2, 1, lambda k: ht(Q2, 3 + k, S2),
                 lambda k: wait_out(act_, "dqkv", k, 3 if k == 0 else 0))
            split(2, S2, lambda k: ht(c_hi, 3 + k, S2))

            def take_uq(g, bi):
                for j in range(2):
                    m = BATCH["uq"][bi][2] + j
                    wait_tile(act_, "uq", bi, j, g)
                    act_.activation(Q2[:, ds((g * 8 + (2 * bi + j)) * S2, S2)], psum2(m), ACT.Copy,
                                    scale=(NOPE + ROPE) ** -0.5).then_inc(q_ok, 1)
            loop("uq", 2, take_uq)

            def take_uk(bi):
                for m in range(4):
                    wait_tile(act_, "uk", bi, m)
                    copy(ht(K2, 4 * bi + m, S2), psum2(m)).then_inc(out_sem("uk", bi, m), 1)
            stage("uk", 0, take_uk)
            stage("uv")
            for k in range(4):
                act_.wait_ge(free[k], FREE0["wo"][k] + 1)
            act_.wait_ge(zero_ok, 6)
            act_.wait_ge(kr_ok, 2)
            for par, r in ((0, slice(64, 96)), (1, slice(32, 64))):
                copy(k2_hi[r, par * S2:(par + 1) * S2], kr[r, :]).then_inc(rope_hi, 1)
            act_.wait_ge(zero_ok, 12)
            attention("mla")

            def take_m(name):
                def take(g, bi):
                    for m in range(4):
                        wait_tile(act_, name, bi, m, g)
                        copy(m_out[:, ds((g * 4 + m) * S2, S2)], psum2(m)).then_inc(out_sem(name, bi, m), 1)
                return take

            def m_ready(name):
                return lambda k: wait_out(act_, name, 0, k % 4, k // 4)
            mt = lambda k: ht(m_out, k, S2)
            loop("wo", 2, take_m("wo"))
            norm(KD, S2, 1, mt, m_ready("wo"))
            norm(KD, S2, 1, x2, x_new(32))
            split(KD, S2, lambda k: ht(H_hi, k, S2))
            ffn("up_b", "down_b", S2, 1, KF, 44, take_m("down_b"))
            norm(KD, S2, 1, mt, m_ready("down_b"))
            norm(KD, S2, 1, x2, x_new(40))
            split(KD, S2, lambda k: ht(H_hi, k, S2))

            def take_pool(bi):
                for m in range(4):
                    wait_tile(act_, "pool", bi, m | 1)
                    act_.activation(ht(m_out, 4 * bi + m, S2), psum2(m), ACT.Copy,
                                    scale=v1("pool_scale", 4 * bi + m)).then_inc(out_sem("pool", bi, m), 1)
            stage("pool", 0, take_pool)
            norm(KD, S2, 1, mt, lambda k: wait_out(act_, "pool", k // 4, k % 4))
            norm(KD, S2, 1, x2, x_new(48))
            split(KD, S2, lambda k: ht(H_hi, k, S2))
            ffn("up_c", "down_c", S2, 2, 2 * KF, 88, take_m("down_c"))
            norm(KD, S2, 1, mt, m_ready("down_c"))

        @block.vector
        def _(v):
            cnt_ = {"r0": 0, "mean": 0, "t": 0, "hi": 0, "xc": 0}
            chain = Chain(v, dve)
            for k in range(4):
                v.sem_inc(free[k], 1)
            v.sem_inc(ada_used, 4)
            v.sem_inc(pt_lo, 2)
            v.sem_inc(o_lo, 1)
            v.sem_inc(midl_ok, 1)
            v.sem_inc(a_ok, 4)
            v.sem_inc(ml_ok, 4)

            def loop(turns, per, body):
                with v.Fori(0, turns) as g:
                    chain.turn(g, per)
                    body(g)
                chain.end(turns)

            def norm(n, T, eps, src=None, xc=None):
                if xc is not None:
                    cnt_["mean"] += 1
                    v.wait_ge(n_mean, cnt_["mean"])
                    for k in range(n):
                        v.scalar_tensor_tensor(xc(k), psumT(1, T), -1.0 / (n * P), src(k), ALU.mult, ALU.add)\
                            .then_inc(n_xc, 1)
                cnt_["r0"] += 1
                v.wait_ge(n_r0, cnt_["r0"])
                a, b, r0 = ht(work, 0, T), ht(work, 1, T), ht(work, 3, T)
                rs = RS[:, 0:T]
                chain.done(v.scalar_tensor_tensor(a, r0, -0.5, r0, ALU.mult, ALU.mult))
                chain.done(v.tensor_scalar(b, psumT(0, T), 1.0 / (n * P), eps, ALU.mult, ALU.add))
                chain.wait()
                chain.done(v.tensor_tensor(a, a, b, ALU.mult))
                chain.wait()
                v.scalar_tensor_tensor(rs, a, 1.5, r0, ALU.add, ALU.mult).then_inc(n_rs, 1)
                v.wait_ge(n_rs, cnt_["r0"])

            def split(n, T, make, hi, lo):
                for k in range(n + 1):
                    if k < n:
                        if k >= 2:
                            v.wait_ge(h_ok, cnt_["hi"])
                        make(k, ht(work, k % 2, T)).then_inc(t_ok, 1)
                    if k:
                        cnt_["hi"] += 1
                        v.wait_ge(t_hi, cnt_["hi"])
                        v.tensor_tensor(lo(k - 1), ht(work, (k - 1) % 2, T), hi(k - 1).bitcast(F32), ALU.subtract)\
                            .then_inc(h_ok, 1)

            v.memset(ones[:, :], 1.0).then_inc(set_up, 1)
            v.memset(F_bf[:, :], 0.0).then_inc(set_up, 1)
            v.wait_ge(cst_in, 48)
            for t, src in ((ident_bf, ident[:, :]), (causal_bf, work[:, 0:P]), (chunk_bf, work[:, P:2 * P]),
                           (ident_r, ident[:, :])):
                v.tensor_copy(t[:, :], src).then_inc(set_up, 1)
            v.wait_ge(set_up, 1)
            for h in range(8):
                v.tensor_scalar(sel_bf[:, h * P:(h + 1) * P], ones[:, :], v1("sel", h), None, ALU.mult)\
                    .then_inc(set_up, 1)

            v.wait_ge(x_in, 32)
            norm(KD, S1, LN_EPS, x1, lambda k: ht(XC, k))

            def ada_part(c, g=None):
                for k in range(KD):
                    n = c * KD + k
                    off = (lambda x, per: x) if g is None else (lambda x, per: g * per + x)
                    v.wait_ge(ada_in[k % 4], off(16 * (n // 4 + 1), 32))
                    w = ada_w[:, (k % 4) * D:(k % 4 + 1) * D]
                    if k == 0:
                        ins = v.tensor_scalar(ada_acc[:, :], w, cond[:, 0:1], None, ALU.mult)
                    else:
                        v.wait_ge(ada_used, off(n + 4, 8))
                        ins = v.scalar_tensor_tensor(ada_acc[:, :], w, cond[:, k:k + 1], ada_acc[:, :],
                                                     ALU.mult, ALU.add)
                    ins.then_inc(ada_used, 1)

            def ada_out(c, part):
                v.wait_ge(ada_mm, c + 1)
                if isinstance(part, int):
                    m, mp = (t[:, part * 8:part * 8 + 8] for t in (mod, modp))
                    b = vec[:, VEC["b_ada"] + part * 8:VEC["b_ada"] + part * 8 + 8]
                else:
                    m, mp = (t[:, ds(part * 8, 8)] for t in (mod, modp))
                    b = vec[:, ds(part * 8 + VEC["b_ada"], 8)]
                chain.done(v.tensor_tensor(m, PS[:, 3, 512:520], b, ALU.add))
                chain.wait()
                chain.done(v.tensor_scalar(mp, m, 1.0, None, ALU.add))

            v.wait_ge(cond_ok, 1)
            for c in range(2):
                ada_part(c)
                ada_out(c, ADA_ORDER[c])

            def modulated(src, scale, shift):
                def make(k, out):
                    chain.done(v.tensor_tensor(out, src(k), RS[:, 0:S1], ALU.mult))
                    chain.wait()
                    return v.tensor_scalar(out, out, modp[:, scale * 8 + k:scale * 8 + k + 1],
                                           mod[:, shift * 8 + k:shift * 8 + k + 1], ALU.mult, ALU.add)
                return make

            chain.wait()
            hh, hl = (lambda k: ht(H_hi, k)), (lambda k: ht(H_lo, k))
            split(KD, S1, modulated(lambda k: ht(XC, k), 1, 0), hh, hl)

            wait_tile(v, "forget", 0, 0)
            fa, fb = work[0:8, 2 * S2:2 * S2 + S1], work[0:8, 3 * S2:3 * S2 + S1]
            v.tensor_scalar(fa, PS[0:8, 0, 0:S1], vec[0:8, VEC["b_f"]:VEC["b_f"] + 1], None, ALU.add)\
                .then_inc(free[0], 1)
            wait_out(v, "forget", 0, 0)
            v.scalar_tensor_tensor(fb, fa, -1.0, fa, ALU.mult, ALU.max).then_inc(f_z, 1)
            v.wait_ge(f_ln, 1)
            chain.done(v.scalar_tensor_tensor(fa, fa, 0.0, fb, ALU.min, ALU.subtract))
            step = 1
            while step < S1:
                chain.wait()
                chain.done(v.tensor_copy(fb[:, 0:step], fa[:, 0:step]))
                chain.done(v.tensor_tensor(fb[:, step:], fa[:, step:], fa[:, :S1 - step], ALU.add))
                fa, fb = fb, fa
                step *= 2
            chain.wait()
            chain.done(v.tensor_scalar(fb, fa, -1.0, None, ALU.mult))
            chain.wait()
            chain.done(v.tensor_copy(F_bf[0:8, :], fb))
            chain.wait()
            chain.done(v.tensor_tensor(fa, fb, F_bf[0:8, :], ALU.subtract))
            chain.wait()
            chain.done(v.tensor_copy(F_tmp[0:8, :], fa))
            chain.wait()
            chain.done(v.tensor_copy(F_bf[32:40, :], F_tmp[0:8, :]))
            chain.done(v.tensor_tensor(fb, fa, F_tmp[0:8, :], ALU.subtract))
            chain.wait()
            v.tensor_copy(F_bf[64:72, :], fb).then_inc(f_ok, 1)

            def take_qk(g):
                ada_part(2, g)
                for m in range(4):
                    wait_tile(v, "qk", 0, m, g)
                    v.tensor_scalar(QK[:, ds((g * 4 + m) * S1, S1)], psum1(m), v1("qk_scale", g), None, ALU.mult)\
                        .then_inc(free[m], 1)
                ada_out(g + 2, g + 2)
            loop(4, 2, take_qk)

            def take_v(g):
                for m in range(4):
                    wait_tile(v, "v", 0, m, g)
                    v.tensor_copy(v_raw[:, ds(g * 512 + m * D, 512)], psum1(m)).then_inc(free[m], 1)
            loop(2, 0, take_v)

            def attention(kind):
                tiles, keys, T, pairs, c0, u0, p0 = ATT[kind]
                nq = len(tiles)
                U = 2 * nq
                mla = kind == "mla"
                dbuf = db2 if mla else db

                def body(p):
                    if kind == "chunk":
                        v.wait_ge(rel_in, p * 16 + 16)
                        for par in range(2):
                            r = rel_raw[:, par * 256:(par + 1) * 256]
                            v.tensor_scalar(r, r, v1("rel_far", p * 2 + par), None, ALU.subtract)\
                                .then_inc(rel_ok, 1)
                    for t in range(U + 2):
                        if 1 <= t <= U:
                            w = t - 1
                            q0, qn, _ = tiles[w % nq]
                            v.wait_ge(p_ok, p * U + (u0 + w + 3))
                            v.wait_ge(pt_full, p * U + (u0 + w + 1))
                            r = small[0:qn, 4 + w % 2:5 + w % 2]
                            chain.done(v.reciprocal(r, small[0:qn, 2 + w % 2:3 + w % 2]))
                            chain.wait()
                            v.tensor_scalar(dbuf[0:qn, (w % 2) * P:(w % 2) * P + qn], ident[0:qn, 0:qn], r, None,
                                            ALU.mult).then_inc(d_ok, 1)
                        if t < U:
                            q0, qn, ke = tiles[t % nq]
                            v.wait_ge(s_full, p * U + (u0 + t + 1))
                            v.wait_ge(p_ok, p * U + (u0 + t + 1))
                            v.tensor_reduce(small[0:qn, t % 2:t % 2 + 1], PS[0:qn, t % 2, c0:c0 + ke], AX.X,
                                            ALU.max, negate=True).then_inc(nmax_ok, 1)
                        if t >= 2:
                            w = t - 2
                            par, i = divmod(w, nq)
                            q0, qn, _ = tiles[i]
                            v.wait_ge(pt_hi, p * U + (u0 + w + 1))
                            nj = min(i + 1, 4)
                            po = 512 * (w % 2)
                            if i == 4:
                                o = slice(q0, q0 + qn)
                                chain.done(v.tensor_tensor(
                                    ht(work_r, 3, S2)[0:META, o], PS[0:META, 2, po + 4 * qn:po + 5 * qn],
                                    ht(work_r, 2, S2)[0:META, o].bitcast(F32), ALU.subtract))
                            a, b = (x[:, :].rearrange("p (j t) -> p j t", t=T)[:, 0:nj, q0:q0 + qn]
                                    for x in ((PT2_hi, PT2_lo) if mla else (PT_hi, PT_lo)))
                            ins = v.tensor_tensor(b, PS[:, 2, po:po + nj * qn].rearrange("p (j t) -> p j t", t=qn),
                                                  a.bitcast(F32), ALU.subtract)
                            ins.then_inc(pt_lo, 1)
                    v.wait_ge(o_hi, p + (p0 + 1))
                    if mla:
                        v.tensor_tensor(OQ_lo[:, ds(p * (2 * S2), S2)], PS[:, 3, c0:c0 + S2],
                                        OK_hi[:, ds(p * S2 + SHIFT, S2)].bitcast(F32), ALU.subtract).then_inc(o_lo, 1)
                    else:
                        o = 8 if kind == "chunk" else 0
                        v.tensor_tensor(O_split[:, ds(p * S1 + ((o + 4) * S1 + SHIFT), S1)], PS[:, 3, 0:S1],
                                        O_split[:, ds(p * S1 + (o * S1 + SHIFT), S1)].bitcast(F32), ALU.subtract)\
                            .then_inc(o_lo, 1)
                loop(pairs, U + (2 if mla else 0), body)

            attention("fox")
            attention("chunk")

            def take_merge(g):
                v.wait_ge(ml_ok, g * 4 + 4)
                for bi in (1, 3):
                    for m in range(4):
                        gm, am = gate[:, m * S1:(m + 1) * S1], acc[:, m * S1:(m + 1) * S1]
                        wait_out(v, "merge", bi - 1, m, g)
                        wait_tile(v, "merge", bi, m, g)
                        v.tensor_tensor(am if bi == 1 else gm, psum1(m), gm, ALU.mult)\
                            .then_inc(out_sem("merge", bi, m), 1)
                        if bi == 3:
                            wait_out(v, "merge", 3, m, g)
                            v.tensor_tensor(am, am, gm, ALU.add).then_inc(a_ok, 1)
                for m in range(4):
                    v.wait_ge(mh_ok, g * 4 + (m + 1))
                    o = (g * 4 + m) * S1
                    v.tensor_tensor(mg_lo[:, ds(o, S1)], acc[:, m * S1:(m + 1) * S1],
                                    mg_hi[:, ds(o, S1)].bitcast(F32), ALU.subtract).then_inc(ml_ok, 1)
            loop(2, 0, take_merge)

            def residual(name, part):
                def body(g):
                    for m in range(4):
                        wait_tile(v, name, 0, m, g)
                        w = ht(work, m, S1)
                        v.tensor_scalar(w, psum1(m), modp[:, ds(g * 4 + (part * 8 + m), 1)], None, ALU.mult)\
                            .then_inc(free[m], 1)
                        wait_out(v, name, 0, m, g)
                        x = X[:, ds((g * 4 + m) * S2 + META, S1)]
                        v.scalar_tensor_tensor(x, x, ALPHA, w, ALU.mult, ALU.add).then_inc(x_ok, 1)
                loop(2, 0, body)

            def affine(gain, bias):
                for k in range(KD):
                    chain.done(v.tensor_tensor(x1(k), x1(k), RS[:, 0:S1], ALU.mult))
                for k in range(KD):
                    if k == 0:
                        chain.wait()
                    v.tensor_scalar(x1(k), x1(k), v1(gain, k), v1(bias, k), ALU.mult, ALU.add).then_inc(x_ok, 1)

            def ffn(up, T, layer, y0, mid0):
                def body(g):
                    for j in range(2):
                        for tap in range(2):
                            for m in (2 * j, 2 * j + 1):
                                if tap == 0:
                                    v.wait_ge(y_ok, g * 4 + (y0 + m + 1))
                                elif m == 2 * j:
                                    chain.wait()
                                y, u = ht(work, m, T), psumT(m, T)
                                s = 1 + tap
                                w = v1("conv", g * 16 + (layer * 8 * KF + 4 * m + 1 - tap))
                                ins = v.scalar_tensor_tensor(y[:, s:], u[:, :T - s], w, y[:, s:], ALU.mult, ALU.add)
                                chain.done(ins) if tap == 0 else ins.then_inc(free[m], 1)
                    for j in range(2):
                        v.wait_ge(s_ok, g * 2 + (mid0 + j + 1))
                        wait_out(v, up, 0, 2 * j + 1, g)
                        y = ht(work, 2 * j + 1, T)
                        v.tensor_tensor(y, ht(work, 2 * j, T), y, ALU.mult).then_inc(mid_ok, 1)
                    for j in range(2):
                        v.wait_ge(midh_ok, g * 2 + (mid0 + j + 1))
                        o = (g * 2 + j) * S2
                        v.tensor_tensor(mid_lo[:, ds(o, T)], ht(work, 2 * j + 1, T),
                                        mid_hi[:, ds(o, T)].bitcast(F32), ALU.subtract).then_inc(midl_ok, 1)
                loop(11, 4, body)

            residual("out", 2)
            norm(KD, S1, LN_EPS, x1, x1)
            affine("ln1_g", "ln1_b")
            norm(KD, S1, LN_EPS, x1, lambda k: ht(XC, k))
            split(KD, S1, modulated(lambda k: ht(XC, k), 4, 3), hh, hl)
            ffn("up_a", S1, 0, 0, 0)
            residual("down_a", 5)
            norm(KD, S1, LN_EPS, x1, x1)
            affine("ln2_g", "ln2_b")

            x2 = lambda k: ht(X, k, S2)
            h2, l2 = (lambda k: ht(H_hi, k, S2)), (lambda k: ht(H_lo, k, S2))

            def scaled(src, gain, i0):
                return lambda k, out: v.scalar_tensor_tensor(out, src(k), v1(gain, i0 + k), RS[:, :],
                                                             ALU.mult, ALU.mult)

            def post(gain, i0, x0):
                for k in range(KD):
                    w = ht(work, 2 + k % 2, S2)
                    if k >= 2:
                        v.wait_ge(x_ok, x0 + k - 1)
                    chain.done(v.scalar_tensor_tensor(w, ht(m_out, k, S2), v1(gain, i0 + k), RS[:, :],
                                                      ALU.mult, ALU.mult))
                    chain.wait()
                    v.tensor_tensor(x2(k), x2(k), w, ALU.add).then_inc(x_ok, 1)

            norm(KD, S2, RMS_EPS)
            split(KD, S2, scaled(x2, "mix_pre", 0), h2, l2)
            for bi, m, dst in [(0, i, ht(Q2, i, S2)) for i in range(4)] + [(1, 0, ht(Q2, 4, S2)), (1, 1, kr[:, :])]:
                wait_tile(v, "dqkv", bi, m)
                v.tensor_copy(dst, psum2(m)).then_inc(out_sem("dqkv", bi, m), 1)
            v.wait_ge(tab_in, 32)
            wait_out(v, "dqkv", 1, 1)
            swap = [(i + ROPE // 2) % ROPE for i in range(ROPE)]
            for r in (slice(32, 64), slice(64, 96)):
                w = ht(K2, 0, S2)[r, :]
                chain.done(v.stream_shuffle(w, kr[r, :], swap))
                chain.wait()
                chain.done(v.tensor_tensor(w, w, sin_t[r, :], ALU.mult))
                chain.done(v.tensor_tensor(kr[r, :], kr[r, :], cos_t[r, :], ALU.mult))
                chain.wait()
                v.tensor_tensor(kr[r, :], kr[r, :], w, ALU.add).then_inc(kr_ok, 1)
            for t in (c_hi, c_lo):
                chain.done(v.memset(t[:, 5 * S2:].bitcast(F32), 0.0))
            norm(3, S2, RMS_EPS)
            split(3, S2, scaled(lambda k: ht(Q2, k, S2), "q_norm", 0), lambda k: ht(c_hi, k, S2),
                  lambda k: ht(c_lo, k, S2))
            norm(2, S2, RMS_EPS)
            split(2, S2, scaled(lambda k: ht(Q2, 3 + k, S2), "kv_norm", 0), lambda k: ht(c_hi, 3 + k, S2),
                  lambda k: ht(c_lo, 3 + k, S2))

            def take_uq(g):
                s = (NOPE + ROPE) ** -0.5
                for bi in range(4):
                    for j in range(2):
                        m = BATCH["uq"][bi][2] + j
                        r = slice(64, 96) if j == 0 else slice(32, 64)
                        q = Q2[r, ds((g * 8 + (2 * bi + j)) * S2, S2)]
                        w = ht(work, j, S2)[r, :]
                        chain.wait()
                        v.wait_ge(q_ok, g * 8 + (2 * bi + j + 1))
                        chain.done(v.scalar_tensor_tensor(q, PS[r, m, COL2:COL2 + S2], s, cos_t[r, :], ALU.mult,
                                                          ALU.mult))
                        v.stream_shuffle(w, PS[r, m, COL2:COL2 + S2], swap).then_inc(out_sem("uq", bi, j), 1)
                        wait_out(v, "uq", bi, j, g)
                        chain.done(v.scalar_tensor_tensor(w, w, s, sin_t[r, :], ALU.mult, ALU.mult))
                        chain.wait()
                        chain.done(v.tensor_tensor(q, q, w, ALU.add))
            v.wait_ge(h_ok, cnt_["hi"])
            loop(2, 24, take_uq)
            chain.wait()
            for bi in range(2):
                for t in range(5):
                    wait_tile(v, "uv", bi, t)
                    o = t * D + bi * 512
                    v.tensor_copy(v_raw2[:, o:o + 512], PS[:, t % 4, 0:512]).then_inc(out_sem("uv", bi, t), 1)
            attention("mla")
            norm(KD, S2, RMS_EPS)
            post("mix_post", 0, 32)
            norm(KD, S2, RMS_EPS)
            split(KD, S2, scaled(x2, "ffn_pre", 0), h2, l2)
            ffn("up_b", S2, 1, 44, KF)
            norm(KD, S2, RMS_EPS)
            post("ffn_post", 0, 40)
            norm(KD, S2, RMS_EPS)

            def pooled(k, out):
                w = POOLS[k // 2]
                a = ht(pool_a, k % 2, S2)
                chain.done(v.scalar_tensor_tensor(a, x2(k), v1("mix_pre", KD + k), RS[:, :], ALU.mult, ALU.mult))
                s, step = a, 1
                bufs = [ht(pool_s, 0, S2), ht(pool_s, 1, S2)]
                while step < w:
                    chain.wait()
                    n = bufs.pop(0)
                    chain.done(v.tensor_copy(n[:, 0:step], s[:, 0:step]))
                    chain.done(v.tensor_tensor(n[:, step:], s[:, step:], s[:, :S2 - step], ALU.add))
                    if s is not a:
                        bufs.append(s)
                    s = n
                    step *= 2
                chain.wait()
                i = VEC["cnt"] + 16 * (k // 2)
                small_ = pool_c[:, 0:16]
                chain.done(v.tensor_tensor(small_, s[:, 0:16], vec[:, i:i + 16], ALU.mult))
                chain.done(v.scalar_tensor_tensor(out[:, 16:], s[:, 16:], 1.0 / w, a[:, 16:], ALU.mult,
                                                  ALU.subtract))
                chain.wait()
                return v.tensor_tensor(out[:, 0:16], small_, a[:, 0:16], ALU.subtract)

            split(KD, S2, pooled, h2, l2)
            norm(KD, S2, RMS_EPS)
            post("mix_post", KD, 48)
            norm(KD, S2, RMS_EPS)
            split(KD, S2, scaled(x2, "ffn_pre", KD), h2, l2)
            ffn("up_c", S2, 2, 88, 2 * KF)
            norm(KD, S2, RMS_EPS)
            post("ffn_post", KD, 56)


def rows(a):
    return a.reshape(-1, P, a.shape[-1])


def columns(a):
    return a.reshape(-1, P).T


def weight_stream(np, w):
    out = np.zeros((NSTREAM, P, BLK), np.float32)
    at = [0]

    def put(block):
        flat = block.transpose(1, 0, 2).reshape(P, -1)
        out[at[0], :, :flat.shape[1]] = flat
        at[0] += 1

    def cut(m, c0, width, kk=2):
        m = rows(m[:, c0:c0 + width])
        for k in range(0, m.shape[0], kk):
            put(m[k:k + kk])

    w_in = w["w_in"][0]
    put(rows(w_in[:, 1536:1536 + P]))
    for c in (0, 512, 1544, 2056, 1024, 2568):
        cut(w_in, c, 512)
    for g in range(2):
        cut(w_in, 3080 + 512 * g, 512)
        cut(w["w_br_fox"][0], 512 * g, 512)
        cut(w_in, 4104 + 512 * g, 512)
        cut(w["w_br_chunk"][0], 512 * g, 512)
    for g in range(2):
        cut(w["w_out"][0], 512 * g, 512)

    def ffn(up, down):
        a, b = (up[:, i * FF:(i + 1) * FF].reshape(D, KF, P) for i in range(2))
        both = np.stack([a, b], 2).reshape(D, 2 * FF)
        for g in range(11):
            cut(both, 512 * g, 512)
        for g in range(2):
            m, k = rows(down[:, 512 * g:512 * (g + 1)]), 0
            for n in DOWN_ROWS:
                put(m[k:k + n])
                k += n

    ffn(w["w_up"][0], w["w_down"][0])
    m = w["mla_w_dqkv_2"][0]
    cut(m, 0, 512)
    z = np.zeros((D, ROPE), np.float32)
    rope = m[:, RQ + RKV:]
    cut(np.concatenate([m[:, 512:640], z, rope, rope, z], 1), 0, 256, 4)
    m = w["mla_w_uq_2"][0].reshape(RQ, H2, NOPE + ROPE)
    z = np.zeros((RQ, ROPE), np.float32)
    for h in range(0, H2, 2):
        cut(np.concatenate([m[:, h], z, z, m[:, h + 1, NOPE:], m[:, h + 1, :NOPE]], 1), 0, 256, 3)
    m = w["mla_w_ukv_2"][0].reshape(RKV, H2, 2, NOPE)
    for part in range(2):
        for g in range(2):
            cut(m[:, 8 * g:8 * g + 8, part].reshape(RKV, 512), 0, 512)
    for g in range(2):
        cut(w["mla_w_o_2"][0], 512 * g, 512)
    ffn(w["ffn_w_up_2"][0], w["ffn_w_down_2"][0])
    m = w["pool_w_group_2"][0]
    for g in range(0, 4, 2):
        put(rows(m[g:g + 2].reshape(512, 256)))
    ffn(w["ffn_w_up_2"][1], w["ffn_w_down_2"][1])
    assert at[0] == NBLK, (at[0], NBLK)
    return out


def vector_table(np, w):
    t = np.zeros((P, NVEC), np.float32)

    def put(name, cols):
        t[:, VEC[name]:VEC[name] + cols.shape[1]] = cols

    put("c", columns(w["c"]))
    for name in ("b_ada", "ln1_g", "ln1_b", "ln2_g", "ln2_b"):
        put(name, columns(w[name]))
    t[0:8, VEC["b_f"]] = w["b_f"][0]
    put("qk_scale", np.broadcast_to(np.array([[0.125, 1.0, 0.125, 1.0]], np.float32), (P, 4)))
    put("rel_far", np.broadcast_to(w["rel_bias"][0][:, 256][None], (P, 8)))
    r = np.arange(P)[:, None]
    put("sel", ((r < 96) & (r % 32 == np.arange(8)[None])).astype(np.float32))
    for name, src in (("mix_pre", "norm_mix_pre_2"), ("mix_post", "norm_mix_post_2"),
                      ("ffn_pre", "norm_ffn_pre_2"), ("ffn_post", "norm_ffn_post_2"),
                      ("q_norm", "mla_q_norm_2"), ("kv_norm", "mla_kv_norm_2"), ("pool_scale", "pool_scale_2")):
        put(name, columns(w[src]))
    put("eps", np.broadcast_to(np.array([[LN_EPS, RMS_EPS]], np.float32), (P, 2)))
    put("cnt", np.broadcast_to(np.concatenate(
        [1.0 / np.minimum(np.arange(16) + 1, n) for n in POOLS]).astype(np.float32)[None], (P, 64)))
    layers = [(w["conv_w"][0], w["conv_b"][0])]
    layers += [(w["ffn_conv_w_2"][i], w["ffn_conv_b_2"][i]) for i in range(2)]
    conv = []
    for taps, bias in layers:
        a = np.concatenate([taps, bias[None]], 0).reshape(4, 2, KF, P)
        conv.append(a.transpose(3, 2, 1, 0).reshape(P, -1))
    put("conv", np.concatenate(conv, 1))
    return t


def kernel(**inputs):
    import numpy as np
    import concourse.bacc as bacc
    from concourse.bass_utils import run_bass_kernel_spmd

    w = {k: np.asarray(v) for k, v in inputs.items()}
    q, s = np.arange(P)[:, None], np.arange(P)[None]
    neg = np.float32(-3e38)
    consts = np.concatenate([np.eye(P), np.where(s <= q, 0, neg), np.where((q < 64) & (s >= 64), neg, 0)], 1)
    far = np.clip(P + q - np.arange(2 * P)[None], -P, P) + P
    pos = np.arange(S2, dtype=np.float32)[None] / (10000.0 ** (np.arange(0, ROPE, 2, dtype=np.float32) / ROPE))[:, None]
    turn = np.zeros((2, P, S2), np.float32)
    for r in (32, 64):
        turn[0, r:r + ROPE] = np.concatenate([np.cos(pos), np.cos(pos)])
        turn[1, r:r + ROPE] = np.concatenate([-np.sin(pos), np.sin(pos)])
    arrays = {
        "xT": np.ascontiguousarray(w["x"][0].T).reshape(KD, P, S1),
        "meta": np.ascontiguousarray(w["meta_tokens_2"].T).reshape(KD, P, META),
        "stream": weight_stream(np, w),
        "ada": np.concatenate([rows(w["w_ada"][0][:, part * D:(part + 1) * D]) for part in ADA_ORDER]),
        "vecs": vector_table(np, w),
        "consts": consts.astype(np.float32),
        "rel": np.ascontiguousarray(w["rel_bias"][0][:, far]),
        "rope": turn,
    }
    nc = bacc.Bacc("TRN2", target_bir_lowering=False, num_devices=1)
    args = {n: nc.dram_tensor(n, a.shape, mybir.dt.from_np(a.dtype), kind="ExternalInput").ap()
            for n, a in arrays.items()}
    yT = nc.dram_tensor("yT", (KD, P, S1), F32, kind="ExternalOutput").ap()
    program(nc, yT=yT, **args)
    got = run_bass_kernel_spmd(nc, [arrays], core_ids=[0]).results[0]["yT"]
    return np.ascontiguousarray(got.reshape(D, S1).T)[None]
```

```python
from contextlib import ExitStack

import concourse.bass as bass
from concourse import mybir

P = 128
D = 1024
KD = D // P
S1 = 512
META = 16
S2 = S1 + META
H1 = 8
H2 = 16
FF = 2816
KF = FF // P
QB = 128
RQ, RKV = 384, 256
NOPE, ROPE = 64, 32
POOLS = (2, 4, 8, 16)
ALPHA = 2.0 ** 0.25
LN_EPS, RMS_EPS = 1e-5, 1e-6

BLK = 1024
C_PAD = P - META
SHIFT = 16
RING = 4

F32 = mybir.dt.float32
F32R = mybir.dt.float32r
BF16 = mybir.dt.bfloat16
ALU = mybir.AluOpType
ACT = mybir.ActivationFunctionType
AX = mybir.AxisListType
ds = bass.ds

STAGES = [
    ("forget", 1, 1), ("qk", 4, 4), ("v", 4, 2), ("merge", 12, 2), ("out", 4, 2),
    ("up_a", 4, 11), ("down_a", 12, 2),
    ("dqkv", 6, 1), ("uq", 4, 2), ("uk", 2, 1), ("uv", 2, 1), ("wo", 4, 2),
    ("up_b", 4, 11), ("down_b", 12, 2), ("pool", 2, 1), ("up_c", 4, 11), ("down_c", 12, 2),
]
DOWN_ROWS = (2,) * (KF - 12) + (1,) * (24 - KF)
BLK0, _n = {}, 0
for _name, _b, _t in STAGES:
    BLK0[_name] = _n
    _n += _b * _t
NBLK = _n
NSTREAM = NBLK + RING

BATCH = {
    "forget": [(1, 0, 0)], "qk": [(4, 3, 0)], "v": [(4, 3, 0)],
    "merge": [(4, 3, 0), (4, 5, 0), (4, 9, 0), (4, 11, 0)],
    "out": [(4, 3, 0)], "up_a": [(4, 3, 0)], "down_a": [(4, 11, 0)], "dqkv": [(4, 3, 0), (2, 5, 0)],
    "uq": [(2, 0, 0), (2, 1, 2), (2, 2, 0), (2, 3, 2)], "uk": [(4, 0, 0), (4, 1, 0)],
    "uv": [(5, 0, 0), (5, 1, 0)], "wo": [(4, 3, 0)],
    "up_b": [(4, 3, 0)], "down_b": [(4, 11, 0)], "pool": [(4, 0, 0), (4, 1, 0)], "up_c": [(4, 3, 0)],
    "down_c": [(4, 11, 0)],
}
NB = {name: b for name, b, _ in STAGES}
FULL0, FREE0, _f, _u = {}, {}, 0, [0, 0, 0, 0]


def tiles_in(name, k, before=None):
    return sum(1 for n, _, p in BATCH[name][:before] for j in range(n) if (p + j) % 4 == k)


for _name, _b, _t in STAGES:
    FULL0[_name], FREE0[_name] = _f, list(_u)
    _f += sum(n - 1 for n, _, _ in BATCH[_name]) * _t
    for _k in range(4):
        _u[_k] += tiles_in(_name, _k) * _t
FREE_END = list(_u)


def free_before(name, batch, i, g=0):
    k = (BATCH[name][batch][2] + i) % 4
    return g * tiles_in(name, k) + (FREE0[name][k] + tiles_in(name, k, batch) + i // 4)


TILES1 = [(i * QB, QB, (i + 1) * QB) for i in range(S1 // QB)]
TILES2 = TILES1[:3] + [(384, 72, 512), (456, 72, S2)]
KEYS1 = [(i * QB, QB) for i in range(S1 // QB)]
KEYS2 = KEYS1 + [(S1, META)]
ATT = {
    "fox": (TILES1, KEYS1, S1, H1 // 2, 0, 0, 0),
    "chunk": (TILES1, KEYS1, S1, H1 // 2, 0, 32, 4),
    "mla": (TILES2, KEYS2, S2, H2 // 2, 256, 64, 8),
}
STG = {"fox": ("q", "k", "v"), "chunk": ("q", "k", "rel", "v"), "mla": ("q", "k", "v")}
STG0 = {"fox": 0, "chunk": 3 * H1, "mla": 7 * H1}
LEAD = 3
COL2 = 248
HALF2 = S2 // 2

VEC, _v = {}, 0
for _name, _w in [("c", 8), ("b_ada", 48), ("ln1_g", 8), ("ln1_b", 8), ("ln2_g", 8), ("ln2_b", 8),
                  ("b_f", 1), ("qk_scale", 4), ("rel_far", 8), ("sel", 8),
                  ("mix_pre", 16), ("mix_post", 16), ("ffn_pre", 16), ("ffn_post", 16),
                  ("q_norm", 3), ("kv_norm", 2), ("pool_scale", 8), ("eps", 2),
                  ("cnt", 64), ("conv", 3 * 4 * 2 * KF)]:
    VEC[_name] = _v
    _v += _w
NVEC = _v
SET_UP = 14
ADA_ORDER = (1, 0, 2, 3, 4, 5)


def program(nc, xT, meta, stream, ada, vecs, consts, rel, rope, yT):
    with ExitStack() as ctx:
        def sb(name, cols, dt=F32):
            return ctx.enter_context(nc.sbuf_tensor(name, [P, cols], dt))

        def region(*tensors):
            with ExitStack() as over:
                return [over.enter_context(nc.sbuf_tensor(n, [P, c], dt)) for n, c, dt in tensors]

        def sem(name):
            return ctx.enter_context(nc.semaphore(name))

        X = sb("X", KD * S2)
        w_raw = sb("w_raw", RING * BLK)
        w_hi = sb("w_hi", RING * BLK, F32R)
        w_lo = sb("w_lo", RING * BLK, F32R)
        (work_r,) = region(("work_r", 4 * S2, F32R))
        work = sb("work", 4 * S2)
        RS = sb("RS", S2)
        vec = sb("vec", NVEC)
        mod = sb("mod", 48)
        modp = sb("modp", 48)
        ident = sb("ident", P)
        ones = sb("ones", P)
        ident_bf = sb("ident_bf", P, BF16)
        causal_bf = sb("causal_bf", P, BF16)
        chunk_bf = sb("chunk_bf", P, BF16)
        ident_r = sb("ident_r", P, F32R)
        cond = sb("cond", 8)
        small = sb("small", 8)
        (m_out,) = region(("m_out", KD * S2, F32))
        v_raw2, kr = region(("v_raw2", 5 * D, F32), ("kr", S2, F32))
        H_hi = sb("H_hi", KD * S2, F32R)
        H_lo = sb("H_lo", KD * S2, F32R)
        (_, QK, XC, ada_w, ada_acc) = region(
            ("shift", SHIFT, F32),             ("QK", 16 * S1, F32), ("XC", KD * S2, F32), ("ada_w", 4 * D, F32), ("ada_acc", D, F32))
        (_, QK_, v_raw, q_hi, q_lo, k_hi, k_lo, v_hi, v_lo, PT_hi, PT_lo, rel_raw, rel_hi, rel_lo,
         sel_bf, F_bf, F_tmp) = region(
            ("shift_", SHIFT, F32), ("QK_", 16 * S1, F32), ("v_raw", 4 * D, F32), ("q_hi", S1, F32R), ("q_lo", S1, F32R),
            ("k_hi", S1, F32R), ("k_lo", S1, F32R), ("v_hi", 2 * 4 * P, F32R), ("v_lo", 2 * 4 * P, F32R),
            ("PT_hi", 4 * S1, F32R), ("PT_lo", 4 * S1, F32R),
            ("rel_raw", 2 * 256, F32), ("rel_hi", 2 * 256, F32R), ("rel_lo", 2 * 256, F32R),
            ("sel_bf", 8 * P, BF16), ("F_bf", S1, BF16), ("F_tmp", S1, BF16))
        (O_split, mg_hi, mg_lo, gate, acc) = region(
            ("O_split", SHIFT + 16 * S1, F32R), ("mg_hi", KD * S1, F32R), ("mg_lo", KD * S1, F32R),
            ("gate", 4 * S1, F32), ("acc", 4 * S1, F32))
        mid_hi, mid_lo = region(("mid_hi", KF * S2, F32R), ("mid_lo", KF * S2, F32R))
        (Q2, K2, c_hi, c_lo, cos_t, sin_t) = region(
            ("Q2", H2 * S2, F32), ("K2", KD * S2, F32), ("c_hi", 5 * S2 + C_PAD, F32R),
            ("c_lo", 5 * S2 + C_PAD, F32R),
            ("cos_t", S2, F32), ("sin_t", S2, F32))
        (Q2_, K2_, q2_hi, q2_lo, k2_hi, k2_lo, v2_hi, v2_lo, PT2_hi, PT2_lo) = region(
            ("Q2_", H2 * S2, F32), ("K2_", KD * S2, F32), ("q2_hi", 2 * S2, F32R), ("q2_lo", 2 * S2, F32R),
            ("k2_hi", 2 * S2, F32R), ("k2_lo", 2 * S2, F32R), ("v2_hi", 2 * 5 * P, F32R),
            ("v2_lo", 2 * 5 * P, F32R), ("PT2_hi", 4 * S2, F32R), ("PT2_lo", 4 * S2, F32R))
        (OQ_lo, OK_hi) = region(("OQ_lo", H2 * S2 - SHIFT, F32R), ("OK_hi", SHIFT + KD * S2, F32R))
        (pool_a, pool_s, pool_c) = region(
            ("pool_a", 2 * S2, F32), ("pool_s", 2 * S2, F32), ("pool_c", 4 * P, F32))
        PS = ctx.enter_context(nc.psum_tensor("PS", [P, 4, 2 * 512], F32))

        w_in = [sem(f"w_in{i}") for i in range(RING)]
        w_hi_ok, w_lo_ok, w_used = sem("w_hi_ok"), sem("w_lo_ok"), sem("w_used")
        full = sem("full")
        free = [sem(f"free{i}") for i in range(4)]
        x_in, cst_in, set_up = sem("x_in"), sem("cst_in"), sem("set_up")
        ada_in = [sem(f"ada_in{i}") for i in range(4)]
        ada_used, ada_mm, cond_ok = sem("ada_used"), sem("ada_mm"), sem("cond_ok")
        n_mean, n_xc, n_sq, n_sq_used, n_ln, n_r0, n_rs = (
            sem(s) for s in ("n_mean", "n_xc", "n_sq", "n_sq_used", "n_ln", "n_r0", "n_rs"))
        t_ok, t_hi, h_ok = sem("t_ok"), sem("t_hi"), sem("h_ok")
        x4_ok = sem("x4_ok")
        xr_ok = sem("xr_ok")
        x_ok = sem("x_ok")
        dve, act, pool = sem("dve_step"), sem("act_step"), sem("pool_step")
        f_z, f_e, f_ln, f_ok = sem("f_z"), sem("f_e"), sem("f_ln"), sem("f_ok")
        q_ok, v_ok = sem("q_ok"), sem("v_ok")
        tab_in, zero_ok, kr_ok, rope_hi = sem("tab_in"), sem("zero_ok"), sem("kr_ok"), sem("rope_hi")
        rope_lo = sem("rope_lo")
        stg_hi, stg_lo, rel_in, rel_ok = sem("stg_hi"), sem("stg_lo"), sem("rel_in"), sem("rel_ok")
        s_full, nmax_ok, p_ok, d_ok = sem("s_full"), sem("nmax_ok"), sem("p_ok"), sem("d_ok")
        pt_full, pt_hi, pt_lo, pv_done = sem("pt_full"), sem("pt_hi"), sem("pt_lo"), sem("pv_done")
        o_hi, o_lo = sem("o_hi"), sem("o_lo")
        g_ok, a_ok, m_ok, mh_ok, ml_ok = sem("g_ok"), sem("a_ok"), sem("m_ok"), sem("mh_ok"), sem("ml_ok")
        y_ok, c_ok, s_ok, mid_ok, midh_ok, midl_ok = (
            sem(s) for s in ("y_ok", "c_ok", "s_ok", "mid_ok", "midh_ok", "midl_ok"))
        out_done = sem("out_done")

        def x1(k):
            return X[:, k * S2 + META:(k + 1) * S2]

        def ht(t, k, n=S1):
            return t[:, k * S2:k * S2 + n]

        def v1(name, i):
            c = VEC[name]
            if isinstance(i, int):
                return vec[:, c + i:c + i + 1]
            return vec[:, ds(i + c, 1)]

        def v1w(name, w):
            return vec[:, VEC[name]:VEC[name] + w]

        def wtile(t, slot, kk, m, cols=4):
            o = slot * BLK + (kk * cols + m) * P
            return t[:, o:o + P]

        def psum1(k):
            return PS[:, k, 0:S1]

        def psum2(k):
            return PS[:, k, COL2:COL2 + S2]

        def psumT(k, T):
            return psum1(k) if T == S1 else psum2(k)

        def wait_tile(eng, name, bi, i, g=0):
            n, end, _ = BATCH[name][bi]
            if i == n - 1:
                eng.wait_ge(w_used, g * NB[name] + (BLK0[name] + end + 1 + RING))
            else:
                per = sum(x[0] - 1 for x in BATCH[name])
                own = sum(x[0] - 1 for x in BATCH[name][:bi])
                eng.wait_ge(full, g * per + (FULL0[name] + own + i + 1))

        def wait_out(eng, name, bi, i, g=0):
            eng.wait_ge(free[(BATCH[name][bi][2] + i) % 4], free_before(name, bi, i, g) + 2)

        def out_sem(name, bi, i):
            return free[(BATCH[name][bi][2] + i) % 4]

        class Chain:

            def __init__(self, eng, s):
                self.eng, self.s, self.base, self.k, self.g, self.per = eng, s, 0, 0, None, 0

            def done(self, ins):
                ins.then_inc(self.s, 1)
                self.k += 1

            def wait(self):
                n = self.base + self.k
                self.eng.wait_ge(self.s, n if self.g is None else self.g * self.per + n)

            def turn(self, g, per):
                self.base, self.k, self.g, self.per = self.base + self.k, 0, g, per

            def end(self, turns):
                assert self.k == self.per, (self.k, self.per)
                self.base, self.k, self.g = self.base + turns * self.per, 0, None

        def over_pairs(eng, pairs, U, step, chain=None, per=0):
            for t in range(LEAD):
                step(0, t, True, False)
            with eng.Fori(0, pairs - 1) as p:
                if chain is not None:
                    chain.turn(p, per)
                for t in range(LEAD, U + LEAD):
                    if t < U:
                        step(p, t, False, False)
                    else:
                        step(p + 1, t - U, False, False)
            if chain is not None:
                chain.end(pairs - 1)
            for t in range(LEAD, U):
                step(pairs - 1, t, False, True)

        def qk_rows(mla, name, par):
            if mla and name == "q":
                return slice(0, P)
            return slice(64 * par, 64 * par + 64)

        def head_raw(kind, name, p, par):
            mla = kind == "mla"
            o = 8 if kind == "chunk" else 0
            r = qk_rows(mla, name, par)
            if name == "q":
                return Q2[:, ds(p * (2 * S2) + par * S2, S2)] if mla else QK[r, ds(p * S1 + o * S1, S1)]
            if name == "k":
                return K2[r, ds(p * S2, S2)] if mla else QK[r, ds(p * S1 + (o + 4) * S1, S1)]
            if name == "rel":
                return rel_raw[:, par * 256:(par + 1) * 256]
            if mla:
                return v_raw2[:, :].rearrange("p (t c) -> p t c", t=5)[:, :, ds(p * P + par * 64, 64)]
            return v_raw[:, :].rearrange("p (t c) -> p t c", t=4)[:, :, ds(p * P + (o * 64 + par * 64), 64)]

        def head_part(kind, name, par, hi):
            mla = kind == "mla"
            r = qk_rows(mla, name, par)
            if name in ("q", "k"):
                t = {("q", 1): (q_hi, q2_hi), ("q", 0): (q_lo, q2_lo), ("k", 1): (k_hi, k2_hi),
                     ("k", 0): (k_lo, k2_lo)}[name, hi][mla]
                return t[r, par * S2:(par + 1) * S2] if mla else t[r, :]
            if name == "rel":
                return (rel_hi if hi else rel_lo)[:, par * 256:(par + 1) * 256]
            t, n = ((v2_hi, v2_lo) if mla else (v_hi, v_lo))[1 - hi], 5 if mla else 4
            return t[:, par * n * P:(par + 1) * n * P].rearrange("p (t c) -> p t c", t=n)[:, :, par * 64:par * 64 + 64]

        block = ctx.enter_context(nc.Block())

        @block.sync
        def _(sp):
            sp.dma_start(vec[:, :], vecs).then_inc(cst_in, 16)
            sp.dma_start(ident[:, :], consts[:, 0:P]).then_inc(cst_in, 16)
            sp.dma_start(work[:, 0:2 * P], consts[:, P:]).then_inc(cst_in, 16)
            sp.dma_start(X[:, :].rearrange("p (k t) -> p k t", k=KD)[:, :, META:S2],
                         xT.rearrange("k p t -> p k t")).then_inc(x_in, 16)
            sp.dma_start(X[:, :].rearrange("p (k t) -> p k t", k=KD)[:, :, 0:META],
                         meta.rearrange("k p t -> p k t")).then_inc(x_in, 16)

            def load_w(n, slot):
                sp.wait_ge(w_lo_ok, n + 1)
                sp.dma_start(w_raw[:, slot * BLK:(slot + 1) * BLK],
                             stream[ds(n, 1)].rearrange("a p c -> p (a c)")).then_inc(w_in[slot], 16)

            def load_ada(n, slot):
                sp.wait_ge(ada_used, n + 1)
                sp.dma_start(ada_w[:, slot * D:(slot + 1) * D],
                             ada[ds(n, 1)].rearrange("a p c -> p (a c)")).then_inc(ada_in[slot], 16)

            for n in range(4):
                load_ada(n, n)
            for n in range(4):
                load_w(n, n)
            for n in range(4, 12):
                load_ada(n, n % 4)
            for n in range(4, 8):
                load_w(n, n % 4)
            for n in range(12, 20):
                load_ada(n, n % 4)
            with sp.Fori(0, 3) as g:
                for j in range(4):
                    for i in (2 * j, 2 * j + 1):
                        load_ada(g * 8 + (20 + i), i % 4)
                    load_w(g * 4 + (8 + j), j)
            for j in range(4):
                load_ada(44 + j, j)
                load_w(20 + j, j)
            with sp.Fori(0, (NSTREAM - 24) // 4) as g:
                for j in range(4):
                    load_w(g * 4 + (24 + j), j)
            for n in range(NSTREAM - NSTREAM % 4, NSTREAM):
                load_w(n, n % 4)

            for k in range(KD):
                sp.wait_ge(x_ok, 7 * KD + k + 1)
            sp.dma_start(yT.rearrange("k p t -> p k t"),
                         X[:, :].rearrange("p (k t) -> p k t", k=KD)[:, :, META:S2]).then_inc(out_done, 16)
            sp.wait_ge(out_done, 16)

        @block.tensor
        def _(pe):
            cnt_ = {"sq": 0, "norm": 0}
            pe.sem_inc(w_used, RING)
            pe.sem_inc(pt_full, 2)
            pe.sem_inc(pv_done, 2)

            def spans(T):
                return [(0, S1, 0)] if T == S1 else [(0, HALF2, COL2), (HALF2, S2, COL2)]

            def mm3(out, w_h, w_l, x_h, x_l, cuts, start, stop):
                last = None
                for i, (w, x) in enumerate(((w_l, x_h), (w_h, x_l), (w_h, x_h))):
                    for a, b, c0 in cuts:
                        last = pe.matmul(out[:, c0 + a:c0 + b], w, x[:, a:b], start=start and i == 0,
                                         stop=stop and i == 2)
                return last

            def begin(name, batch, i, g):
                pe.wait_ge(free[(BATCH[name][batch][2] + i) % 4], free_before(name, batch, i, g) + 1)

            def batch(name, bi, g, n, blocks, tiles, kks, cols, x, T, h_ready=None, w_tile=None):
                done = 0
                for bi_, b in enumerate(blocks):
                    slot = (BLK0[name] + b) % RING
                    kk = kks[bi_] if isinstance(kks, tuple) else kks
                    pe.wait_ge(w_lo_ok, n + (b + 1 + RING))
                    for m in range(tiles):
                        if bi_ == 0:
                            begin(name, bi, m, g)
                        for k in range(kk):
                            kt = done + k
                            if m == 0 and h_ready is not None:
                                pe.wait_ge(h_ok, h_ready + kt + 1)
                            xh, xl = x(kt)
                            last = mm3(PS[:, m, :], wtile(w_hi, slot, k, m, cols), wtile(w_lo, slot, k, m, cols),
                                       xh, xl, spans(T), bi_ == 0 and k == 0,
                                       bi_ == len(blocks) - 1 and k == kk - 1)
                        if bi_ == len(blocks) - 1 and m < tiles - 1:
                            last.then_inc(full, 1)
                    last.then_inc(w_used, 1)
                    done += kk

            def norm(n, T, ready, mean, src, four=0):
                if mean:
                    first = 3 if four else 0
                    for k in range(first, n):
                        if four and k == first:
                            pe.wait_ge(x4_ok, four)
                        elif ready is not None:
                            pe.wait_ge(ready[0], ready[1] + k + 1)
                        x = ht(m_out, 0) if four and k == first else src(k)
                        for a, b, c0 in spans(T):
                            last = pe.matmul(PS[:, 1, c0 + a:c0 + b], ones[:, :], x[:, a:b],
                                             start=k == first, stop=k == n - 1)
                    last.then_inc(n_mean, 1)
                if cnt_["norm"]:
                    pe.wait_ge(n_rs, cnt_["norm"])
                cnt_["norm"] += 1
                for k in range(n):
                    cnt_["sq"] += 1
                    pe.wait_ge(n_sq, cnt_["sq"])
                    for a, b, c0 in spans(T):
                        last = pe.matmul(PS[:, 0, c0 + a:c0 + b], ones[:, :], ht(work, k % (4 if mean else 2), T)[:, a:b],
                                         start=k == 0, stop=k == n - 1)
                    last.then_inc(n_sq_used, 1)

            def hx(T):
                return lambda k: (ht(H_hi, k, T), ht(H_lo, k, T))

            def attention(kind):
                tiles, keys, T, pairs, c0, u0, p0 = ATT[kind]
                nq = len(tiles)
                U = 2 * nq
                mla = kind == "mla"
                qh, ql, kh, kl = (q2_hi, q2_lo, k2_hi, k2_lo) if mla else (q_hi, q_lo, k_hi, k_lo)
                vh, vl = (v2_hi, v2_lo) if mla else (v_hi, v_lo)
                ns, s0 = len(STG[kind]), STG0[kind]

                def scores(p, t):
                    par, i = divmod(t, nq)
                    q0, qn, ke = tiles[i]
                    if i == 0:
                        pe.wait_ge(stg_lo, p * (2 * ns) + (s0 + par * ns + ns - 1))
                    pe.wait_ge(p_ok, p * U + (u0 + t + 1))
                    if mla:
                        rows = slice(0, P)
                        o = par * S2
                        cuts = [(0, 256)] + ([(256, max(ke, 512))] if ke > 256 else [])
                    else:
                        rows = slice(64 * par, 64 * par + 64)
                        o = 0
                        cuts = [(0, max(ke, 256))]
                    out = PS[:, t % 2, :]
                    for a, b in cuts:
                        for j, (l, r) in enumerate(((ql, kh), (qh, kl), (qh, kh))):
                            pe.matmul(out[0:qn, c0 + a:c0 + b], l[rows, o + q0:o + q0 + qn],
                                      r[rows, o + a:o + b], start=j == 0, stop=False, skip_group_check=True)
                    if kind == "fox":
                        b = cuts[0][1]
                        pe.matmul(out[:, 0:b], sel_bf[:, ds(p * (2 * P) + par * P, P)], F_bf[:, 0:b],
                                  start=False, stop=False, skip_group_check=True)
                    if kind == "chunk":
                        lo = 0 if q0 else P
                        for r in (rel_lo, rel_hi):
                            pe.matmul(out[:, q0 - P + lo:q0 + P], ident_r[:, :],
                                      r[:, par * 256 + lo:par * 256 + 256], start=False, stop=False,
                                      skip_group_check=True)
                    mask = chunk_bf if kind == "chunk" else causal_bf
                    pe.matmul(out[0:qn, c0 + q0:c0 + ke], ident_bf[:, 0:qn], mask[:, 0:ke - q0],
                              start=False, stop=True, skip_group_check=True).then_inc(s_full, 1)

                def turn_over(p, w):
                    i = w % nq
                    qn = tiles[i][1]
                    pe.wait_ge(d_ok, p * U + (u0 + w + 1))
                    pe.wait_ge(pt_lo, p * U + (u0 + w + 1))
                    pb = ht(work, w % 2, S2)
                    for j in range(i + 1):
                        k0, kn = keys[j]
                        o = 512 * (w % 2) + j * qn
                        last = pe.transpose(PS[0:kn, 2, o:o + qn], pb[0:qn, k0:k0 + kn], ident[0:qn, 0:qn])
                    last.then_inc(pt_full, 1)

                def outputs(p, par, late):
                    pe.wait_ge(pt_lo, p * U + (u0 + par * nq + (nq if late else 2) + 2))
                    pe.wait_ge(stg_lo, p * (2 * ns) + (s0 + (par + 1) * ns))
                    if par == 0 and not late:
                        pe.wait_ge(o_lo, p + (p0 + 1))
                    n = nq if late else 2
                    for j in range(n):
                        kn = keys[j][1]
                        a, b = (256 if late else 0), (T if late else 256)
                        if mla and late:
                            a = (256, 256, 256, 272, 456)[j]
                        if mla and j == nq - 1:
                            sh, sl, so = work_r[:, 2 * S2:3 * S2], work_r[:, 3 * S2:4 * S2], 0
                        else:
                            sh, sl, so = (PT2_hi, PT2_lo, j * S2) if mla else (PT_hi, PT_lo, j * S1)
                        vo = (par * nq + j) * P
                        for n_, (l, r) in enumerate(((vl, sh), (vh, sl), (vh, sh))):
                            last = pe.matmul(
                                PS[:, 3, 256 + a:256 + b], l[0:kn, vo:vo + P], r[0:kn, so + a:so + b],
                                start=par == 0 and j == 0 and n_ == 0,
                                stop=par == 1 and j == n - 1 and n_ == 2, skip_group_check=True)
                    last.then_inc(pv_done, 1)

                def step(p, t, first, last):
                    if t + 1 < U:
                        scores(p, t + 1)
                    elif not last:
                        scores(p + 1, 0)
                    if t % nq == 3:
                        outputs(p, t // nq, False)
                    if t == nq + 1:
                        outputs(p, 0, True)
                    elif t == 1 and not first:
                        outputs(p - 1, 1, True)
                    turn_over(p, t)

                scores(0, 0)
                over_pairs(pe, pairs, U, step)
                outputs(pairs - 1, 1, True)

            pe.wait_ge(set_up, SET_UP)
            pe.wait_ge(x_in, 32)
            norm(KD, S1, None, True, x1)
            def ada_turn(c):
                pe.wait_ge(ada_used, c * KD + (KD + 4))
                for m in range(KD):
                    last = pe.matmul(PS[:, 3, 512 + m:513 + m], ada_acc[:, m * P:(m + 1) * P], ones[:, 0:1],
                                     start=True, stop=True, skip_group_check=True)
                last.then_inc(ada_mm, 1)

            ada_turn(0)
            ada_turn(1)
            batch("forget", 0, 0, BLK0["forget"], [0], 1, 8, 1, hx(S1), S1, 0)
            with pe.Fori(0, 4) as g:
                batch("qk", 0, g, g * 4 + BLK0["qk"], range(4), 4, 2, 4, hx(S1), S1, 0)
                ada_turn(g + 2)
            with pe.Fori(0, 2) as g:
                for b in range(4):
                    slot = (BLK0["v"] + b) % RING
                    pe.wait_ge(w_lo_ok, g * 4 + (BLK0["v"] + b + 1 + RING))
                    for t in range(4):
                        if b == 0:
                            begin("v", 0, t, g)
                        for k in range(2):
                            kt = b * 2 + k
                            wr = slice(slot * BLK + k * 512, slot * BLK + k * 512 + 512)
                            hs = slice(kt * S2 + t * P, kt * S2 + t * P + P)
                            for j, (l, r) in enumerate(((H_lo, w_hi), (H_hi, w_lo), (H_hi, w_hi))):
                                last = pe.matmul(PS[:, t, 0:512], l[:, hs], r[:, wr],
                                                 start=kt == 0 and j == 0, stop=kt == 7 and j == 2)
                        if b == 3 and t < 3:
                            last.then_inc(full, 1)
                    last.then_inc(w_used, 1)
            for k in range(4):
                pe.wait_ge(free[k], FREE0["merge"][k] + 1)
            pe.wait_ge(f_ok, 1)
            attention("fox")
            attention("chunk")
            pe.wait_ge(o_lo, 8 + 1)

            def ox(kind):
                o = SHIFT + (0 if kind == "fox" else 8) * S1
                return lambda k: (O_split[:, o + k * S1:o + (k + 1) * S1],
                                  O_split[:, o + (4 + k) * S1:o + (5 + k) * S1])

            with pe.Fori(0, 2) as g:
                n = g * 12 + BLK0["merge"]
                batch("merge", 0, g, n, range(0, 4), 4, 2, 4, hx(S1), S1)
                batch("merge", 1, g, n, range(4, 6), 4, 2, 4, ox("fox"), S1)
                batch("merge", 2, g, n, range(6, 10), 4, 2, 4, hx(S1), S1)
                batch("merge", 3, g, n, range(10, 12), 4, 2, 4, ox("chunk"), S1)
            pe.wait_ge(ml_ok, 12)
            with pe.Fori(0, 2) as g:
                batch("out", 0, g, g * 4 + BLK0["out"], range(4), 4, 2, 4,
                      lambda k: (mg_hi[:, k * S1:(k + 1) * S1], mg_lo[:, k * S1:(k + 1) * S1]), S1)

            def ffn(up, down, T, h0, mid0):
                with pe.Fori(0, 11) as g:
                    batch(up, 0, g, g * 4 + BLK0[up], range(4), 4, 2, 4, hx(T), T, h0)
                pe.wait_ge(midl_ok, mid0 + KF + 1)
                with pe.Fori(0, 2) as g:
                    batch(down, 0, g, g * 12 + BLK0[down], range(12), 4, DOWN_ROWS, 4,
                          lambda k: (ht(mid_hi, k, T), ht(mid_lo, k, T)), T)

            def norm_after(nxt, n, T, ready, mean, src, four=0):
                for k in (0, 1):
                    pe.wait_ge(free[k], FREE0[nxt][k] + 1)
                norm(n, T, ready, mean, src, four)

            norm_after("up_a", KD, S1, (x_ok, 0), True, x1, 1)
            norm_after("up_a", KD, S1, (x_ok, 8), True, x1)
            ffn("up_a", "down_a", S1, 8, 0)
            norm_after("dqkv", KD, S1, (x_ok, 16), True, x1, 2)

            norm(KD, S2, None, False, None)
            batch("dqkv", 0, 0, BLK0["dqkv"], range(4), 4, 2, 4, hx(S2), S2, 16)
            batch("dqkv", 1, 0, BLK0["dqkv"], range(4, 6), 2, 4, 2, hx(S2), S2)
            norm_after("uq", 3, S2, None, False, None)
            norm(2, S2, None, False, None)
            pe.wait_ge(n_rs, cnt_["norm"])
            cx = lambda o: (lambda k: (ht(c_hi, o + k, S2), ht(c_lo, o + k, S2)))
            with pe.Fori(0, 2) as g:
                for b in range(4):
                    slot = (BLK0["uq"] + b) % RING
                    pe.wait_ge(w_lo_ok, g * 4 + (BLK0["uq"] + b + 1 + RING))
                    for j in range(2):
                        m = (2 * b + j) % 4
                        begin("uq", b, j, g)
                        for k in range(3):
                            pe.wait_ge(h_ok, 24 + k + 1)
                            xh, xl = cx(0)(k)
                            last = mm3(PS[:, m, :], wtile(w_hi, slot, k, j, 2), wtile(w_lo, slot, k, j, 2),
                                       xh, xl, spans(S2), k == 0, k == 2)
                        last.then_inc(full if j == 0 else w_used, 1)
            pe.wait_ge(h_ok, 29)
            for b in range(2):
                slot = (BLK0["uk"] + b) % RING
                pe.wait_ge(w_lo_ok, BLK0["uk"] + b + 1 + RING)
                for m in range(4):
                    begin("uk", b, m, 0)
                    for k in range(2):
                        xh, xl = cx(3)(k)
                        last = mm3(PS[:, m, :], wtile(w_hi, slot, k, m), wtile(w_lo, slot, k, m),
                                   xh, xl, spans(S2), k == 0, k == 1)
                    if m < 3:
                        last.then_inc(full, 1)
                last.then_inc(w_used, 1)
            for b in range(2):
                slot = (BLK0["uv"] + b) % RING
                pe.wait_ge(w_lo_ok, BLK0["uv"] + b + 1 + RING)
                for t in range(5):
                    begin("uv", b, t, 0)
                    t0 = KEYS2[t][0]
                    for k in range(2):
                        wr = slice(slot * BLK + k * 512, slot * BLK + k * 512 + 512)
                        cs = slice((3 + k) * S2 + t0, (3 + k) * S2 + t0 + P)
                        for j, (l, r) in enumerate(((c_lo, w_hi), (c_hi, w_lo), (c_hi, w_hi))):
                            last = pe.matmul(PS[:, t % 4, 0:512], l[:, cs], r[:, wr],
                                             start=k == 0 and j == 0, stop=k == 1 and j == 2)
                    if t < 4:
                        last.then_inc(full, 1)
                last.then_inc(w_used, 1)
            for k in range(4):
                pe.wait_ge(free[k], FREE0["wo"][k] + 1)
            attention("mla")
            pe.wait_ge(o_lo, 16 + 1)
            with pe.Fori(0, 2) as g:
                batch("wo", 0, g, g * 4 + BLK0["wo"], range(4), 4, 2, 4,
                      lambda k: (OK_hi[:, SHIFT + k * S2:SHIFT + (k + 1) * S2], ht(OQ_lo, 2 * k, S2)), S2)
            norm_after("up_b", KD, S2, None, False, None)
            norm(KD, S2, None, False, None)
            ffn("up_b", "down_b", S2, 29, KF)
            norm_after("pool", KD, S2, None, False, None)
            norm(KD, S2, None, False, None)
            for b in range(2):
                slot = (BLK0["pool"] + b) % RING
                pe.wait_ge(w_lo_ok, BLK0["pool"] + b + 1 + RING)
                for m in range(4):
                    begin("pool", b, m, 0)
                    grp = m // 2
                    for k in range(2):
                        kt = (2 * b + grp) * 2 + k
                        pe.wait_ge(h_ok, 37 + kt + 1)
                        xh, xl = hx(S2)(kt)
                        last = mm3(PS[:, m, :], wtile(w_hi, slot, grp * 2 + k, m % 2, 2),
                                   wtile(w_lo, slot, grp * 2 + k, m % 2, 2), xh, xl, spans(S2), k == 0, k == 1)
                    if m < 3:
                        last.then_inc(full, 1)
                last.then_inc(w_used, 1)
            norm_after("up_c", KD, S2, None, False, None)
            norm(KD, S2, None, False, None)
            ffn("up_c", "down_c", S2, 45, 2 * KF)
            for k in (0, 1):
                pe.wait_ge(free[k], FREE_END[k] + 1)
            norm(KD, S2, None, False, None)

        @block.gpsimd
        def _(gp):
            gp.sem_inc(w_lo_ok, RING)

            def lower(n, slot):
                gp.wait_ge(w_hi_ok, n + 1)
                o = slice(slot * BLK, (slot + 1) * BLK)
                gp.tensor_tensor(w_lo[:, o], w_raw[:, o], w_hi[:, o].bitcast(F32), ALU.subtract)\
                  .then_inc(w_lo_ok, 1)

            def lower_blocks(a, b):
                while a % RING and a < b:
                    lower(a, a % RING)
                    a += 1
                turns = (b - a) // RING
                if turns:
                    with gp.Fori(0, turns) as g:
                        for j in range(RING):
                            lower(g * RING + (a + j), j)
                for n in range(a + turns * RING, b):
                    lower(n, n % RING)

            def split_heads(kind):
                ns, s0 = len(STG[kind]), STG0[kind]
                with gp.Fori(0, ATT[kind][3]) as p:
                    for par in range(2):
                        for j, name in enumerate(STG[kind]):
                            n = s0 + par * ns + j
                            gp.wait_ge(stg_hi, p * (2 * ns) + (n + 1))
                            if par or j:
                                gp.wait_ge(stg_lo, p * (2 * ns) + n)
                            gp.tensor_tensor(head_part(kind, name, par, 0), head_raw(kind, name, p, par),
                                             head_part(kind, name, par, 1).bitcast(F32), ALU.subtract)\
                              .then_inc(stg_lo, 1)

            lower_blocks(0, BLK0["merge"] + RING)
            split_heads("fox")
            split_heads("chunk")
            lower_blocks(BLK0["merge"] + RING, BLK0["wo"] + RING)
            gp.wait_ge(w_lo_ok, BLK0["wo"] + 2 * RING)
            for par, r in ((0, slice(64, 96)), (1, slice(32, 64))):
                gp.wait_ge(rope_hi, par + 1)
                gp.tensor_tensor(k2_lo[r, par * S2:(par + 1) * S2], kr[r, :],
                                 k2_hi[r, par * S2:(par + 1) * S2].bitcast(F32), ALU.subtract)\
                  .then_inc(rope_lo, 1)
            gp.wait_ge(rope_lo, 2)
            split_heads("mla")
            lower_blocks(BLK0["wo"] + RING, NBLK)

        @block.scalar
        def _(act_):
            cnt_ = {"sq": 0, "xc": 0, "ln": 0, "t": 0}
            chain = Chain(act_, act)
            act_.sem_inc(p_ok, 2)

            def log_and_exp():
                act_.preload_act_table_set("natural_log_exp_and_others")

            def copy(out, in_, scale=1.0):
                return act_.activation(out, in_, ACT.Copy, scale=scale)

            def upper(name, b, g=0):
                n = BLK0[name] + b
                slot = n % RING
                per = NB[name] if not isinstance(g, int) else 0
                g = g if per else 0
                act_.wait_ge(w_in[slot], g * (16 * per // RING) + 16 * (n // RING + 1))
                act_.wait_ge(w_used, g * per + (n + 1))
                o = slice(slot * BLK, (slot + 1) * BLK)
                copy(w_hi[:, o], w_raw[:, o]).then_inc(w_hi_ok, 1)

            def stage(name, g=0, take=None):
                b = RING
                for bi, (_, end, _) in enumerate(BATCH[name]):
                    while b < end + RING:
                        upper(name, b, g)
                        b += 1
                    if take is not None:
                        take(bi)
                while b < NB[name] + RING:
                    upper(name, b, g)
                    b += 1

            def loop(name, turns, take=None, per=0):
                with act_.Fori(0, turns) as g:
                    chain.turn(g, per)
                    stage(name, g, None if take is None else lambda bi: take(g, bi))
                chain.end(turns)

            def norm(n, T, eps, src, ready, mean=False):
                if cnt_["t"]:
                    act_.wait_ge(h_ok, cnt_["t"])
                bufs = 4 if mean else 2
                for k in range(n):
                    if mean:
                        cnt_["xc"] += 1
                        act_.wait_ge(n_xc, cnt_["xc"])
                    else:
                        ready(k)
                    if k >= bufs:
                        act_.wait_ge(n_sq_used, cnt_["sq"] + 1 - bufs)
                    act_.activation(ht(work, k % bufs, T), src(k), ACT.Square).then_inc(n_sq, 1)
                    cnt_["sq"] += 1
                act_.wait_ge(n_sq_used, cnt_["sq"])
                cnt_["ln"] += 1
                act_.activation(ht(work, 2, T), psumT(0, T), ACT.Ln, bias=v1("eps", eps),
                                scale=1.0 / (n * P)).then_inc(n_ln, 1)
                act_.wait_ge(n_ln, cnt_["ln"])
                act_.activation(ht(work, 3, T), ht(work, 2, T), ACT.Exp, scale=-0.5).then_inc(n_r0, 1)

            def affine(gain, bias, n0):
                for k in range(KD):
                    act_.wait_ge(xr_ok, n0 + k + 1)
                    act_.activation(x1(k), x1(k), ACT.Identity, bias=v1(bias, k), scale=v1(gain, k)).then_inc(x_ok, 1)

            def split(n, T, hi):
                for k in range(n):
                    cnt_["t"] += 1
                    act_.wait_ge(t_ok, cnt_["t"])
                    copy(hi(k), ht(work, k % 2, T)).then_inc(t_hi, 1)

            def attention(kind):
                tiles, keys, T, pairs, c0, u0, p0 = ATT[kind]
                nq = len(tiles)
                U = 2 * nq
                mla = kind == "mla"
                ns, s0 = len(STG[kind]), STG0[kind]

                def load_rel(p, par):
                    act_.dma_start(rel_raw[:, par * 256:(par + 1) * 256],
                                   rel[ds(p * 2 + par, 1)].rearrange("h p c -> p (h c)")).then_inc(rel_in, 16)

                def stage_head(p, par, j):
                    name = STG[kind][j]
                    if name == "rel":
                        act_.wait_ge(rel_ok, p * 2 + (par + 1))
                    if name == "v" and not (isinstance(p, int) and p0 + p + par == 0):
                        act_.wait_ge(pv_done, p * 4 + (4 * p0 + 2 * par))
                    copy(head_part(kind, name, par, 1), head_raw(kind, name, p, par)).then_inc(stg_hi, 1)

                def exps(p, t):
                    q0, qn, ke = tiles[t % nq]
                    act_.wait_ge(nmax_ok, p * U + (u0 + t + 1))
                    act_.wait_ge(pt_full, p * U + (u0 + t + 1))
                    act_.activation(ht(work, t % 2, S2)[0:qn, 0:ke], PS[0:qn, t % 2, c0:c0 + ke],
                                    ACT.Exp, bias=small[0:qn, t % 2:t % 2 + 1],
                                    accum_out=small[0:qn, 2 + t % 2:3 + t % 2]).then_inc(p_ok, 1)

                def weights(p, w):
                    par, i = divmod(w, nq)
                    q0, qn, _ = tiles[i]
                    act_.wait_ge(pt_full, p * U + (u0 + w + 3))
                    if i in (0, 2):
                        act_.wait_ge(pv_done, p * 4 + (4 * p0 + 2 * par + 1 + i // 2))
                    nj = min(i + 1, 4)
                    po = 512 * (w % 2)
                    if i == 4:
                        copy(work_r[0:META, 2 * S2 + q0:2 * S2 + q0 + qn], PS[0:META, 2, po + 4 * qn:po + 5 * qn])
                    dst = PT2_hi if mla else PT_hi
                    copy(dst[:, :].rearrange("p (j t) -> p j t", t=T)[:, 0:nj, q0:q0 + qn],
                         PS[:, 2, po:po + nj * qn].rearrange("p (j t) -> p j t", t=qn)).then_inc(pt_hi, 1)

                def take_out(p):
                    act_.wait_ge(pv_done, p * 4 + (4 * p0 + 6))
                    if mla:
                        copy(OK_hi[:, ds(p * S2 + SHIFT, S2)], PS[:, 3, 256:256 + S2]).then_inc(o_hi, 1)
                    else:
                        o = 8 if kind == "chunk" else 0
                        copy(O_split[:, ds(p * S1 + (o * S1 + SHIFT), S1)], PS[:, 3, 256:256 + S1]).then_inc(o_hi, 1)

                def step(p, t, first, last):
                    par, i = divmod(t, nq)
                    exps(p, t)
                    if t:
                        weights(p, t - 1)
                    elif not first:
                        weights(p - 1, U - 1)
                    nxt, other = (p, 1) if par == 0 else (p + 1, 0)
                    if not (last and par) and i < ns:
                        if kind == "chunk" and i == 0:
                            load_rel(nxt, other)
                        stage_head(nxt, other, i)
                    if t == 2 and not first:
                        take_out(p - 1)

                act_.wait_ge(pv_done, 4 * p0 + 2)
                if kind == "chunk":
                    load_rel(0, 0)
                for j in range(ns):
                    stage_head(0, 0, j)
                over_pairs(act_, pairs, U, step)
                weights(pairs - 1, U - 1)
                take_out(pairs - 1)

            def ffn(up, down, T, layer, mid0, y0, down_take=None, down_per=0):
                def take(g, _):
                    act_.wait_ge(midl_ok, g * 2 + (mid0 + 1))
                    for m in range(4):
                        wait_tile(act_, up, 0, m, g)
                        c = layer * 8 * KF + 4 * m
                        act_.activation(ht(work, m, T), psumT(m, T), ACT.Identity,
                                        bias=v1("conv", g * 16 + (c + 3)), scale=v1("conv", g * 16 + (c + 2)))\
                            .then_inc(y_ok, 1)
                    for j in range(2):
                        wait_out(act_, up, 0, 2 * j, g)
                        act_.activation(ht(work, 2 * j, T), ht(work, 2 * j, T), ACT.Silu).then_inc(s_ok, 1)
                    for j in range(2):
                        act_.wait_ge(mid_ok, g * 2 + (mid0 + j + 1))
                        copy(mid_hi[:, ds((g * 2 + j) * S2, T)], ht(work, 2 * j + 1, T)).then_inc(midh_ok, 1)
                loop(up, 11, take)
                log_and_exp()
                loop(down, 2, down_take, down_per)

            act_.wait_ge(cst_in, 48)
            act_.activation(cond[:, :], v1w("c", 8), ACT.Silu).then_inc(cond_ok, 1)
            log_and_exp()
            for b in range(RING):
                upper("forget", b)
            norm(KD, S1, 0, lambda k: ht(XC, k), None, True)
            split(KD, S1, lambda k: ht(H_hi, k))

            def take_forget(_):
                act_.wait_ge(f_z, 1)
                chain.done(act_.activation(work[0:8, 3 * S2:3 * S2 + S1], work[0:8, 3 * S2:3 * S2 + S1],
                                           ACT.Exp, scale=-1.0))
                chain.wait()
                act_.activation(work[0:8, 3 * S2:3 * S2 + S1], work[0:8, 3 * S2:3 * S2 + S1],
                                ACT.Ln, bias=1.0).then_inc(f_ln, 1)
            stage("forget", 0, take_forget)
            loop("qk", 4)
            loop("v", 2)
            act_.wait_ge(zero_ok, 4)
            for k in range(4):
                act_.wait_ge(free[k], FREE0["merge"][k] + 1)
            attention("fox")
            attention("chunk")

            def take_merge(g, bi):
                for m in range(4):
                    if bi in (0, 2):
                        if bi == 2:
                            wait_out(act_, "merge", 1, m, g)
                        else:
                            act_.wait_ge(a_ok, g * 4 + (m + 1))
                        wait_tile(act_, "merge", bi, m, g)
                        act_.activation(gate[:, m * S1:(m + 1) * S1], psum1(m), ACT.Sigmoid)\
                            .then_inc(out_sem("merge", bi, m), 1)
                    if bi == 3:
                        act_.wait_ge(a_ok, g * 4 + (4 + m + 1))
                        copy(mg_hi[:, ds((g * 4 + m) * S1, S1)], acc[:, m * S1:(m + 1) * S1]).then_inc(mh_ok, 1)
            loop("merge", 2, take_merge)
            log_and_exp()
            loop("out", 2)
            norm(KD, S1, 0, x1, None, True)
            affine("ln1_g", "ln1_b", 0)
            norm(KD, S1, 0, lambda k: ht(XC, k), None, True)
            split(KD, S1, lambda k: ht(H_hi, k))
            ffn("up_a", "down_a", S1, 0, 0, 0)
            norm(KD, S1, 0, x1, None, True)
            affine("ln2_g", "ln2_b", KD)

            act_.wait_ge(w_used, BLK0["dqkv"] + RING)
            act_.dma_start(cos_t[:, :], rope[0]).then_inc(tab_in, 16)
            act_.dma_start(sin_t[:, :], rope[1]).then_inc(tab_in, 16)
            act_.wait_ge(x_in, 32)
            x2 = lambda k: ht(X, k, S2)
            x_new = lambda base: (lambda k: act_.wait_ge(x_ok, base + k + 1))
            norm(KD, S2, 1, x2, x_new(24))
            split(KD, S2, lambda k: ht(H_hi, k, S2))
            stage("dqkv")
            norm(3, S2, 1, lambda k: ht(Q2, k, S2), lambda k: wait_out(act_, "dqkv", 0, k))
            split(3, S2, lambda k: ht(c_hi, k, S2))
            norm(2, S2, 1, lambda k: ht(Q2, 3 + k, S2),
                 lambda k: wait_out(act_, "dqkv", k, 3 if k == 0 else 0))
            split(2, S2, lambda k: ht(c_hi, 3 + k, S2))

            def take_uq(g, bi):
                for j in range(2):
                    m = BATCH["uq"][bi][2] + j
                    wait_tile(act_, "uq", bi, j, g)
                    act_.activation(Q2[:, ds((g * 8 + (2 * bi + j)) * S2, S2)], psum2(m), ACT.Copy,
                                    scale=(NOPE + ROPE) ** -0.5).then_inc(q_ok, 1)
            loop("uq", 2, take_uq)

            def take_uk(bi):
                for m in range(4):
                    wait_tile(act_, "uk", bi, m)
                    copy(ht(K2, 4 * bi + m, S2), psum2(m)).then_inc(out_sem("uk", bi, m), 1)
            stage("uk", 0, take_uk)
            stage("uv")
            for k in range(4):
                act_.wait_ge(free[k], FREE0["wo"][k] + 1)
            act_.wait_ge(zero_ok, 8)
            act_.wait_ge(kr_ok, 2)
            for par, r in ((0, slice(64, 96)), (1, slice(32, 64))):
                copy(k2_hi[r, par * S2:(par + 1) * S2], kr[r, :]).then_inc(rope_hi, 1)
            act_.wait_ge(zero_ok, 10)
            attention("mla")

            def take_m(name):
                def take(g, bi):
                    for m in range(4):
                        wait_tile(act_, name, bi, m, g)
                        copy(m_out[:, ds((g * 4 + m) * S2, S2)], psum2(m)).then_inc(out_sem(name, bi, m), 1)
                return take

            def m_ready(name):
                return lambda k: wait_out(act_, name, 0, k % 4, k // 4)
            mt = lambda k: ht(m_out, k, S2)
            loop("wo", 2, take_m("wo"))
            norm(KD, S2, 1, mt, m_ready("wo"))
            norm(KD, S2, 1, x2, x_new(32))
            split(KD, S2, lambda k: ht(H_hi, k, S2))
            ffn("up_b", "down_b", S2, 1, KF, 44, take_m("down_b"))
            norm(KD, S2, 1, mt, m_ready("down_b"))
            norm(KD, S2, 1, x2, x_new(40))
            split(KD, S2, lambda k: ht(H_hi, k, S2))

            def take_pool(bi):
                for m in range(4):
                    wait_tile(act_, "pool", bi, m | 1)
                    act_.activation(ht(m_out, 4 * bi + m, S2), psum2(m), ACT.Copy,
                                    scale=v1("pool_scale", 4 * bi + m)).then_inc(out_sem("pool", bi, m), 1)
            stage("pool", 0, take_pool)
            norm(KD, S2, 1, mt, lambda k: wait_out(act_, "pool", k // 4, k % 4))
            norm(KD, S2, 1, x2, x_new(48))
            split(KD, S2, lambda k: ht(H_hi, k, S2))
            ffn("up_c", "down_c", S2, 2, 2 * KF, 88, take_m("down_c"))
            norm(KD, S2, 1, mt, m_ready("down_c"))

        @block.vector
        def _(v):
            cnt_ = {"r0": 0, "mean": 0, "hi": 0}
            chain = Chain(v, dve)
            for k in range(4):
                v.sem_inc(free[k], 1)
            v.sem_inc(ada_used, 4)
            v.sem_inc(pt_lo, 2)
            v.sem_inc(o_lo, 1)
            v.sem_inc(midl_ok, 1)
            v.sem_inc(a_ok, 4)
            v.sem_inc(ml_ok, 4)

            def loop(turns, per, body):
                with v.Fori(0, turns) as g:
                    chain.turn(g, per)
                    body(g)
                chain.end(turns)

            def less_mean(n, T, src, xc):
                cnt_["mean"] += 1
                v.wait_ge(n_mean, cnt_["mean"])
                for k in range(n):
                    v.scalar_tensor_tensor(xc(k), psumT(1, T), -1.0 / (n * P), src(k), ALU.mult, ALU.add)\
                        .then_inc(n_xc, 1)

            def norm(n, T, eps, src=None, xc=None):
                if xc is not None:
                    less_mean(n, T, src, xc)
                cnt_["r0"] += 1
                a, b, r0 = ht(work, 0, T), ht(work, 1, T), ht(work, 3, T)
                rs = RS[:, 0:T]
                v.wait_ge(n_ln, cnt_["r0"])
                chain.done(v.tensor_scalar(b, psumT(0, T), 1.0 / (n * P), eps, ALU.mult, ALU.add))
                v.wait_ge(n_r0, cnt_["r0"])
                chain.done(v.scalar_tensor_tensor(a, r0, -0.5, r0, ALU.mult, ALU.mult))
                chain.wait()
                chain.done(v.tensor_tensor(a, a, b, ALU.mult))
                chain.wait()
                v.scalar_tensor_tensor(rs, a, 1.5, r0, ALU.add, ALU.mult).then_inc(n_rs, 1)
                v.wait_ge(n_rs, cnt_["r0"])

            def split(n, T, make, hi, lo):
                for k in range(n + 1):
                    if k < n:
                        if k >= 2:
                            v.wait_ge(h_ok, cnt_["hi"])
                        make(k, ht(work, k % 2, T)).then_inc(t_ok, 1)
                    if k:
                        cnt_["hi"] += 1
                        v.wait_ge(t_hi, cnt_["hi"])
                        v.tensor_tensor(lo(k - 1), ht(work, (k - 1) % 2, T), hi(k - 1).bitcast(F32), ALU.subtract)\
                            .then_inc(h_ok, 1)

            v.memset(ones[:, :], 1.0).then_inc(set_up, 1)
            v.memset(F_bf[:, :], 0.0).then_inc(set_up, 1)
            v.wait_ge(cst_in, 48)
            for t, src in ((ident_bf, ident[:, :]), (causal_bf, work[:, 0:P]), (chunk_bf, work[:, P:2 * P]),
                           (ident_r, ident[:, :])):
                v.tensor_copy(t[:, :], src).then_inc(set_up, 1)
            v.wait_ge(set_up, 1)
            for h in range(8):
                v.tensor_scalar(sel_bf[:, h * P:(h + 1) * P], ones[:, :], v1("sel", h), None, ALU.mult)\
                    .then_inc(set_up, 1)

            def ada_part(c, g=None, k0=0, k1=KD):
                for k in range(k0, k1):
                    n = c * KD + k
                    off = (lambda x, per: x) if g is None else (lambda x, per: g * per + x)
                    v.wait_ge(ada_in[k % 4], off(16 * (n // 4 + 1), 32))
                    w = ada_w[:, (k % 4) * D:(k % 4 + 1) * D]
                    if k == 0:
                        ins = v.tensor_scalar(ada_acc[:, :], w, cond[:, 0:1], None, ALU.mult)
                    else:
                        v.wait_ge(ada_used, off(n + 4, 8))
                        ins = v.scalar_tensor_tensor(ada_acc[:, :], w, cond[:, k:k + 1], ada_acc[:, :],
                                                     ALU.mult, ALU.add)
                    ins.then_inc(ada_used, 1)

            def ada_out(c, part):
                v.wait_ge(ada_mm, c + 1)
                if isinstance(part, int):
                    m, mp = (t[:, part * 8:part * 8 + 8] for t in (mod, modp))
                    b = vec[:, VEC["b_ada"] + part * 8:VEC["b_ada"] + part * 8 + 8]
                else:
                    m, mp = (t[:, ds(part * 8, 8)] for t in (mod, modp))
                    b = vec[:, ds(part * 8 + VEC["b_ada"], 8)]
                chain.done(v.tensor_tensor(m, PS[:, 3, 512:520], b, ALU.add))
                chain.wait()
                chain.done(v.tensor_scalar(mp, m, 1.0, None, ALU.add))

            v.wait_ge(cond_ok, 1)
            ada_part(0, None, 0, 4)
            v.wait_ge(x_in, 32)
            less_mean(KD, S1, x1, lambda k: ht(XC, k))
            ada_part(0, None, 4, 8)
            norm(KD, S1, LN_EPS)
            ada_out(0, ADA_ORDER[0])
            ada_part(1)
            ada_out(1, ADA_ORDER[1])

            def modulated(src, scale, shift):
                def make(k, out):
                    chain.done(v.tensor_tensor(out, src(k), RS[:, 0:S1], ALU.mult))
                    chain.wait()
                    return v.tensor_scalar(out, out, modp[:, scale * 8 + k:scale * 8 + k + 1],
                                           mod[:, shift * 8 + k:shift * 8 + k + 1], ALU.mult, ALU.add)
                return make

            chain.wait()
            hh, hl = (lambda k: ht(H_hi, k)), (lambda k: ht(H_lo, k))
            split(KD, S1, modulated(lambda k: ht(XC, k), 1, 0), hh, hl)

            wait_tile(v, "forget", 0, 0)
            fa, fb = work[0:8, 2 * S2:2 * S2 + S1], work[0:8, 3 * S2:3 * S2 + S1]
            v.tensor_scalar(fa, PS[0:8, 0, 0:S1], vec[0:8, VEC["b_f"]:VEC["b_f"] + 1], None, ALU.add)\
                .then_inc(free[0], 1)
            wait_out(v, "forget", 0, 0)
            v.scalar_tensor_tensor(fb, fa, -1.0, fa, ALU.mult, ALU.max).then_inc(f_z, 1)
            v.wait_ge(f_ln, 1)
            chain.done(v.scalar_tensor_tensor(fa, fa, 0.0, fb, ALU.min, ALU.subtract))
            step = 1
            while step < S1:
                chain.wait()
                chain.done(v.tensor_copy(fb[:, 0:step], fa[:, 0:step]))
                chain.done(v.tensor_tensor(fb[:, step:], fa[:, step:], fa[:, :S1 - step], ALU.add))
                fa, fb = fb, fa
                step *= 2
            chain.wait()
            chain.done(v.tensor_scalar(fb, fa, -1.0, None, ALU.mult))
            chain.wait()
            chain.done(v.tensor_copy(F_bf[0:8, :], fb))
            chain.wait()
            chain.done(v.tensor_tensor(fa, fb, F_bf[0:8, :], ALU.subtract))
            chain.wait()
            chain.done(v.tensor_copy(F_tmp[0:8, :], fa))
            chain.wait()
            chain.done(v.tensor_copy(F_bf[32:40, :], F_tmp[0:8, :]))
            chain.done(v.tensor_tensor(fb, fa, F_tmp[0:8, :], ALU.subtract))
            chain.wait()
            v.tensor_copy(F_bf[64:72, :], fb).then_inc(f_ok, 1)

            def take_qk(g):
                ada_part(2, g)
                for m in range(4):
                    wait_tile(v, "qk", 0, m, g)
                    v.tensor_scalar(QK[:, ds((g * 4 + m) * S1, S1)], psum1(m), v1("qk_scale", g), None, ALU.mult)\
                        .then_inc(free[m], 1)
                ada_out(g + 2, g + 2)
            loop(4, 2, take_qk)

            def take_v(g):
                for m in range(4):
                    wait_tile(v, "v", 0, m, g)
                    v.tensor_copy(v_raw[:, ds(g * 512 + m * D, 512)], psum1(m)).then_inc(free[m], 1)
            take_v(0)
            for t in (v_hi, v_lo, PT_hi, PT_lo):
                v.memset(t[:, :].bitcast(F32), 0.0).then_inc(zero_ok, 1)
            take_v(1)

            def attention(kind):
                tiles, keys, T, pairs, c0, u0, p0 = ATT[kind]
                nq = len(tiles)
                U = 2 * nq
                mla = kind == "mla"

                def far(p, par):
                    v.wait_ge(rel_in, p * 32 + 16 * (par + 1))
                    x = rel_raw[:, par * 256:(par + 1) * 256]
                    v.tensor_scalar(x, x, v1("rel_far", p * 2 + par), None, ALU.subtract).then_inc(rel_ok, 1)

                def maximum(p, t):
                    q0, qn, ke = tiles[t % nq]
                    v.wait_ge(s_full, p * U + (u0 + t + 1))
                    v.wait_ge(p_ok, p * U + (u0 + t + 1))
                    v.tensor_reduce(small[0:qn, t % 2:t % 2 + 1], PS[0:qn, t % 2, c0:c0 + ke], AX.X,
                                    ALU.max, negate=True).then_inc(nmax_ok, 1)

                def normalize(p, w):
                    _, qn, ke = tiles[w % nq]
                    v.wait_ge(p_ok, p * U + (u0 + w + 3))
                    r = small[0:qn, 4 + w % 2:5 + w % 2]
                    chain.done(v.reciprocal(r, small[0:qn, 2 + w % 2:3 + w % 2]))
                    chain.wait()
                    pb = ht(work, w % 2, S2)[0:qn, 0:ke]
                    v.tensor_scalar(pb, pb, r, None, ALU.mult).then_inc(d_ok, 1)

                def weights(p, w):
                    i = w % nq
                    q0, qn, _ = tiles[i]
                    v.wait_ge(pt_hi, p * U + (u0 + w + 1))
                    nj = min(i + 1, 4)
                    po = 512 * (w % 2)
                    if i == 4:
                        o = slice(q0, q0 + qn)
                        v.tensor_tensor(ht(work_r, 3, S2)[0:META, o], PS[0:META, 2, po + 4 * qn:po + 5 * qn],
                                        ht(work_r, 2, S2)[0:META, o].bitcast(F32), ALU.subtract)
                    a, b = (x[:, :].rearrange("p (j t) -> p j t", t=T)[:, 0:nj, q0:q0 + qn]
                            for x in ((PT2_hi, PT2_lo) if mla else (PT_hi, PT_lo)))
                    v.tensor_tensor(b, PS[:, 2, po:po + nj * qn].rearrange("p (j t) -> p j t", t=qn),
                                    a.bitcast(F32), ALU.subtract).then_inc(pt_lo, 1)

                def take_out(p):
                    v.wait_ge(o_hi, p + (p0 + 1))
                    if mla:
                        v.tensor_tensor(OQ_lo[:, ds(p * (2 * S2), S2)], PS[:, 3, 256:256 + S2],
                                        OK_hi[:, ds(p * S2 + SHIFT, S2)].bitcast(F32), ALU.subtract)\
                            .then_inc(o_lo, 1)
                    else:
                        o = 8 if kind == "chunk" else 0
                        v.tensor_tensor(O_split[:, ds(p * S1 + ((o + 4) * S1 + SHIFT), S1)], PS[:, 3, 256:256 + S1],
                                        O_split[:, ds(p * S1 + (o * S1 + SHIFT), S1)].bitcast(F32), ALU.subtract)\
                            .then_inc(o_lo, 1)

                def step(p, t, first, last):
                    par, i = divmod(t, nq)
                    normalize(p, t)
                    if t + 1 < U:
                        maximum(p, t + 1)
                    elif not last:
                        maximum(p + 1, 0)
                    if t:
                        weights(p, t - 1)
                    elif not first:
                        weights(p - 1, U - 1)
                    if kind == "chunk" and i == 1 and not (last and par):
                        nxt, other = (p, 1) if par == 0 else (p + 1, 0)
                        far(nxt, other)
                    if t == 2 and not first:
                        take_out(p - 1)

                if kind == "chunk":
                    far(0, 0)
                maximum(0, 0)
                over_pairs(v, pairs, U, step, chain, U)
                weights(pairs - 1, U - 1)
                take_out(pairs - 1)

            attention("fox")
            attention("chunk")

            def take_merge(g):
                v.wait_ge(ml_ok, g * 4 + 4)
                for bi in (1, 3):
                    for m in range(4):
                        gm, am = gate[:, m * S1:(m + 1) * S1], acc[:, m * S1:(m + 1) * S1]
                        wait_out(v, "merge", bi - 1, m, g)
                        wait_tile(v, "merge", bi, m, g)
                        v.tensor_tensor(am if bi == 1 else gm, psum1(m), gm, ALU.mult)\
                            .then_inc(out_sem("merge", bi, m), 1)
                        if bi == 3:
                            wait_out(v, "merge", 3, m, g)
                            v.tensor_tensor(am, am, gm, ALU.add).then_inc(a_ok, 1)
                for m in range(4):
                    v.wait_ge(mh_ok, g * 4 + (m + 1))
                    o = (g * 4 + m) * S1
                    v.tensor_tensor(mg_lo[:, ds(o, S1)], acc[:, m * S1:(m + 1) * S1],
                                    mg_hi[:, ds(o, S1)].bitcast(F32), ALU.subtract).then_inc(ml_ok, 1)
            loop(2, 0, take_merge)

            def residual(name, part, x0):
                def body(g):
                    for m in range(4):
                        wait_tile(v, name, 0, m, g)
                        w = ht(work, m, S1)
                        v.tensor_scalar(w, psum1(m), modp[:, g * 4 + (part * 8 + m):g * 4 + (part * 8 + m) + 1], None, ALU.mult)\
                            .then_inc(free[m], 1)
                        wait_out(v, name, 0, m, g)
                        x = x1(g * 4 + m)
                        v.scalar_tensor_tensor(x, x, ALPHA, w, ALU.mult, ALU.add).then_inc(x_ok, 1)
                body(0)
                v.wait_ge(x_ok, x0 + 4)
                s0, s1 = ht(m_out, 0), ht(m_out, 1)
                chain.done(v.tensor_tensor(s0, x1(0), x1(1), ALU.add))
                chain.done(v.tensor_tensor(s1, x1(2), x1(3), ALU.add))
                chain.wait()
                v.tensor_tensor(s0, s0, s1, ALU.add).then_inc(x4_ok, 1)
                body(1)

            def scaled_x():
                for k in range(KD):
                    v.tensor_tensor(x1(k), x1(k), RS[:, 0:S1], ALU.mult).then_inc(xr_ok, 1)

            def ffn(up, T, layer, y0, mid0):
                def body(g):
                    for j in range(2):
                        for tap in range(2):
                            for m in (2 * j, 2 * j + 1):
                                if tap == 0:
                                    v.wait_ge(y_ok, g * 4 + (y0 + m + 1))
                                elif m == 2 * j:
                                    chain.wait()
                                y, u = ht(work, m, T), psumT(m, T)
                                s = 1 + tap
                                w = v1("conv", g * 16 + (layer * 8 * KF + 4 * m + 1 - tap))
                                ins = v.scalar_tensor_tensor(y[:, s:], u[:, :T - s], w, y[:, s:], ALU.mult, ALU.add)
                                chain.done(ins) if tap == 0 else ins.then_inc(free[m], 1)
                    for j in range(2):
                        v.wait_ge(s_ok, g * 2 + (mid0 + j + 1))
                        wait_out(v, up, 0, 2 * j + 1, g)
                        y = ht(work, 2 * j + 1, T)
                        v.tensor_tensor(y, ht(work, 2 * j, T), y, ALU.mult).then_inc(mid_ok, 1)
                    for j in range(2):
                        v.wait_ge(midh_ok, g * 2 + (mid0 + j + 1))
                        o = (g * 2 + j) * S2
                        v.tensor_tensor(mid_lo[:, ds(o, T)], ht(work, 2 * j + 1, T),
                                        mid_hi[:, ds(o, T)].bitcast(F32), ALU.subtract).then_inc(midl_ok, 1)
                loop(11, 4, body)

            residual("out", 2, 0)
            norm(KD, S1, LN_EPS, x1, x1)
            scaled_x()
            norm(KD, S1, LN_EPS, x1, lambda k: ht(XC, k))
            split(KD, S1, modulated(lambda k: ht(XC, k), 4, 3), hh, hl)
            ffn("up_a", S1, 0, 0, 0)
            residual("down_a", 5, 16)
            norm(KD, S1, LN_EPS, x1, x1)
            scaled_x()

            x2 = lambda k: ht(X, k, S2)
            h2, l2 = (lambda k: ht(H_hi, k, S2)), (lambda k: ht(H_lo, k, S2))

            def scaled(src, gain, i0):
                return lambda k, out: v.scalar_tensor_tensor(out, src(k), v1(gain, i0 + k), RS[:, :],
                                                             ALU.mult, ALU.mult)

            def post(gain, i0, x0):
                for k in range(KD):
                    w = ht(work, 2 + k % 2, S2)
                    if k >= 2:
                        v.wait_ge(x_ok, x0 + k - 1)
                    chain.done(v.scalar_tensor_tensor(w, ht(m_out, k, S2), v1(gain, i0 + k), RS[:, :],
                                                      ALU.mult, ALU.mult))
                    chain.wait()
                    v.tensor_tensor(x2(k), x2(k), w, ALU.add).then_inc(x_ok, 1)

            norm(KD, S2, RMS_EPS)
            split(KD, S2, scaled(x2, "mix_pre", 0), h2, l2)
            for t in (PT2_hi, PT2_lo):
                v.memset(t[:, :].bitcast(F32), 0.0).then_inc(zero_ok, 1)
            for bi, m, dst in [(0, i, ht(Q2, i, S2)) for i in range(4)] + [(1, 0, ht(Q2, 4, S2)), (1, 1, kr[:, :])]:
                wait_tile(v, "dqkv", bi, m)
                v.tensor_copy(dst, psum2(m)).then_inc(out_sem("dqkv", bi, m), 1)
            v.wait_ge(tab_in, 32)
            wait_out(v, "dqkv", 1, 1)
            swap = [(i + ROPE // 2) % ROPE for i in range(ROPE)]
            for r in (slice(32, 64), slice(64, 96)):
                w = ht(K2, 0, S2)[r, :]
                chain.done(v.stream_shuffle(w, kr[r, :], swap))
                chain.wait()
                chain.done(v.tensor_tensor(w, w, sin_t[r, :], ALU.mult))
                chain.done(v.tensor_tensor(kr[r, :], kr[r, :], cos_t[r, :], ALU.mult))
                chain.wait()
                v.tensor_tensor(kr[r, :], kr[r, :], w, ALU.add).then_inc(kr_ok, 1)
            for t in (c_hi, c_lo):
                chain.done(v.memset(t[:, 5 * S2:].bitcast(F32), 0.0))
            norm(3, S2, RMS_EPS)
            split(3, S2, scaled(lambda k: ht(Q2, k, S2), "q_norm", 0), lambda k: ht(c_hi, k, S2),
                  lambda k: ht(c_lo, k, S2))
            norm(2, S2, RMS_EPS)
            split(2, S2, scaled(lambda k: ht(Q2, 3 + k, S2), "kv_norm", 0), lambda k: ht(c_hi, 3 + k, S2),
                  lambda k: ht(c_lo, 3 + k, S2))

            def take_uq(g):
                s = (NOPE + ROPE) ** -0.5
                for bi in range(4):
                    for j in range(2):
                        m = BATCH["uq"][bi][2] + j
                        r = slice(64, 96) if j == 0 else slice(32, 64)
                        q = Q2[r, ds((g * 8 + (2 * bi + j)) * S2, S2)]
                        w = ht(work, j, S2)[r, :]
                        chain.wait()
                        v.wait_ge(q_ok, g * 8 + (2 * bi + j + 1))
                        chain.done(v.scalar_tensor_tensor(q, PS[r, m, COL2:COL2 + S2], s, cos_t[r, :], ALU.mult,
                                                          ALU.mult))
                        v.stream_shuffle(w, PS[r, m, COL2:COL2 + S2], swap).then_inc(out_sem("uq", bi, j), 1)
                        wait_out(v, "uq", bi, j, g)
                        chain.done(v.scalar_tensor_tensor(w, w, s, sin_t[r, :], ALU.mult, ALU.mult))
                        chain.wait()
                        chain.done(v.tensor_tensor(q, q, w, ALU.add))
            v.wait_ge(h_ok, cnt_["hi"])
            loop(2, 24, take_uq)
            chain.wait()
            for bi in range(2):
                for t in range(5):
                    wait_tile(v, "uv", bi, t)
                    o = t * D + bi * 512
                    v.tensor_copy(v_raw2[:, o:o + 512], PS[:, t % 4, 0:512]).then_inc(out_sem("uv", bi, t), 1)
            for t in (k2_hi, k2_lo, v2_hi, v2_lo):
                v.memset(t[:, :].bitcast(F32), 0.0).then_inc(zero_ok, 1)
            attention("mla")
            norm(KD, S2, RMS_EPS)
            post("mix_post", 0, 32)
            norm(KD, S2, RMS_EPS)
            split(KD, S2, scaled(x2, "ffn_pre", 0), h2, l2)
            ffn("up_b", S2, 1, 44, KF)
            norm(KD, S2, RMS_EPS)
            post("ffn_post", 0, 40)
            norm(KD, S2, RMS_EPS)

            def pooled(k, out):
                w = POOLS[k // 2]
                a = ht(pool_a, k % 2, S2)
                chain.done(v.scalar_tensor_tensor(a, x2(k), v1("mix_pre", KD + k), RS[:, :], ALU.mult, ALU.mult))
                s, step = a, 1
                bufs = [ht(pool_s, 0, S2), ht(pool_s, 1, S2)]
                while step < w:
                    chain.wait()
                    n = bufs.pop(0)
                    chain.done(v.tensor_copy(n[:, 0:step], s[:, 0:step]))
                    chain.done(v.tensor_tensor(n[:, step:], s[:, step:], s[:, :S2 - step], ALU.add))
                    if s is not a:
                        bufs.append(s)
                    s = n
                    step *= 2
                chain.wait()
                i = VEC["cnt"] + 16 * (k // 2)
                small_ = pool_c[:, 0:16]
                chain.done(v.tensor_tensor(small_, s[:, 0:16], vec[:, i:i + 16], ALU.mult))
                chain.done(v.scalar_tensor_tensor(out[:, 16:], s[:, 16:], 1.0 / w, a[:, 16:], ALU.mult,
                                                  ALU.subtract))
                chain.wait()
                return v.tensor_tensor(out[:, 0:16], small_, a[:, 0:16], ALU.subtract)

            split(KD, S2, pooled, h2, l2)
            norm(KD, S2, RMS_EPS)
            post("mix_post", KD, 48)
            norm(KD, S2, RMS_EPS)
            split(KD, S2, scaled(x2, "ffn_pre", KD), h2, l2)
            ffn("up_c", S2, 2, 88, 2 * KF)
            norm(KD, S2, RMS_EPS)
            post("ffn_post", KD, 56)


def rows(a):
    return a.reshape(-1, P, a.shape[-1])


def columns(a):
    return a.reshape(-1, P).T


def weight_stream(np, w):
    out = np.zeros((NSTREAM, P, BLK), np.float32)
    at = [0]

    def put(block):
        flat = block.transpose(1, 0, 2).reshape(P, -1)
        out[at[0], :, :flat.shape[1]] = flat
        at[0] += 1

    def cut(m, c0, width, kk=2):
        m = rows(m[:, c0:c0 + width])
        for k in range(0, m.shape[0], kk):
            put(m[k:k + kk])

    w_in = w["w_in"][0]
    put(rows(w_in[:, 1536:1536 + P]))
    for c in (0, 512, 1544, 2056, 1024, 2568):
        cut(w_in, c, 512)
    for g in range(2):
        cut(w_in, 3080 + 512 * g, 512)
        cut(w["w_br_fox"][0], 512 * g, 512)
        cut(w_in, 4104 + 512 * g, 512)
        cut(w["w_br_chunk"][0], 512 * g, 512)
    for g in range(2):
        cut(w["w_out"][0], 512 * g, 512)

    def ffn(up, down):
        a, b = (up[:, i * FF:(i + 1) * FF].reshape(D, KF, P) for i in range(2))
        both = np.stack([a, b], 2).reshape(D, 2 * FF)
        for g in range(11):
            cut(both, 512 * g, 512)
        for g in range(2):
            m, k = rows(down[:, 512 * g:512 * (g + 1)]), 0
            for n in DOWN_ROWS:
                put(m[k:k + n])
                k += n

    ffn(w["w_up"][0], w["w_down"][0])
    m = w["mla_w_dqkv_2"][0]
    cut(m, 0, 512)
    z = np.zeros((D, ROPE), np.float32)
    rope = m[:, RQ + RKV:]
    cut(np.concatenate([m[:, 512:640], z, rope, rope, z], 1), 0, 256, 4)
    m = w["mla_w_uq_2"][0].reshape(RQ, H2, NOPE + ROPE)
    z = np.zeros((RQ, ROPE), np.float32)
    for h in range(0, H2, 2):
        cut(np.concatenate([m[:, h], z, z, m[:, h + 1, NOPE:], m[:, h + 1, :NOPE]], 1), 0, 256, 3)
    m = w["mla_w_ukv_2"][0].reshape(RKV, H2, 2, NOPE)
    for part in range(2):
        for g in range(2):
            cut(m[:, 8 * g:8 * g + 8, part].reshape(RKV, 512), 0, 512)
    for g in range(2):
        cut(w["mla_w_o_2"][0], 512 * g, 512)
    ffn(w["ffn_w_up_2"][0], w["ffn_w_down_2"][0])
    m = w["pool_w_group_2"][0]
    for g in range(0, 4, 2):
        put(rows(m[g:g + 2].reshape(512, 256)))
    ffn(w["ffn_w_up_2"][1], w["ffn_w_down_2"][1])
    assert at[0] == NBLK, (at[0], NBLK)
    return out


def vector_table(np, w):
    t = np.zeros((P, NVEC), np.float32)

    def put(name, cols):
        t[:, VEC[name]:VEC[name] + cols.shape[1]] = cols

    put("c", columns(w["c"]))
    for name in ("b_ada", "ln1_g", "ln1_b", "ln2_g", "ln2_b"):
        put(name, columns(w[name]))
    t[0:8, VEC["b_f"]] = w["b_f"][0]
    put("qk_scale", np.broadcast_to(np.array([[0.125, 1.0, 0.125, 1.0]], np.float32), (P, 4)))
    put("rel_far", np.broadcast_to(w["rel_bias"][0][:, 256][None], (P, 8)))
    r = np.arange(P)[:, None]
    put("sel", ((r < 96) & (r % 32 == np.arange(8)[None])).astype(np.float32))
    for name, src in (("mix_pre", "norm_mix_pre_2"), ("mix_post", "norm_mix_post_2"),
                      ("ffn_pre", "norm_ffn_pre_2"), ("ffn_post", "norm_ffn_post_2"),
                      ("q_norm", "mla_q_norm_2"), ("kv_norm", "mla_kv_norm_2"), ("pool_scale", "pool_scale_2")):
        put(name, columns(w[src]))
    put("eps", np.broadcast_to(np.array([[LN_EPS, RMS_EPS]], np.float32), (P, 2)))
    put("cnt", np.broadcast_to(np.concatenate(
        [1.0 / np.minimum(np.arange(16) + 1, n) for n in POOLS]).astype(np.float32)[None], (P, 64)))
    layers = [(w["conv_w"][0], w["conv_b"][0])]
    layers += [(w["ffn_conv_w_2"][i], w["ffn_conv_b_2"][i]) for i in range(2)]
    conv = []
    for taps, bias in layers:
        a = np.concatenate([taps, bias[None]], 0).reshape(4, 2, KF, P)
        conv.append(a.transpose(3, 2, 1, 0).reshape(P, -1))
    put("conv", np.concatenate(conv, 1))
    return t


def kernel(**inputs):
    import numpy as np
    import concourse.bacc as bacc
    from concourse.bass_utils import run_bass_kernel_spmd

    w = {k: np.asarray(v) for k, v in inputs.items()}
    q, s = np.arange(P)[:, None], np.arange(P)[None]
    neg = np.float32(-3e38)
    consts = np.concatenate([np.eye(P), np.where(s <= q, 0, neg), np.where((q < 64) & (s >= 64), neg, 0)], 1)
    far = np.clip(P + q - np.arange(2 * P)[None], -P, P) + P
    pos = np.arange(S2, dtype=np.float32)[None] / (10000.0 ** (np.arange(0, ROPE, 2, dtype=np.float32) / ROPE))[:, None]
    turn = np.zeros((2, P, S2), np.float32)
    for r in (32, 64):
        turn[0, r:r + ROPE] = np.concatenate([np.cos(pos), np.cos(pos)])
        turn[1, r:r + ROPE] = np.concatenate([-np.sin(pos), np.sin(pos)])
    arrays = {
        "xT": np.ascontiguousarray(w["x"][0].T).reshape(KD, P, S1),
        "meta": np.ascontiguousarray(w["meta_tokens_2"].T).reshape(KD, P, META),
        "stream": weight_stream(np, w),
        "ada": np.concatenate([rows(w["w_ada"][0][:, part * D:(part + 1) * D]) for part in ADA_ORDER]),
        "vecs": vector_table(np, w),
        "consts": consts.astype(np.float32),
        "rel": np.ascontiguousarray(w["rel_bias"][0][:, far]),
        "rope": turn,
    }
    nc = bacc.Bacc("TRN2", target_bir_lowering=False, num_devices=1)
    args = {n: nc.dram_tensor(n, a.shape, mybir.dt.from_np(a.dtype), kind="ExternalInput").ap()
            for n, a in arrays.items()}
    yT = nc.dram_tensor("yT", (KD, P, S1), F32, kind="ExternalOutput").ap()
    program(nc, yT=yT, **args)
    got = run_bass_kernel_spmd(nc, [arrays], core_ids=[0]).results[0]["yT"]
    return np.ascontiguousarray(got.reshape(D, S1).T)[None]
```

```python
from contextlib import ExitStack

import concourse.bass as bass
from concourse import mybir

P = 128
D = 1024
KD = D // P
S1 = 512
META = 16
S2 = S1 + META
H1 = 8
H2 = 16
FF = 2816
KF = FF // P
QB = 128
RQ, RKV = 384, 256
NOPE, ROPE = 64, 32
POOLS = (2, 4, 8, 16)
ALPHA = 2.0 ** 0.25
LN_EPS, RMS_EPS = 1e-5, 1e-6

BLK = 1024
C_PAD = P - META
SHIFT = 16
RING = 4

F32 = mybir.dt.float32
F32R = mybir.dt.float32r
BF16 = mybir.dt.bfloat16
ALU = mybir.AluOpType
ACT = mybir.ActivationFunctionType
AX = mybir.AxisListType
ds = bass.ds

STAGES = [
    ("forget", 1, 1), ("qk", 4, 4), ("v", 4, 2), ("merge", 12, 2), ("out", 4, 2),
    ("up_a", 4, 11), ("down_a", 12, 2),
    ("dqkv", 6, 1), ("uq", 4, 2), ("uk", 2, 1), ("uv", 2, 1), ("wo", 4, 2),
    ("up_b", 4, 11), ("down_b", 12, 2), ("pool", 2, 1), ("up_c", 4, 11), ("down_c", 12, 2),
]
DOWN_ROWS = (2,) * (KF - 12) + (1,) * (24 - KF)
BLK0, _n = {}, 0
for _name, _b, _t in STAGES:
    BLK0[_name] = _n
    _n += _b * _t
NBLK = _n
NSTREAM = NBLK + RING

BATCH = {
    "forget": [(1, 0, 0)], "qk": [(4, 3, 0)], "v": [(4, 3, 0)],
    "merge": [(4, 3, 0), (4, 5, 0), (4, 9, 0), (4, 11, 0)],
    "out": [(4, 3, 0)], "up_a": [(4, 3, 0)], "down_a": [(4, 11, 0)], "dqkv": [(4, 3, 0), (2, 5, 0)],
    "uq": [(2, 0, 0), (2, 1, 2), (2, 2, 0), (2, 3, 2)], "uk": [(4, 0, 0), (4, 1, 0)],
    "uv": [(5, 0, 0), (5, 1, 0)], "wo": [(4, 3, 0)],
    "up_b": [(4, 3, 0)], "down_b": [(4, 11, 0)], "pool": [(4, 0, 0), (4, 1, 0)], "up_c": [(4, 3, 0)],
    "down_c": [(4, 11, 0)],
}
NB = {name: b for name, b, _ in STAGES}
FULL0, FREE0, _f, _u = {}, {}, 0, [0, 0, 0, 0]


def tiles_in(name, k, before=None):
    return sum(1 for n, _, p in BATCH[name][:before] for j in range(n) if (p + j) % 4 == k)


for _name, _b, _t in STAGES:
    FULL0[_name], FREE0[_name] = _f, list(_u)
    _f += sum(n - 1 for n, _, _ in BATCH[_name]) * _t
    for _k in range(4):
        _u[_k] += tiles_in(_name, _k) * _t
FREE_END = list(_u)


def free_before(name, batch, i, g=0):
    k = (BATCH[name][batch][2] + i) % 4
    return g * tiles_in(name, k) + (FREE0[name][k] + tiles_in(name, k, batch) + i // 4)


TILES1 = [(i * QB, QB, (i + 1) * QB) for i in range(S1 // QB)]
TILES2 = TILES1[:3] + [(384, 72, 512), (456, 72, S2)]
KEYS1 = [(i * QB, QB) for i in range(S1 // QB)]
KEYS2 = KEYS1 + [(S1, META)]
ATT = {
    "fox": (TILES1, KEYS1, S1, H1 // 2, 0, 0, 0),
    "chunk": (TILES1, KEYS1, S1, H1 // 2, 0, 32, 4),
    "mla": (TILES2, KEYS2, S2, H2 // 2, 256, 64, 8),
}
STG = {"fox": ("q", "k", "v"), "chunk": ("q", "k", "rel", "v"), "mla": ("q", "k", "v")}
STG0 = {"fox": 0, "chunk": 3 * H1, "mla": 7 * H1}
LEAD = 3
COL2 = 248
HALF2 = S2 // 2
PADDED = 16 + S2

VEC, _v = {}, 0
for _name, _w in [("c", 8), ("b_ada", 48), ("ln1_g", 8), ("ln1_b", 8), ("ln2_g", 8), ("ln2_b", 8),
                  ("b_f", 1), ("qk_scale", 4), ("rel_far", 8), ("sel", 8),
                  ("mix_pre", 16), ("mix_post", 16), ("ffn_pre", 16), ("ffn_post", 16),
                  ("q_norm", 3), ("kv_norm", 2), ("pool_scale", 8), ("eps", 2),
                  ("cnt", 64), ("conv", 3 * 4 * 2 * KF)]:
    VEC[_name] = _v
    _v += _w
NVEC = _v
SET_UP = 14
ADA_ORDER = (1, 0, 2, 3, 4, 5)


def program(nc, xT, meta, stream, ada, vecs, consts, rel, rope, yT):
    with ExitStack() as ctx:
        def sb(name, cols, dt=F32):
            return ctx.enter_context(nc.sbuf_tensor(name, [P, cols], dt))

        def region(*tensors):
            with ExitStack() as over:
                return [over.enter_context(nc.sbuf_tensor(n, [P, c], dt)) for n, c, dt in tensors]

        def sem(name):
            return ctx.enter_context(nc.semaphore(name))

        X = sb("X", KD * S2)
        w_raw = sb("w_raw", RING * BLK)
        w_hi = sb("w_hi", RING * BLK, F32R)
        w_lo = sb("w_lo", RING * BLK, F32R)
        (work_r,) = region(("work_r", 4 * S2, F32R))
        work = sb("work", 4 * S2)
        RS = sb("RS", S2)
        vec = sb("vec", NVEC)
        mod = sb("mod", 48)
        modp = sb("modp", 48)
        ident = sb("ident", P)
        ones = sb("ones", P)
        ident_bf = sb("ident_bf", P, BF16)
        causal_bf = sb("causal_bf", P, BF16)
        chunk_bf = sb("chunk_bf", P, BF16)
        ident_r = sb("ident_r", P, F32R)
        cond = sb("cond", 8)
        small = sb("small", 8)
        (m_out,) = region(("m_out", KD * S2, F32))
        v_raw2, kr = region(("v_raw2", 5 * D, F32), ("kr", S2, F32))
        H_hi = sb("H_hi", KD * S2, F32R)
        H_lo = sb("H_lo", KD * S2, F32R)
        (_, QK, XC, ada_w, ada_acc) = region(
            ("shift", SHIFT, F32), ("QK", 16 * S1, F32), ("XC", KD * S2, F32), ("ada_w", 4 * D, F32),
            ("ada_acc", D, F32))
        (_, _, v_raw, q_hi, q_lo, k_hi, k_lo, v_hi, v_lo, PT_hi, PT_lo, rel_raw, rel_hi, rel_lo,
         sel_bf, F_bf, F_tmp) = region(
            ("shift_", SHIFT, F32), ("over_QK", 16 * S1, F32), ("v_raw", 4 * D, F32), ("q_hi", S1, F32R),
            ("q_lo", S1, F32R),
            ("k_hi", S1, F32R), ("k_lo", S1, F32R), ("v_hi", 2 * 4 * P, F32R), ("v_lo", 2 * 4 * P, F32R),
            ("PT_hi", 4 * S1, F32R), ("PT_lo", 4 * S1, F32R),
            ("rel_raw", 2 * 256, F32), ("rel_hi", 2 * 256, F32R), ("rel_lo", 2 * 256, F32R),
            ("sel_bf", 8 * P, BF16), ("F_bf", S1, BF16), ("F_tmp", S1, BF16))
        (O_split, mg_hi, mg_lo, gate, acc) = region(
            ("O_split", SHIFT + 16 * S1, F32R), ("mg_hi", KD * S1, F32R), ("mg_lo", KD * S1, F32R),
            ("gate", 4 * S1, F32), ("acc", 4 * S1, F32))
        mid_hi, mid_lo = region(("mid_hi", KF * S2, F32R), ("mid_lo", KF * S2, F32R))
        (Q2, K2, c_hi, c_lo, cos_t, sin_t) = region(
            ("Q2", H2 * S2, F32), ("K2", KD * S2, F32), ("c_hi", 5 * S2 + C_PAD, F32R),
            ("c_lo", 5 * S2 + C_PAD, F32R), ("cos_t", S2, F32), ("sin_t", S2, F32))
        (_, _, q2_hi, q2_lo, k2_hi, k2_lo, v2_hi, v2_lo, PT2_hi, PT2_lo) = region(
            ("over_Q2", H2 * S2, F32), ("over_K2", KD * S2, F32), ("q2_hi", 2 * S2, F32R), ("q2_lo", 2 * S2, F32R),
            ("k2_hi", 2 * S2, F32R), ("k2_lo", 2 * S2, F32R), ("v2_hi", 2 * 5 * P, F32R),
            ("v2_lo", 2 * 5 * P, F32R), ("PT2_hi", 4 * S2, F32R), ("PT2_lo", 4 * S2, F32R))
        (OQ_lo, OK_hi) = region(("OQ_lo", H2 * S2 - SHIFT, F32R), ("OK_hi", SHIFT + KD * S2, F32R))
        (pool_a, pool_s, pool_c) = region(
            ("pool_a", 2 * PADDED, F32), ("pool_s", 2 * PADDED, F32), ("pool_c", 2 * 16, F32))
        PS = ctx.enter_context(nc.psum_tensor("PS", [P, 4, 2 * 512], F32))

        w_in = [sem(f"w_in{i}") for i in range(RING)]
        w_hi_ok, w_lo_ok = sem("w_hi_ok"), sem("w_lo_ok")
        w_used = sem("w_used")
        full = sem("full")
        free = [sem(f"free{i}") for i in range(4)]
        x_in, cst_in, set_up, tab_in = sem("x_in"), sem("cst_in"), sem("set_up"), sem("tab_in")
        dve, act = sem("dve_step"), sem("act_step")
        ada_in = [sem(f"ada_in{i}") for i in range(4)]
        ada_used, ada_mm, cond_ok = sem("ada_used"), sem("ada_mm"), sem("cond_ok")
        n_mean, n_xc, n_sq, n_sq_used, n_ln, n_r0, n_rs = (
            sem(s) for s in ("n_mean", "n_xc", "n_sq", "n_sq_used", "n_ln", "n_r0", "n_rs"))
        sq4_ok, sum4_ok = sem("sq4_ok"), sem("sum4_ok")
        x4_ok = sem("x4_ok")
        xr_ok = sem("xr_ok")
        x_ok = sem("x_ok")
        t_ok, t_hi, h_ok = sem("t_ok"), sem("t_hi"), sem("h_ok")
        f_z, f_ln, f_ok = sem("f_z"), sem("f_ln"), sem("f_ok")
        zero_ok = sem("zero_ok")
        q_ok = sem("q_ok")
        rw_ok, rq_ok = sem("rw_ok"), sem("rq_ok")
        kr_ok, rope_hi, rope_lo = sem("kr_ok"), sem("rope_hi"), sem("rope_lo")
        stg_hi, stg_lo, rel_in, rel_ok = sem("stg_hi"), sem("stg_lo"), sem("rel_in"), sem("rel_ok")
        s_full, nmax_ok = sem("s_full"), sem("nmax_ok")
        p_ok, pn_ok = sem("p_ok"), sem("pn_ok")
        pt_full, pt_hi, pt_lo = sem("pt_full"), sem("pt_hi"), sem("pt_lo")
        pv_done = sem("pv_done")
        o_hi, o_lo = sem("o_hi"), sem("o_lo")
        a_ok, mh_ok, ml_ok = sem("a_ok"), sem("mh_ok"), sem("ml_ok")
        y_ok, s_ok, mid_ok, midh_ok, midl_ok = (sem(s) for s in ("y_ok", "s_ok", "mid_ok", "midh_ok", "midl_ok"))
        out_done = sem("out_done")

        def x1(k):
            return X[:, k * S2 + META:(k + 1) * S2]

        def ht(t, k, n=S1):
            return t[:, k * S2:k * S2 + n]

        def v1(name, i):
            c = VEC[name]
            if isinstance(i, int):
                return vec[:, c + i:c + i + 1]
            return vec[:, ds(i + c, 1)]

        def wtile(t, slot, kk, m, cols=4):
            o = slot * BLK + (kk * cols + m) * P
            return t[:, o:o + P]

        def psum1(k):
            return PS[:, k, 0:S1]

        def psum2(k):
            return PS[:, k, COL2:COL2 + S2]

        def psumT(k, T):
            return psum1(k) if T == S1 else psum2(k)

        def wait_tile(eng, name, bi, i, g=0):
            n, end, _ = BATCH[name][bi]
            if i == n - 1:
                eng.wait_ge(w_used, g * NB[name] + (BLK0[name] + end + 1 + RING))
            else:
                per = sum(x[0] - 1 for x in BATCH[name])
                own = sum(x[0] - 1 for x in BATCH[name][:bi])
                eng.wait_ge(full, g * per + (FULL0[name] + own + i + 1))

        def wait_out(eng, name, bi, i, g=0):
            eng.wait_ge(free[(BATCH[name][bi][2] + i) % 4], free_before(name, bi, i, g) + 2)

        def out_sem(name, bi, i):
            return free[(BATCH[name][bi][2] + i) % 4]

        class Chain:

            def __init__(self, eng, s):
                self.eng, self.s, self.base, self.k, self.g, self.per = eng, s, 0, 0, None, 0

            def done(self, ins):
                ins.then_inc(self.s, 1)
                self.k += 1

            def wait(self):
                n = self.base + self.k
                self.eng.wait_ge(self.s, n if self.g is None else self.g * self.per + n)

            def turn(self, g, per):
                self.base, self.k, self.g, self.per = self.base + self.k, 0, g, per

            def end(self, turns):
                assert self.k == self.per, (self.k, self.per)
                self.base, self.k, self.g = self.base + turns * self.per, 0, None

        def over_pairs(eng, pairs, U, step, chain=None, per=0):
            for t in range(LEAD):
                step(0, t, True, False)
            with eng.Fori(0, pairs - 1) as p:
                if chain is not None:
                    chain.turn(p, per)
                for t in range(LEAD, U + LEAD):
                    if t < U:
                        step(p, t, False, False)
                    else:
                        step(p + 1, t - U, False, False)
            if chain is not None:
                chain.end(pairs - 1)
            for t in range(LEAD, U):
                step(pairs - 1, t, False, True)

        def qk_rows(mla, name, par):
            if mla and name == "q":
                return slice(0, P)
            return slice(64 * par, 64 * par + 64)

        def head_raw(kind, name, p, par):
            mla = kind == "mla"
            o = 8 if kind == "chunk" else 0
            r = qk_rows(mla, name, par)
            if name == "q":
                return Q2[:, ds(p * (2 * S2) + par * S2, S2)] if mla else QK[r, ds(p * S1 + o * S1, S1)]
            if name == "k":
                return K2[r, ds(p * S2, S2)] if mla else QK[r, ds(p * S1 + (o + 4) * S1, S1)]
            if name == "rel":
                return rel_raw[:, par * 256:(par + 1) * 256]
            if mla:
                return v_raw2[:, :].rearrange("p (t c) -> p t c", t=5)[:, :, ds(p * P + par * 64, 64)]
            return v_raw[:, :].rearrange("p (t c) -> p t c", t=4)[:, :, ds(p * P + (o * 64 + par * 64), 64)]

        def head_part(kind, name, par, hi):
            mla = kind == "mla"
            r = qk_rows(mla, name, par)
            if name in ("q", "k"):
                t = {("q", 1): (q_hi, q2_hi), ("q", 0): (q_lo, q2_lo), ("k", 1): (k_hi, k2_hi),
                     ("k", 0): (k_lo, k2_lo)}[name, hi][mla]
                return t[r, par * S2:(par + 1) * S2] if mla else t[r, :]
            if name == "rel":
                return (rel_hi if hi else rel_lo)[:, par * 256:(par + 1) * 256]
            t, n = ((v2_hi, v2_lo) if mla else (v_hi, v_lo))[1 - hi], 5 if mla else 4
            t = t[:, par * n * P:(par + 1) * n * P].rearrange("p (t c) -> p t c", t=n)
            return t[:, :, par * 64:par * 64 + 64]

        block = ctx.enter_context(nc.Block())

        @block.sync
        def _(sp):
            sp.dma_start(vec[:, :], vecs).then_inc(cst_in, 16)
            sp.dma_start(ident[:, :], consts[:, 0:P]).then_inc(cst_in, 16)
            sp.dma_start(work[:, 0:2 * P], consts[:, P:]).then_inc(cst_in, 16)
            sp.dma_start(X[:, :].rearrange("p (k t) -> p k t", k=KD)[:, :, META:S2],
                         xT.rearrange("k p t -> p k t")).then_inc(x_in, 16)
            sp.dma_start(X[:, :].rearrange("p (k t) -> p k t", k=KD)[:, :, 0:META],
                         meta.rearrange("k p t -> p k t")).then_inc(x_in, 16)

            def load_w(n, slot):
                sp.wait_ge(w_lo_ok, n + 1)
                sp.dma_start(w_raw[:, slot * BLK:(slot + 1) * BLK],
                             stream[ds(n, 1)].rearrange("a p c -> p (a c)")).then_inc(w_in[slot], 16)

            def load_ada(n, slot):
                sp.wait_ge(ada_used, n + 1)
                sp.dma_start(ada_w[:, slot * D:(slot + 1) * D],
                             ada[ds(n, 1)].rearrange("a p c -> p (a c)")).then_inc(ada_in[slot], 16)

            for n in range(4):
                load_ada(n, n)
            for n in range(4):
                load_w(n, n)
            for n in range(4, 12):
                load_ada(n, n % 4)
            for n in range(4, 8):
                load_w(n, n % 4)
            for n in range(12, 20):
                load_ada(n, n % 4)
            with sp.Fori(0, 3) as g:
                for j in range(4):
                    for i in (2 * j, 2 * j + 1):
                        load_ada(g * 8 + (20 + i), i % 4)
                    load_w(g * 4 + (8 + j), j)
            for j in range(4):
                load_ada(44 + j, j)
                load_w(20 + j, j)
            with sp.Fori(0, (NSTREAM - 24) // 4) as g:
                for j in range(4):
                    load_w(g * 4 + (24 + j), j)
            for n in range(NSTREAM - NSTREAM % 4, NSTREAM):
                load_w(n, n % 4)

            for k in range(KD):
                sp.wait_ge(x_ok, 7 * KD + k + 1)
                sp.dma_start(yT[k], x1(k)).then_inc(out_done, 16)
            sp.wait_ge(out_done, 16 * KD)

        @block.tensor
        def _(pe):
            cnt_ = {"sq": 0, "norm": 0}
            pe.sem_inc(w_used, RING)
            pe.sem_inc(pt_full, 2)
            pe.sem_inc(pv_done, 2)

            def spans(T):
                return [(0, S1, 0)] if T == S1 else [(0, HALF2, COL2), (HALF2, S2, COL2)]

            def mm3(out, w_h, w_l, x_h, x_l, cuts, start, stop):
                last = None
                for i, (w, x) in enumerate(((w_l, x_h), (w_h, x_l), (w_h, x_h))):
                    for a, b, c0 in cuts:
                        last = pe.matmul(out[:, c0 + a:c0 + b], w, x[:, a:b], start=start and i == 0,
                                         stop=stop and i == 2)
                return last

            def begin(name, batch, i, g):
                pe.wait_ge(free[(BATCH[name][batch][2] + i) % 4], free_before(name, batch, i, g) + 1)

            def batch(name, bi, g, n, blocks, tiles, kks, cols, x, T, h_ready=None, w_tile=None):
                done = 0
                for bi_, b in enumerate(blocks):
                    slot = (BLK0[name] + b) % RING
                    kk = kks[bi_] if isinstance(kks, tuple) else kks
                    pe.wait_ge(w_lo_ok, n + (b + 1 + RING))
                    for m in range(tiles):
                        if bi_ == 0:
                            begin(name, bi, m, g)
                        for k in range(kk):
                            kt = done + k
                            if m == 0 and h_ready is not None:
                                pe.wait_ge(h_ok, h_ready + kt + 1)
                            xh, xl = x(kt)
                            last = mm3(PS[:, m, :], wtile(w_hi, slot, k, m, cols), wtile(w_lo, slot, k, m, cols),
                                       xh, xl, spans(T), bi_ == 0 and k == 0,
                                       bi_ == len(blocks) - 1 and k == kk - 1)
                        if bi_ == len(blocks) - 1 and m < tiles - 1:
                            last.then_inc(full, 1)
                    last.then_inc(w_used, 1)
                    done += kk

            def norm(n, T, ready, mean, src, four=0):
                if mean:
                    first = 3 if four else 0
                    for k in range(first, n):
                        if four and k == first:
                            pe.wait_ge(x4_ok, four)
                        elif ready is not None:
                            pe.wait_ge(ready[0], ready[1] + k + 1)
                        x = ht(m_out, 0) if four and k == first else src(k)
                        for a, b, c0 in spans(T):
                            last = pe.matmul(PS[:, 1, c0 + a:c0 + b], ones[:, :], x[:, a:b],
                                             start=k == first, stop=k == n - 1)
                    last.then_inc(n_mean, 1)
                if cnt_["norm"]:
                    pe.wait_ge(n_rs, cnt_["norm"])
                cnt_["norm"] += 1
                for k in range(n):
                    cnt_["sq"] += 1
                    pe.wait_ge(n_sq, cnt_["sq"])
                    for a, b, c0 in spans(T):
                        square = ht(work, k % (4 if mean else 2), T)
                        last = pe.matmul(PS[:, 0, c0 + a:c0 + b], ones[:, :], square[:, a:b],
                                         start=k == 0, stop=k == n - 1)
                    last.then_inc(n_sq_used, 1)

            def hx(T):
                return lambda k: (ht(H_hi, k, T), ht(H_lo, k, T))

            def attention(kind):
                tiles, keys, T, pairs, c0, u0, p0 = ATT[kind]
                nq = len(tiles)
                U = 2 * nq
                mla = kind == "mla"
                qh, ql, kh, kl = (q2_hi, q2_lo, k2_hi, k2_lo) if mla else (q_hi, q_lo, k_hi, k_lo)
                vh, vl = (v2_hi, v2_lo) if mla else (v_hi, v_lo)
                ns, s0 = len(STG[kind]), STG0[kind]

                def scores(p, t):
                    par, i = divmod(t, nq)
                    q0, qn, ke = tiles[i]
                    if i == 0:
                        pe.wait_ge(stg_lo, p * (2 * ns) + (s0 + par * ns + ns - 1))
                    pe.wait_ge(p_ok, p * U + (u0 + t + 1))
                    if mla:
                        rows = slice(0, P)
                        o = par * S2
                        cuts = [(0, 256)] + ([(256, max(ke, 512))] if ke > 256 else [])
                    else:
                        rows = slice(64 * par, 64 * par + 64)
                        o = 0
                        cuts = [(0, max(ke, 256))]
                    out = PS[:, t % 2, :]
                    for a, b in cuts:
                        for j, (l, r) in enumerate(((ql, kh), (qh, kl), (qh, kh))):
                            pe.matmul(out[0:qn, c0 + a:c0 + b], l[rows, o + q0:o + q0 + qn],
                                      r[rows, o + a:o + b], start=j == 0, stop=False, skip_group_check=True)
                    if kind == "fox":
                        b = cuts[0][1]
                        pe.matmul(out[:, 0:b], sel_bf[:, ds(p * (2 * P) + par * P, P)], F_bf[:, 0:b],
                                  start=False, stop=False, skip_group_check=True)
                    if kind == "chunk":
                        lo = 0 if q0 else P
                        for r in (rel_lo, rel_hi):
                            pe.matmul(out[:, q0 - P + lo:q0 + P], ident_r[:, :],
                                      r[:, par * 256 + lo:par * 256 + 256], start=False, stop=False,
                                      skip_group_check=True)
                    mask = chunk_bf if kind == "chunk" else causal_bf
                    pe.matmul(out[0:qn, c0 + q0:c0 + ke], ident_bf[:, 0:qn], mask[:, 0:ke - q0],
                              start=False, stop=True, skip_group_check=True).then_inc(s_full, 1)

                def turn_over(p, w):
                    i = w % nq
                    qn = tiles[i][1]
                    pe.wait_ge(pn_ok, p * U + (u0 + w + 1))
                    pe.wait_ge(pt_lo, p * U + (u0 + w + 1))
                    pb = ht(work, w % 2, S2)
                    for j in range(i + 1):
                        k0, kn = keys[j]
                        o = 512 * (w % 2) + j * qn
                        last = pe.transpose(PS[0:kn, 2, o:o + qn], pb[0:qn, k0:k0 + kn], ident[0:qn, 0:qn])
                    last.then_inc(pt_full, 1)

                def outputs(p, par, late):
                    pe.wait_ge(pt_lo, p * U + (u0 + par * nq + (nq if late else 2) + 2))
                    pe.wait_ge(stg_lo, p * (2 * ns) + (s0 + (par + 1) * ns))
                    if par == 0 and not late:
                        pe.wait_ge(o_lo, p + (p0 + 1))
                    n = nq if late else 2
                    for j in range(n):
                        kn = keys[j][1]
                        a, b = (256 if late else 0), (T if late else 256)
                        if mla and late:
                            a = (256, 256, 256, 272, 456)[j]
                        if mla and j == nq - 1:
                            sh, sl, so = work_r[:, 2 * S2:3 * S2], work_r[:, 3 * S2:4 * S2], 0
                        else:
                            sh, sl, so = (PT2_hi, PT2_lo, j * S2) if mla else (PT_hi, PT_lo, j * S1)
                        vo = (par * nq + j) * P
                        for n_, (l, r) in enumerate(((vl, sh), (vh, sl), (vh, sh))):
                            last = pe.matmul(
                                PS[:, 3, 256 + a:256 + b], l[0:kn, vo:vo + P], r[0:kn, so + a:so + b],
                                start=par == 0 and j == 0 and n_ == 0,
                                stop=par == 1 and j == n - 1 and n_ == 2, skip_group_check=True)
                    last.then_inc(pv_done, 1)

                def run(before=None, after=None):
                    def step(p, t, first, last):
                        if t + 1 < U:
                            scores(p, t + 1)
                        elif not last:
                            scores(p + 1, 0)
                        elif after is not None:
                            after["scores"](0, 0)
                        if t % nq == 3:
                            outputs(p, t // nq, False)
                        if t == nq + 1:
                            outputs(p, 0, True)
                        elif t == 1 and not first:
                            outputs(p - 1, 1, True)
                        elif t == 1 and before is not None:
                            before["finish"]()
                        turn_over(p, t)

                    if before is None:
                        scores(0, 0)
                    over_pairs(pe, pairs, U, step)
                    if after is None:
                        finish()

                def finish():
                    outputs(pairs - 1, 1, True)

                return {"run": run, "scores": scores, "finish": finish}

            pe.wait_ge(set_up, SET_UP)
            pe.wait_ge(x_in, 32)
            norm(KD, S1, None, True, x1)
            def ada_turn(c):
                pe.wait_ge(ada_used, c * KD + (KD + 4))
                for m in range(KD):
                    last = pe.matmul(PS[:, 3, 512 + m:513 + m], ada_acc[:, m * P:(m + 1) * P], ones[:, 0:1],
                                     start=True, stop=True, skip_group_check=True)
                last.then_inc(ada_mm, 1)

            ada_turn(0)
            ada_turn(1)
            batch("forget", 0, 0, BLK0["forget"], [0], 1, 8, 1, hx(S1), S1, 0)
            with pe.Fori(0, 4) as g:
                batch("qk", 0, g, g * 4 + BLK0["qk"], range(4), 4, 2, 4, hx(S1), S1, 0)
                ada_turn(g + 2)
            with pe.Fori(0, 2) as g:
                for b in range(4):
                    slot = (BLK0["v"] + b) % RING
                    pe.wait_ge(w_lo_ok, g * 4 + (BLK0["v"] + b + 1 + RING))
                    for t in range(4):
                        if b == 0:
                            begin("v", 0, t, g)
                        for k in range(2):
                            kt = b * 2 + k
                            wr = slice(slot * BLK + k * 512, slot * BLK + k * 512 + 512)
                            hs = slice(kt * S2 + t * P, kt * S2 + t * P + P)
                            for j, (l, r) in enumerate(((H_lo, w_hi), (H_hi, w_lo), (H_hi, w_hi))):
                                last = pe.matmul(PS[:, t, 0:512], l[:, hs], r[:, wr],
                                                 start=kt == 0 and j == 0, stop=kt == 7 and j == 2)
                        if b == 3 and t < 3:
                            last.then_inc(full, 1)
                    last.then_inc(w_used, 1)
            for k in range(4):
                pe.wait_ge(free[k], FREE0["merge"][k] + 1)
            pe.wait_ge(f_ok, 1)
            fox, chunk = attention("fox"), attention("chunk")
            fox["run"](after=chunk)
            chunk["run"](before=fox)
            pe.wait_ge(o_lo, 8 + 1)

            def ox(kind):
                o = SHIFT + (0 if kind == "fox" else 8) * S1
                return lambda k: (O_split[:, o + k * S1:o + (k + 1) * S1],
                                  O_split[:, o + (4 + k) * S1:o + (5 + k) * S1])

            with pe.Fori(0, 2) as g:
                n = g * 12 + BLK0["merge"]
                batch("merge", 0, g, n, range(0, 4), 4, 2, 4, hx(S1), S1)
                batch("merge", 1, g, n, range(4, 6), 4, 2, 4, ox("fox"), S1)
                batch("merge", 2, g, n, range(6, 10), 4, 2, 4, hx(S1), S1)
                batch("merge", 3, g, n, range(10, 12), 4, 2, 4, ox("chunk"), S1)
            pe.wait_ge(ml_ok, 12)
            with pe.Fori(0, 2) as g:
                batch("out", 0, g, g * 4 + BLK0["out"], range(4), 4, 2, 4,
                      lambda k: (mg_hi[:, k * S1:(k + 1) * S1], mg_lo[:, k * S1:(k + 1) * S1]), S1)

            def ffn(up, down, T, h0, mid0):
                with pe.Fori(0, 11) as g:
                    batch(up, 0, g, g * 4 + BLK0[up], range(4), 4, 2, 4, hx(T), T, h0)
                pe.wait_ge(midl_ok, mid0 + KF + 1)
                with pe.Fori(0, 2) as g:
                    batch(down, 0, g, g * 12 + BLK0[down], range(12), 4, DOWN_ROWS, 4,
                          lambda k: (ht(mid_hi, k, T), ht(mid_lo, k, T)), T)

            def norm_after(nxt, n, T, ready, mean, src, four=0):
                for k in (0, 1):
                    pe.wait_ge(free[k], FREE0[nxt][k] + 1)
                norm(n, T, ready, mean, src, four)

            def norm_four(nxt, n4):
                pe.wait_ge(free[0], (FREE0[nxt] if nxt else FREE_END)[0] + 1)
                pe.wait_ge(n_rs, cnt_["norm"])
                cnt_["norm"] += 1
                for m in range(-1, 4):
                    if m < 0:
                        pe.wait_ge(sum4_ok, n4)
                    else:
                        cnt_["sq"] += 1
                        pe.wait_ge(n_sq, cnt_["sq"])
                    src = RS[:, :] if m < 0 else ht(work, m, S2)
                    for a, b, c0 in spans(S2):
                        last = pe.matmul(PS[:, 0, c0 + a:c0 + b], ones[:, :], src[:, a:b], start=m < 0, stop=m == 3)
                    if m >= 0:
                        last.then_inc(n_sq_used, 1)

            norm_after("up_a", KD, S1, (x_ok, 0), True, x1, 1)
            norm_after("up_a", KD, S1, (x_ok, 8), True, x1)
            ffn("up_a", "down_a", S1, 8, 0)
            norm_after("dqkv", KD, S1, (x_ok, 16), True, x1, 2)

            norm(KD, S2, None, False, None)
            batch("dqkv", 0, 0, BLK0["dqkv"], range(4), 4, 2, 4, hx(S2), S2, 16)
            batch("dqkv", 1, 0, BLK0["dqkv"], range(4, 6), 2, 4, 2, hx(S2), S2)
            norm_after("uq", 3, S2, None, False, None)
            norm(2, S2, None, False, None)
            pe.wait_ge(n_rs, cnt_["norm"])
            cx = lambda o: (lambda k: (ht(c_hi, o + k, S2), ht(c_lo, o + k, S2)))
            with pe.Fori(0, 2) as g:
                for b in range(4):
                    slot = (BLK0["uq"] + b) % RING
                    pe.wait_ge(w_lo_ok, g * 4 + (BLK0["uq"] + b + 1 + RING))
                    for j in range(2):
                        m = (2 * b + j) % 4
                        begin("uq", b, j, g)
                        for k in range(3):
                            pe.wait_ge(h_ok, 24 + k + 1)
                            xh, xl = cx(0)(k)
                            last = mm3(PS[:, m, :], wtile(w_hi, slot, k, j, 2), wtile(w_lo, slot, k, j, 2),
                                       xh, xl, spans(S2), k == 0, k == 2)
                        last.then_inc(full if j == 0 else w_used, 1)
            pe.wait_ge(h_ok, 29)
            for b in range(2):
                slot = (BLK0["uk"] + b) % RING
                pe.wait_ge(w_lo_ok, BLK0["uk"] + b + 1 + RING)
                for m in range(4):
                    begin("uk", b, m, 0)
                    for k in range(2):
                        xh, xl = cx(3)(k)
                        last = mm3(PS[:, m, :], wtile(w_hi, slot, k, m), wtile(w_lo, slot, k, m),
                                   xh, xl, spans(S2), k == 0, k == 1)
                    if m < 3:
                        last.then_inc(full, 1)
                last.then_inc(w_used, 1)
            for b in range(2):
                slot = (BLK0["uv"] + b) % RING
                pe.wait_ge(w_lo_ok, BLK0["uv"] + b + 1 + RING)
                for t in range(5):
                    begin("uv", b, t, 0)
                    t0 = KEYS2[t][0]
                    for k in range(2):
                        wr = slice(slot * BLK + k * 512, slot * BLK + k * 512 + 512)
                        cs = slice((3 + k) * S2 + t0, (3 + k) * S2 + t0 + P)
                        for j, (l, r) in enumerate(((c_lo, w_hi), (c_hi, w_lo), (c_hi, w_hi))):
                            last = pe.matmul(PS[:, t % 4, 0:512], l[:, cs], r[:, wr],
                                             start=k == 0 and j == 0, stop=k == 1 and j == 2)
                    if t < 4:
                        last.then_inc(full, 1)
                last.then_inc(w_used, 1)
            for k in range(4):
                pe.wait_ge(free[k], FREE0["wo"][k] + 1)
            attention("mla")["run"]()
            pe.wait_ge(o_lo, 16 + 1)
            with pe.Fori(0, 2) as g:
                batch("wo", 0, g, g * 4 + BLK0["wo"], range(4), 4, 2, 4,
                      lambda k: (OK_hi[:, SHIFT + k * S2:SHIFT + (k + 1) * S2], ht(OQ_lo, 2 * k, S2)), S2)
            norm_four("up_b", 1)
            norm(KD, S2, None, False, None)
            ffn("up_b", "down_b", S2, 29, KF)
            norm_four("pool", 2)
            norm(KD, S2, None, False, None)
            for b in range(2):
                slot = (BLK0["pool"] + b) % RING
                pe.wait_ge(w_lo_ok, BLK0["pool"] + b + 1 + RING)
                for m in range(4):
                    begin("pool", b, m, 0)
                    grp = m // 2
                    for k in range(2):
                        kt = (2 * b + grp) * 2 + k
                        pe.wait_ge(h_ok, 37 + kt + 1)
                        xh, xl = hx(S2)(kt)
                        last = mm3(PS[:, m, :], wtile(w_hi, slot, grp * 2 + k, m % 2, 2),
                                   wtile(w_lo, slot, grp * 2 + k, m % 2, 2), xh, xl, spans(S2), k == 0, k == 1)
                    if m < 3:
                        last.then_inc(full, 1)
                last.then_inc(w_used, 1)
            norm_four("up_c", 3)
            norm(KD, S2, None, False, None)
            ffn("up_c", "down_c", S2, 45, 2 * KF)
            norm_four(None, 4)

        @block.gpsimd
        def _(gp):
            gp.sem_inc(w_lo_ok, RING)
            gp.sem_inc(rq_ok, 2)

            def lower(n, slot):
                gp.wait_ge(w_hi_ok, n + 1)
                o = slice(slot * BLK, (slot + 1) * BLK)
                gp.tensor_tensor(w_lo[:, o], w_raw[:, o], w_hi[:, o].bitcast(F32), ALU.subtract)\
                  .then_inc(w_lo_ok, 1)

            def lower_blocks(a, b):
                while a % RING and a < b:
                    lower(a, a % RING)
                    a += 1
                turns = (b - a) // RING
                if turns:
                    with gp.Fori(0, turns) as g:
                        for j in range(RING):
                            lower(g * RING + (a + j), j)
                for n in range(a + turns * RING, b):
                    lower(n, n % RING)

            def split_heads(kind):
                ns, s0 = len(STG[kind]), STG0[kind]
                with gp.Fori(0, ATT[kind][3]) as p:
                    for par in range(2):
                        for j, name in enumerate(STG[kind]):
                            n = s0 + par * ns + j
                            gp.wait_ge(stg_hi, p * (2 * ns) + (n + 1))
                            if par or j:
                                gp.wait_ge(stg_lo, p * (2 * ns) + n)
                            gp.tensor_tensor(head_part(kind, name, par, 0), head_raw(kind, name, p, par),
                                             head_part(kind, name, par, 1).bitcast(F32), ALU.subtract)\
                              .then_inc(stg_lo, 1)

            lower_blocks(0, BLK0["merge"] + RING)
            split_heads("fox")
            split_heads("chunk")
            lower_blocks(BLK0["merge"] + RING, BLK0["uq"] + RING)
            with gp.Fori(0, 2) as g:
                for bi in range(4):
                    n = BLK0["uq"] + RING + bi
                    gp.wait_ge(rq_ok, g * 8 + (2 * bi + 2))
                    lower(g * 4 + n, n % RING)
                    gp.wait_ge(w_lo_ok, g * 4 + (n + 1 + RING))
                    for j in range(2):
                        r = slice(64, 96) if j == 0 else slice(32, 64)
                        gp.wait_ge(rw_ok, g * 8 + (2 * bi + j + 1))
                        q = Q2[r, ds((g * 8 + (2 * bi + j)) * S2, S2)]
                        gp.tensor_tensor(q, q, ht(work, j, S2)[r, :], ALU.add).then_inc(rq_ok, 1)
            gp.wait_ge(rq_ok, H2 + 2)
            lower_blocks(BLK0["uk"] + RING, BLK0["wo"] + RING)
            gp.wait_ge(w_lo_ok, BLK0["wo"] + 2 * RING)
            for par, r in ((0, slice(64, 96)), (1, slice(32, 64))):
                gp.wait_ge(rope_hi, par + 1)
                gp.tensor_tensor(k2_lo[r, par * S2:(par + 1) * S2], kr[r, :],
                                 k2_hi[r, par * S2:(par + 1) * S2].bitcast(F32), ALU.subtract)\
                  .then_inc(rope_lo, 1)
            gp.wait_ge(rope_lo, 2)
            split_heads("mla")
            lower_blocks(BLK0["wo"] + RING, NBLK)

        @block.scalar
        def _(act_):
            cnt_ = {"sq": 0, "xc": 0, "ln": 0, "t": 0, "four": 0}
            chain = Chain(act_, act)
            act_.sem_inc(p_ok, 2)

            def log_and_exp():
                act_.preload_act_table_set("natural_log_exp_and_others")

            def copy(out, in_, scale=1.0):
                return act_.activation(out, in_, ACT.Copy, scale=scale)

            def upper(name, b, g=0):
                n = BLK0[name] + b
                slot = n % RING
                per = NB[name]
                act_.wait_ge(w_in[slot], g * (16 * per // RING) + 16 * (n // RING + 1))
                act_.wait_ge(w_used, g * per + (n + 1))
                o = slice(slot * BLK, (slot + 1) * BLK)
                copy(w_hi[:, o], w_raw[:, o]).then_inc(w_hi_ok, 1)

            def stage(name, g=0, take=None):
                b = RING
                for bi, (_, end, _) in enumerate(BATCH[name]):
                    while b < end + RING:
                        upper(name, b, g)
                        b += 1
                    if take is not None:
                        take(bi)
                while b < NB[name] + RING:
                    upper(name, b, g)
                    b += 1

            def loop(name, turns, take=None, per=0):
                with act_.Fori(0, turns) as g:
                    chain.turn(g, per)
                    stage(name, g, None if take is None else lambda bi: take(g, bi))
                chain.end(turns)

            def norm(n, T, eps, src, ready, mean=False):
                if cnt_["t"]:
                    act_.wait_ge(h_ok, cnt_["t"])
                bufs = 4 if mean else 2
                for k in range(n):
                    if mean:
                        cnt_["xc"] += 1
                        act_.wait_ge(n_xc, cnt_["xc"])
                    else:
                        ready(k)
                    if k >= bufs:
                        act_.wait_ge(n_sq_used, cnt_["sq"] + 1 - bufs)
                    act_.activation(ht(work, k % bufs, T), src(k), ACT.Square).then_inc(n_sq, 1)
                    cnt_["sq"] += 1
                deviation(n, T, eps)

            def deviation(n, T, eps):
                act_.wait_ge(n_sq_used, cnt_["sq"])
                cnt_["ln"] += 1
                act_.activation(ht(work, 2, T), psumT(0, T), ACT.Ln, bias=v1("eps", eps),
                                scale=1.0 / (n * P)).then_inc(n_ln, 1)
                act_.wait_ge(n_ln, cnt_["ln"])
                act_.activation(ht(work, 3, T), ht(work, 2, T), ACT.Exp, scale=-0.5).then_inc(n_r0, 1)

            def affine(gain, bias, n0):
                for k in range(KD):
                    act_.wait_ge(xr_ok, n0 + k + 1)
                    act_.activation(x1(k), x1(k), ACT.Identity, bias=v1(bias, k), scale=v1(gain, k)).then_inc(x_ok, 1)

            def take_squared(name, scale=None):
                cnt_["four"] += 1

                def take(g, bi):
                    half = bi if name == "pool" else g
                    for m in range(4):
                        wait_tile(act_, name, bi, m | 1 if name == "pool" else m, g)
                        tile = ht(m_out, 4 * half + m, S2)
                        copy(tile, psum2(m), 1.0 if scale is None else v1(scale, 4 * half + m))\
                            .then_inc(out_sem(name, bi, m), 1)
                        wait_out(act_, name, bi, m, g)
                        if not half and m == 0:
                            act_.wait_ge(h_ok, cnt_["t"])
                        if half and m == 0:
                            act_.wait_ge(sum4_ok, cnt_["four"])
                        act_.activation(ht(work, m, S2), tile, ACT.Square).then_inc(n_sq if half else sq4_ok, 1)
                cnt_["sq"] += 4
                for g in range(1 if name == "pool" else 2):
                    stage(name, g, lambda bi: take(g, bi))

            def split(n, T, hi, scale=None, shift=None):
                for k in range(n):
                    cnt_["t"] += 1
                    act_.wait_ge(t_ok, cnt_["t"])
                    if scale is not None:
                        w = ht(work, k % 2, T)
                        chain.done(act_.activation(w, w, ACT.Identity, bias=mod[:, shift * 8 + k:shift * 8 + k + 1],
                                                   scale=modp[:, scale * 8 + k:scale * 8 + k + 1]))
                        chain.wait()
                    copy(hi(k), ht(work, k % 2, T)).then_inc(t_hi, 1)

            def attention(kind):
                tiles, keys, T, pairs, c0, u0, p0 = ATT[kind]
                nq = len(tiles)
                U = 2 * nq
                mla = kind == "mla"
                ns, s0 = len(STG[kind]), STG0[kind]

                def load_rel(p, par):
                    act_.dma_start(rel_raw[:, par * 256:(par + 1) * 256],
                                   rel[ds(p * 2 + par, 1)].rearrange("h p c -> p (h c)")).then_inc(rel_in, 16)

                def stage_head(p, par, j):
                    name = STG[kind][j]
                    if name == "rel":
                        act_.wait_ge(rel_ok, p * 2 + (par + 1))
                    if name == "v" and not (isinstance(p, int) and p0 + p + par == 0):
                        act_.wait_ge(pv_done, p * 4 + (4 * p0 + 2 * par))
                    copy(head_part(kind, name, par, 1), head_raw(kind, name, p, par)).then_inc(stg_hi, 1)

                def exps(p, t):
                    q0, qn, ke = tiles[t % nq]
                    act_.wait_ge(nmax_ok, p * U + (u0 + t + 1))
                    act_.wait_ge(pt_full, p * U + (u0 + t + 1))
                    act_.activation(ht(work, t % 2, S2)[0:qn, 0:ke], PS[0:qn, t % 2, c0:c0 + ke],
                                    ACT.Exp, bias=small[0:qn, t % 2:t % 2 + 1],
                                    accum_out=small[0:qn, 2 + t % 2:3 + t % 2]).then_inc(p_ok, 1)

                def weights(p, w):
                    par, i = divmod(w, nq)
                    q0, qn, _ = tiles[i]
                    act_.wait_ge(pt_full, p * U + (u0 + w + 3))
                    if i in (0, 2):
                        act_.wait_ge(pv_done, p * 4 + (4 * p0 + 2 * par + 1 + i // 2))
                    nj = min(i + 1, 4)
                    po = 512 * (w % 2)
                    if i == 4:
                        copy(work_r[0:META, 2 * S2 + q0:2 * S2 + q0 + qn], PS[0:META, 2, po + 4 * qn:po + 5 * qn])
                    dst = PT2_hi if mla else PT_hi
                    copy(dst[:, :].rearrange("p (j t) -> p j t", t=T)[:, 0:nj, q0:q0 + qn],
                         PS[:, 2, po:po + nj * qn].rearrange("p (j t) -> p j t", t=qn)).then_inc(pt_hi, 1)

                def take_out(p):
                    act_.wait_ge(pv_done, p * 4 + (4 * p0 + 6))
                    if mla:
                        copy(OK_hi[:, ds(p * S2 + SHIFT, S2)], PS[:, 3, 256:256 + S2]).then_inc(o_hi, 1)
                    else:
                        o = 8 if kind == "chunk" else 0
                        copy(O_split[:, ds(p * S1 + (o * S1 + SHIFT), S1)], PS[:, 3, 256:256 + S1]).then_inc(o_hi, 1)

                def stage(p, par, i):
                    if i < ns:
                        if kind == "chunk" and i == 0:
                            load_rel(p, par)
                        stage_head(p, par, i)

                def run(before=None, after=None):
                    def step(p, t, first, last):
                        par, i = divmod(t, nq)
                        exps(p, t)
                        if t:
                            weights(p, t - 1)
                        elif not first:
                            weights(p - 1, U - 1)
                        elif before is not None:
                            before["last_weights"]()
                        if par == 0:
                            stage(p, 1, i)
                        elif not last:
                            stage(p + 1, 0, i)
                        elif after is not None:
                            after["stage"](0, 0, i)
                        if t == 2 and not first:
                            take_out(p - 1)
                        elif t == 2 and before is not None:
                            before["last_out"]()

                    if before is None:
                        act_.wait_ge(pv_done, 4 * p0 + 2)
                        for i in range(ns):
                            stage(0, 0, i)
                    over_pairs(act_, pairs, U, step)
                    if after is None:
                        last_weights()
                        last_out()

                def last_weights():
                    weights(pairs - 1, U - 1)

                def last_out():
                    take_out(pairs - 1)

                return {"run": run, "stage": stage, "last_weights": last_weights, "last_out": last_out}

            def ffn(up, down, T, layer, mid0):
                def take(g, _):
                    act_.wait_ge(midl_ok, g * 2 + (mid0 + 1))
                    for m in range(4):
                        wait_tile(act_, up, 0, m, g)
                        c = layer * 8 * KF + 4 * m
                        act_.activation(ht(work, m, T), psumT(m, T), ACT.Identity,
                                        bias=v1("conv", g * 16 + (c + 3)), scale=v1("conv", g * 16 + (c + 2)))\
                            .then_inc(y_ok, 1)
                    for j in range(2):
                        wait_out(act_, up, 0, 2 * j, g)
                        act_.activation(ht(work, 2 * j, T), ht(work, 2 * j, T), ACT.Silu).then_inc(s_ok, 1)
                    for j in range(2):
                        act_.wait_ge(mid_ok, g * 2 + (mid0 + j + 1))
                        copy(mid_hi[:, ds((g * 2 + j) * S2, T)], ht(work, 2 * j + 1, T)).then_inc(midh_ok, 1)
                loop(up, 11, take)
                log_and_exp()
                if T == S1:
                    loop(down, 2)
                else:
                    take_squared(down)

            act_.wait_ge(cst_in, 48)
            act_.activation(cond[:, :], vec[:, VEC["c"]:VEC["c"] + KD], ACT.Silu).then_inc(cond_ok, 1)
            log_and_exp()
            for b in range(RING):
                upper("forget", b)
            norm(KD, S1, 0, lambda k: ht(XC, k), None, True)
            split(KD, S1, lambda k: ht(H_hi, k), 1, 0)

            def take_forget(_):
                act_.wait_ge(f_z, 1)
                chain.done(act_.activation(work[0:8, 3 * S2:3 * S2 + S1], work[0:8, 3 * S2:3 * S2 + S1],
                                           ACT.Exp, scale=-1.0))
                chain.wait()
                act_.activation(work[0:8, 3 * S2:3 * S2 + S1], work[0:8, 3 * S2:3 * S2 + S1],
                                ACT.Ln, bias=1.0).then_inc(f_ln, 1)
            stage("forget", 0, take_forget)
            loop("qk", 4)
            loop("v", 2)
            act_.wait_ge(zero_ok, 4)
            for k in range(4):
                act_.wait_ge(free[k], FREE0["merge"][k] + 1)
            fox, chunk = attention("fox"), attention("chunk")
            fox["run"](after=chunk)
            chunk["run"](before=fox)

            def take_merge(g, bi):
                for m in range(4):
                    if bi in (0, 2):
                        if bi == 2:
                            wait_out(act_, "merge", 1, m, g)
                        else:
                            act_.wait_ge(a_ok, g * 4 + (m + 1))
                        wait_tile(act_, "merge", bi, m, g)
                        act_.activation(gate[:, m * S1:(m + 1) * S1], psum1(m), ACT.Sigmoid)\
                            .then_inc(out_sem("merge", bi, m), 1)
                    if bi == 3:
                        act_.wait_ge(a_ok, g * 4 + (4 + m + 1))
                        copy(mg_hi[:, ds((g * 4 + m) * S1, S1)], acc[:, m * S1:(m + 1) * S1]).then_inc(mh_ok, 1)
            loop("merge", 2, take_merge)
            log_and_exp()
            loop("out", 2)
            norm(KD, S1, 0, x1, None, True)
            affine("ln1_g", "ln1_b", 0)
            norm(KD, S1, 0, lambda k: ht(XC, k), None, True)
            split(KD, S1, lambda k: ht(H_hi, k), 4, 3)
            ffn("up_a", "down_a", S1, 0, 0)
            norm(KD, S1, 0, x1, None, True)
            affine("ln2_g", "ln2_b", KD)

            act_.wait_ge(w_used, BLK0["dqkv"] + RING)
            act_.dma_start(cos_t[:, :], rope[0]).then_inc(tab_in, 16)
            act_.dma_start(sin_t[:, :], rope[1]).then_inc(tab_in, 16)
            act_.wait_ge(x_in, 32)
            x2 = lambda k: ht(X, k, S2)
            x_new = lambda base: (lambda k: act_.wait_ge(x_ok, base + k + 1))
            norm(KD, S2, 1, x2, x_new(24))
            split(KD, S2, lambda k: ht(H_hi, k, S2))
            stage("dqkv")
            norm(3, S2, 1, lambda k: ht(Q2, k, S2), lambda k: wait_out(act_, "dqkv", 0, k))
            split(3, S2, lambda k: ht(c_hi, k, S2))
            norm(2, S2, 1, lambda k: ht(Q2, 3 + k, S2),
                 lambda k: wait_out(act_, "dqkv", k, 3 if k == 0 else 0))
            split(2, S2, lambda k: ht(c_hi, 3 + k, S2))

            def take_uq(g, bi):
                for j in range(2):
                    m = BATCH["uq"][bi][2] + j
                    wait_tile(act_, "uq", bi, j, g)
                    act_.activation(Q2[:, ds((g * 8 + (2 * bi + j)) * S2, S2)], psum2(m), ACT.Copy,
                                    scale=(NOPE + ROPE) ** -0.5).then_inc(q_ok, 1)
            loop("uq", 2, take_uq)

            def take_uk(bi):
                for m in range(4):
                    wait_tile(act_, "uk", bi, m)
                    copy(ht(K2, 4 * bi + m, S2), psum2(m)).then_inc(out_sem("uk", bi, m), 1)
            stage("uk", 0, take_uk)
            stage("uv")
            for k in range(4):
                act_.wait_ge(free[k], FREE0["wo"][k] + 1)
            act_.wait_ge(rq_ok, H2 + 2)
            act_.wait_ge(zero_ok, 8)
            act_.wait_ge(kr_ok, 2)
            for par, r in ((0, slice(64, 96)), (1, slice(32, 64))):
                copy(k2_hi[r, par * S2:(par + 1) * S2], kr[r, :]).then_inc(rope_hi, 1)
            act_.wait_ge(zero_ok, 10)
            attention("mla")["run"]()

            take_squared("wo")
            deviation(KD, S2, 1)
            norm(KD, S2, 1, x2, x_new(32))
            split(KD, S2, lambda k: ht(H_hi, k, S2))
            ffn("up_b", "down_b", S2, 1, KF)
            deviation(KD, S2, 1)
            norm(KD, S2, 1, x2, x_new(40))
            split(KD, S2, lambda k: ht(H_hi, k, S2))

            take_squared("pool", "pool_scale")
            deviation(KD, S2, 1)
            norm(KD, S2, 1, x2, x_new(48))
            split(KD, S2, lambda k: ht(H_hi, k, S2))
            ffn("up_c", "down_c", S2, 2, 2 * KF)
            deviation(KD, S2, 1)

        @block.vector
        def _(v):
            cnt_ = {"r0": 0, "mean": 0, "hi": 0}
            chain = Chain(v, dve)
            for k in range(4):
                v.sem_inc(free[k], 1)
            v.sem_inc(ada_used, 4)
            v.sem_inc(pt_lo, 2)
            v.sem_inc(o_lo, 1)
            v.sem_inc(midl_ok, 1)
            v.sem_inc(a_ok, 4)
            v.sem_inc(ml_ok, 4)

            def loop(turns, per, body):
                with v.Fori(0, turns) as g:
                    chain.turn(g, per)
                    body(g)
                chain.end(turns)

            def less_mean(n, T, src, xc):
                cnt_["mean"] += 1
                v.wait_ge(n_mean, cnt_["mean"])
                for k in range(n):
                    v.scalar_tensor_tensor(xc(k), psumT(1, T), -1.0 / (n * P), src(k), ALU.mult, ALU.add)\
                        .then_inc(n_xc, 1)

            def norm(n, T, eps, src=None, xc=None):
                if xc is not None:
                    less_mean(n, T, src, xc)
                cnt_["r0"] += 1
                a, b, r0 = ht(work, 0, T), ht(work, 1, T), ht(work, 3, T)
                rs = RS[:, 0:T]
                v.wait_ge(n_ln, cnt_["r0"])
                chain.done(v.tensor_scalar(b, psumT(0, T), 1.0 / (n * P), eps, ALU.mult, ALU.add))
                v.wait_ge(n_r0, cnt_["r0"])
                chain.done(v.scalar_tensor_tensor(a, r0, -0.5, r0, ALU.mult, ALU.mult))
                chain.wait()
                chain.done(v.tensor_tensor(a, a, b, ALU.mult))
                chain.wait()
                v.scalar_tensor_tensor(rs, a, 1.5, r0, ALU.add, ALU.mult).then_inc(n_rs, 1)
                v.wait_ge(n_rs, cnt_["r0"])

            def split(n, T, make, hi, lo):
                for k in range(n + 1):
                    if k < n:
                        if k >= 2:
                            v.wait_ge(h_ok, cnt_["hi"])
                        make(k, ht(work, k % 2, T)).then_inc(t_ok, 1)
                    if k:
                        cnt_["hi"] += 1
                        v.wait_ge(t_hi, cnt_["hi"])
                        v.tensor_tensor(lo(k - 1), ht(work, (k - 1) % 2, T), hi(k - 1).bitcast(F32), ALU.subtract)\
                            .then_inc(h_ok, 1)

            v.memset(ones[:, :], 1.0).then_inc(set_up, 1)
            v.memset(F_bf[:, :], 0.0).then_inc(set_up, 1)
            v.wait_ge(cst_in, 48)
            for t, src in ((ident_bf, ident[:, :]), (causal_bf, work[:, 0:P]), (chunk_bf, work[:, P:2 * P]),
                           (ident_r, ident[:, :])):
                v.tensor_copy(t[:, :], src).then_inc(set_up, 1)
            v.wait_ge(set_up, 1)
            for h in range(8):
                v.tensor_scalar(sel_bf[:, h * P:(h + 1) * P], ones[:, :], v1("sel", h), None, ALU.mult)\
                    .then_inc(set_up, 1)

            def ada_part(c, g=None, k0=0, k1=KD):
                for k in range(k0, k1):
                    n = c * KD + k
                    off = (lambda x, per: x) if g is None else (lambda x, per: g * per + x)
                    v.wait_ge(ada_in[k % 4], off(16 * (n // 4 + 1), 32))
                    w = ada_w[:, (k % 4) * D:(k % 4 + 1) * D]
                    if k == 0:
                        ins = v.tensor_scalar(ada_acc[:, :], w, cond[:, 0:1], None, ALU.mult)
                    else:
                        v.wait_ge(ada_used, off(n + 4, 8))
                        ins = v.scalar_tensor_tensor(ada_acc[:, :], w, cond[:, k:k + 1], ada_acc[:, :],
                                                     ALU.mult, ALU.add)
                    ins.then_inc(ada_used, 1)

            def ada_out(c, part):
                v.wait_ge(ada_mm, c + 1)
                if isinstance(part, int):
                    m, mp = (t[:, part * 8:part * 8 + 8] for t in (mod, modp))
                    b = vec[:, VEC["b_ada"] + part * 8:VEC["b_ada"] + part * 8 + 8]
                else:
                    m, mp = (t[:, ds(part * 8, 8)] for t in (mod, modp))
                    b = vec[:, ds(part * 8 + VEC["b_ada"], 8)]
                chain.done(v.tensor_tensor(m, PS[:, 3, 512:520], b, ALU.add))
                chain.wait()
                chain.done(v.tensor_scalar(mp, m, 1.0, None, ALU.add))

            v.wait_ge(cond_ok, 1)
            ada_part(0, None, 0, 4)
            v.wait_ge(x_in, 32)
            less_mean(KD, S1, x1, lambda k: ht(XC, k))
            ada_part(0, None, 4, 8)
            norm(KD, S1, LN_EPS)
            ada_out(0, ADA_ORDER[0])
            ada_part(1)
            ada_out(1, ADA_ORDER[1])

            def over_deviation(src):
                return lambda k, out: v.tensor_tensor(out, src(k), RS[:, 0:S1], ALU.mult)

            chain.wait()
            hh, hl = (lambda k: ht(H_hi, k)), (lambda k: ht(H_lo, k))
            split(KD, S1, over_deviation(lambda k: ht(XC, k)), hh, hl)

            wait_tile(v, "forget", 0, 0)
            fa, fb = work[0:8, 2 * S2:2 * S2 + S1], work[0:8, 3 * S2:3 * S2 + S1]
            v.tensor_scalar(fa, PS[0:8, 0, 0:S1], vec[0:8, VEC["b_f"]:VEC["b_f"] + 1], None, ALU.add)\
                .then_inc(free[0], 1)
            wait_out(v, "forget", 0, 0)
            v.scalar_tensor_tensor(fb, fa, -1.0, fa, ALU.mult, ALU.max).then_inc(f_z, 1)
            v.wait_ge(f_ln, 1)
            chain.done(v.scalar_tensor_tensor(fa, fa, 0.0, fb, ALU.min, ALU.subtract))
            step = 1
            while step < S1:
                chain.wait()
                chain.done(v.tensor_copy(fb[:, 0:step], fa[:, 0:step]))
                chain.done(v.tensor_tensor(fb[:, step:], fa[:, step:], fa[:, :S1 - step], ALU.add))
                fa, fb = fb, fa
                step *= 2
            chain.wait()
            chain.done(v.tensor_scalar(fb, fa, -1.0, None, ALU.mult))
            chain.wait()
            chain.done(v.tensor_copy(F_bf[0:8, :], fb))
            chain.wait()
            chain.done(v.tensor_tensor(fa, fb, F_bf[0:8, :], ALU.subtract))
            chain.wait()
            chain.done(v.tensor_copy(F_tmp[0:8, :], fa))
            chain.wait()
            chain.done(v.tensor_copy(F_bf[32:40, :], F_tmp[0:8, :]))
            chain.done(v.tensor_tensor(fb, fa, F_tmp[0:8, :], ALU.subtract))
            chain.wait()
            v.tensor_copy(F_bf[64:72, :], fb).then_inc(f_ok, 1)

            def take_qk(g):
                ada_part(2, g)
                for m in range(4):
                    wait_tile(v, "qk", 0, m, g)
                    v.tensor_scalar(QK[:, ds((g * 4 + m) * S1, S1)], psum1(m), v1("qk_scale", g), None, ALU.mult)\
                        .then_inc(free[m], 1)
                ada_out(g + 2, g + 2)
            loop(4, 2, take_qk)

            def take_v(g):
                for m in range(4):
                    wait_tile(v, "v", 0, m, g)
                    v.tensor_copy(v_raw[:, ds(g * 512 + m * D, 512)], psum1(m)).then_inc(free[m], 1)
            take_v(0)
            for t in (v_hi, v_lo, PT_hi, PT_lo):
                v.memset(t[:, :].bitcast(F32), 0.0).then_inc(zero_ok, 1)
            take_v(1)

            def attention(kind):
                tiles, keys, T, pairs, c0, u0, p0 = ATT[kind]
                nq = len(tiles)
                U = 2 * nq
                mla = kind == "mla"

                def far(p, par):
                    v.wait_ge(rel_in, p * 32 + 16 * (par + 1))
                    x = rel_raw[:, par * 256:(par + 1) * 256]
                    v.tensor_scalar(x, x, v1("rel_far", p * 2 + par), None, ALU.subtract).then_inc(rel_ok, 1)

                def maximum(p, t):
                    q0, qn, ke = tiles[t % nq]
                    v.wait_ge(s_full, p * U + (u0 + t + 1))
                    v.wait_ge(p_ok, p * U + (u0 + t + 1))
                    v.tensor_reduce(small[0:qn, t % 2:t % 2 + 1], PS[0:qn, t % 2, c0:c0 + ke], AX.X,
                                    ALU.max, negate=True).then_inc(nmax_ok, 1)

                def normalize(p, w):
                    _, qn, ke = tiles[w % nq]
                    v.wait_ge(p_ok, p * U + (u0 + w + 3))
                    r = small[0:qn, 4 + w % 2:5 + w % 2]
                    chain.done(v.reciprocal(r, small[0:qn, 2 + w % 2:3 + w % 2]))
                    chain.wait()
                    pb = ht(work, w % 2, S2)[0:qn, 0:ke]
                    v.tensor_scalar(pb, pb, r, None, ALU.mult).then_inc(pn_ok, 1)

                def weights(p, w):
                    i = w % nq
                    q0, qn, _ = tiles[i]
                    v.wait_ge(pt_hi, p * U + (u0 + w + 1))
                    nj = min(i + 1, 4)
                    po = 512 * (w % 2)
                    if i == 4:
                        o = slice(q0, q0 + qn)
                        v.tensor_tensor(ht(work_r, 3, S2)[0:META, o], PS[0:META, 2, po + 4 * qn:po + 5 * qn],
                                        ht(work_r, 2, S2)[0:META, o].bitcast(F32), ALU.subtract)
                    a, b = (x[:, :].rearrange("p (j t) -> p j t", t=T)[:, 0:nj, q0:q0 + qn]
                            for x in ((PT2_hi, PT2_lo) if mla else (PT_hi, PT_lo)))
                    v.tensor_tensor(b, PS[:, 2, po:po + nj * qn].rearrange("p (j t) -> p j t", t=qn),
                                    a.bitcast(F32), ALU.subtract).then_inc(pt_lo, 1)

                def take_out(p):
                    v.wait_ge(o_hi, p + (p0 + 1))
                    if mla:
                        v.tensor_tensor(OQ_lo[:, ds(p * (2 * S2), S2)], PS[:, 3, 256:256 + S2],
                                        OK_hi[:, ds(p * S2 + SHIFT, S2)].bitcast(F32), ALU.subtract)\
                            .then_inc(o_lo, 1)
                    else:
                        o = 8 if kind == "chunk" else 0
                        v.tensor_tensor(O_split[:, ds(p * S1 + ((o + 4) * S1 + SHIFT), S1)], PS[:, 3, 256:256 + S1],
                                        O_split[:, ds(p * S1 + (o * S1 + SHIFT), S1)].bitcast(F32), ALU.subtract)\
                            .then_inc(o_lo, 1)

                def run(before=None, after=None):
                    def step(p, t, first, last):
                        par, i = divmod(t, nq)
                        normalize(p, t)
                        if t + 1 < U:
                            maximum(p, t + 1)
                        elif not last:
                            maximum(p + 1, 0)
                        elif after is not None:
                            after["maximum"](0, 0)
                        if t:
                            weights(p, t - 1)
                        elif not first:
                            weights(p - 1, U - 1)
                        elif before is not None:
                            before["last_weights"]()
                        if i == 1:
                            if kind == "chunk" and par == 0:
                                far(p, 1)
                            elif kind == "chunk" and not last:
                                far(p + 1, 0)
                            elif par and last and after is not None:
                                after["far"](0, 0)
                        if t == 2 and not first:
                            take_out(p - 1)
                        elif t == 2 and before is not None:
                            before["last_out"]()

                    if before is None:
                        maximum(0, 0)
                    over_pairs(v, pairs, U, step, chain, U)
                    if after is None:
                        last_weights()
                        last_out()

                def last_weights():
                    weights(pairs - 1, U - 1)

                def last_out():
                    take_out(pairs - 1)

                return {"run": run, "maximum": maximum, "far": far, "last_weights": last_weights,
                        "last_out": last_out}

            fox, chunk = attention("fox"), attention("chunk")
            fox["run"](after=chunk)
            chunk["run"](before=fox)

            def take_merge(g):
                v.wait_ge(ml_ok, g * 4 + 4)
                for bi in (1, 3):
                    for m in range(4):
                        gm, am = gate[:, m * S1:(m + 1) * S1], acc[:, m * S1:(m + 1) * S1]
                        wait_out(v, "merge", bi - 1, m, g)
                        wait_tile(v, "merge", bi, m, g)
                        v.tensor_tensor(am if bi == 1 else gm, psum1(m), gm, ALU.mult)\
                            .then_inc(out_sem("merge", bi, m), 1)
                        if bi == 3:
                            wait_out(v, "merge", 3, m, g)
                            v.tensor_tensor(am, am, gm, ALU.add).then_inc(a_ok, 1)
                for m in range(4):
                    v.wait_ge(mh_ok, g * 4 + (m + 1))
                    o = (g * 4 + m) * S1
                    v.tensor_tensor(mg_lo[:, ds(o, S1)], acc[:, m * S1:(m + 1) * S1],
                                    mg_hi[:, ds(o, S1)].bitcast(F32), ALU.subtract).then_inc(ml_ok, 1)
            loop(2, 0, take_merge)

            def residual(name, part, x0):
                def body(g):
                    for m in range(4):
                        wait_tile(v, name, 0, m, g)
                        w = ht(work, m, S1)
                        c = part * 8 + g * 4 + m
                        v.tensor_scalar(w, psum1(m), modp[:, c:c + 1], None, ALU.mult)\
                            .then_inc(free[m], 1)
                        wait_out(v, name, 0, m, g)
                        x = x1(g * 4 + m)
                        v.scalar_tensor_tensor(x, x, ALPHA, w, ALU.mult, ALU.add).then_inc(x_ok, 1)
                body(0)
                v.wait_ge(x_ok, x0 + 4)
                s0, s1 = ht(m_out, 0), ht(m_out, 1)
                chain.done(v.tensor_tensor(s0, x1(0), x1(1), ALU.add))
                chain.done(v.tensor_tensor(s1, x1(2), x1(3), ALU.add))
                chain.wait()
                v.tensor_tensor(s0, s0, s1, ALU.add).then_inc(x4_ok, 1)
                body(1)

            def scaled_x():
                for k in range(KD):
                    v.tensor_tensor(x1(k), x1(k), RS[:, 0:S1], ALU.mult).then_inc(xr_ok, 1)

            def ffn(up, T, layer, y0, mid0):
                def body(g):
                    for j in range(2):
                        for tap in range(2):
                            for m in (2 * j, 2 * j + 1):
                                if tap == 0:
                                    v.wait_ge(y_ok, g * 4 + (y0 + m + 1))
                                elif m == 2 * j:
                                    chain.wait()
                                y, u = ht(work, m, T), psumT(m, T)
                                s = 1 + tap
                                w = v1("conv", g * 16 + (layer * 8 * KF + 4 * m + 1 - tap))
                                ins = v.scalar_tensor_tensor(y[:, s:], u[:, :T - s], w, y[:, s:], ALU.mult, ALU.add)
                                chain.done(ins) if tap == 0 else ins.then_inc(free[m], 1)
                    for j in range(2):
                        v.wait_ge(s_ok, g * 2 + (mid0 + j + 1))
                        wait_out(v, up, 0, 2 * j + 1, g)
                        y = ht(work, 2 * j + 1, T)
                        v.tensor_tensor(y, ht(work, 2 * j, T), y, ALU.mult).then_inc(mid_ok, 1)
                    for j in range(2):
                        v.wait_ge(midh_ok, g * 2 + (mid0 + j + 1))
                        o = (g * 2 + j) * S2
                        v.tensor_tensor(mid_lo[:, ds(o, T)], ht(work, 2 * j + 1, T),
                                        mid_hi[:, ds(o, T)].bitcast(F32), ALU.subtract).then_inc(midl_ok, 1)
                loop(11, 4, body)

            residual("out", 2, 0)
            norm(KD, S1, LN_EPS, x1, x1)
            scaled_x()
            norm(KD, S1, LN_EPS, x1, lambda k: ht(XC, k))
            split(KD, S1, over_deviation(lambda k: ht(XC, k)), hh, hl)
            ffn("up_a", S1, 0, 0, 0)
            residual("down_a", 5, 16)
            norm(KD, S1, LN_EPS, x1, x1)
            scaled_x()

            x2 = lambda k: ht(X, k, S2)
            h2, l2 = (lambda k: ht(H_hi, k, S2)), (lambda k: ht(H_lo, k, S2))

            def scaled(src, gain, i0):
                return lambda k, out: v.scalar_tensor_tensor(out, src(k), v1(gain, i0 + k), RS[:, :],
                                                             ALU.mult, ALU.mult)

            def add_four(n4):
                v.wait_ge(sq4_ok, 4 * n4)
                chain.done(v.tensor_tensor(RS[:, :], ht(work, 0, S2), ht(work, 1, S2), ALU.add))
                w = ht(work, 2, S2)
                chain.done(v.tensor_tensor(w, w, ht(work, 3, S2), ALU.add))
                chain.wait()
                v.tensor_tensor(RS[:, :], RS[:, :], w, ALU.add).then_inc(sum4_ok, 1)

            def post(gain, i0, x0):
                for k in range(KD):
                    w = ht(work, 2 + k % 2, S2)
                    if k >= 2:
                        v.wait_ge(x_ok, x0 + k - 1)
                    chain.done(v.scalar_tensor_tensor(w, ht(m_out, k, S2), v1(gain, i0 + k), RS[:, :],
                                                      ALU.mult, ALU.mult))
                    chain.wait()
                    v.tensor_tensor(x2(k), x2(k), w, ALU.add).then_inc(x_ok, 1)

            norm(KD, S2, RMS_EPS)
            split(KD, S2, scaled(x2, "mix_pre", 0), h2, l2)
            for t in (PT2_hi, PT2_lo):
                v.memset(t[:, :].bitcast(F32), 0.0).then_inc(zero_ok, 1)
            for bi, m, dst in [(0, i, ht(Q2, i, S2)) for i in range(4)] + [(1, 0, ht(Q2, 4, S2)), (1, 1, kr[:, :])]:
                wait_tile(v, "dqkv", bi, m)
                v.tensor_copy(dst, psum2(m)).then_inc(out_sem("dqkv", bi, m), 1)
            v.wait_ge(tab_in, 32)
            wait_out(v, "dqkv", 1, 1)
            swap = [(i + ROPE // 2) % ROPE for i in range(ROPE)]
            for r in (slice(32, 64), slice(64, 96)):
                w = ht(K2, 0, S2)[r, :]
                chain.done(v.stream_shuffle(w, kr[r, :], swap))
                chain.wait()
                chain.done(v.tensor_tensor(w, w, sin_t[r, :], ALU.mult))
                chain.done(v.tensor_tensor(kr[r, :], kr[r, :], cos_t[r, :], ALU.mult))
                chain.wait()
                v.tensor_tensor(kr[r, :], kr[r, :], w, ALU.add).then_inc(kr_ok, 1)
            for t in (c_hi, c_lo):
                chain.done(v.memset(t[:, 5 * S2:].bitcast(F32), 0.0))
            norm(3, S2, RMS_EPS)
            split(3, S2, scaled(lambda k: ht(Q2, k, S2), "q_norm", 0), lambda k: ht(c_hi, k, S2),
                  lambda k: ht(c_lo, k, S2))
            norm(2, S2, RMS_EPS)
            split(2, S2, scaled(lambda k: ht(Q2, 3 + k, S2), "kv_norm", 0), lambda k: ht(c_hi, 3 + k, S2),
                  lambda k: ht(c_lo, 3 + k, S2))

            def take_uq(g):
                s = (NOPE + ROPE) ** -0.5
                for bi in range(4):
                    for j in range(2):
                        m = BATCH["uq"][bi][2] + j
                        r = slice(64, 96) if j == 0 else slice(32, 64)
                        q = Q2[r, ds((g * 8 + (2 * bi + j)) * S2, S2)]
                        w = ht(work, j, S2)[r, :]
                        v.wait_ge(rq_ok, g * 8 + (2 * bi + j + 1))
                        v.wait_ge(q_ok, g * 8 + (2 * bi + j + 1))
                        chain.done(v.scalar_tensor_tensor(q, PS[r, m, COL2:COL2 + S2], s, cos_t[r, :], ALU.mult,
                                                          ALU.mult))
                        v.stream_shuffle(w, PS[r, m, COL2:COL2 + S2], swap).then_inc(out_sem("uq", bi, j), 1)
                        wait_out(v, "uq", bi, j, g)
                        v.scalar_tensor_tensor(w, w, s, sin_t[r, :], ALU.mult, ALU.mult).then_inc(rw_ok, 1)
            v.wait_ge(h_ok, cnt_["hi"])
            loop(2, 8, take_uq)
            chain.wait()
            for bi in range(2):
                for t in range(5):
                    wait_tile(v, "uv", bi, t)
                    o = t * D + bi * 512
                    v.tensor_copy(v_raw2[:, o:o + 512], PS[:, t % 4, 0:512]).then_inc(out_sem("uv", bi, t), 1)
            for t in (k2_hi, k2_lo, v2_hi, v2_lo):
                v.memset(t[:, :].bitcast(F32), 0.0).then_inc(zero_ok, 1)
            attention("mla")["run"]()
            add_four(1)
            norm(KD, S2, RMS_EPS)
            post("mix_post", 0, 32)
            norm(KD, S2, RMS_EPS)
            split(KD, S2, scaled(x2, "ffn_pre", 0), h2, l2)
            ffn("up_b", S2, 1, 44, KF)
            add_four(2)
            norm(KD, S2, RMS_EPS)
            post("ffn_post", 0, 40)
            norm(KD, S2, RMS_EPS)

            a0_, a1_, s0_, s1_ = (t[:, i:i + PADDED] for t in (pool_a, pool_s) for i in (0, PADDED))
            for t in (a0_, a1_, s0_, s1_):
                chain.done(v.memset(t[:, 0:16], 0.0))
            chain.wait()

            def pooled(k, out):
                w = POOLS[k // 2]
                a_, c_ = (a0_, a1_)[k % 2], pool_c[:, k % 2 * 16:k % 2 * 16 + 16]
                chain.done(v.scalar_tensor_tensor(a_[:, 16:], x2(k), v1("mix_pre", KD + k), RS[:, :], ALU.mult,
                                                  ALU.mult))
                s, step = a_, 1
                while step < w:
                    chain.wait()
                    n = s1_ if s is s0_ else s0_
                    chain.done(v.tensor_tensor(n[:, 16:], s[:, 16:], s[:, 16 - step:PADDED - step], ALU.add))
                    s = n
                    step *= 2
                chain.wait()
                i = VEC["cnt"] + 16 * (k // 2)
                chain.done(v.tensor_tensor(c_, s[:, 16:32], vec[:, i:i + 16], ALU.mult))
                chain.done(v.scalar_tensor_tensor(out[:, 16:], s[:, 32:], 1.0 / w, a_[:, 32:], ALU.mult,
                                                  ALU.subtract))
                chain.wait()
                return v.tensor_tensor(out[:, 0:16], c_, a_[:, 16:32], ALU.subtract)

            split(KD, S2, pooled, h2, l2)
            add_four(3)
            norm(KD, S2, RMS_EPS)
            post("mix_post", KD, 48)
            norm(KD, S2, RMS_EPS)
            split(KD, S2, scaled(x2, "ffn_pre", KD), h2, l2)
            ffn("up_c", S2, 2, 88, 2 * KF)
            add_four(4)
            norm(KD, S2, RMS_EPS)
            post("ffn_post", KD, 56)


def rows(a):
    return a.reshape(-1, P, a.shape[-1])


def columns(a):
    return a.reshape(-1, P).T


def weight_stream(np, w):
    out = np.zeros((NSTREAM, P, BLK), np.float32)
    at = [0]

    def put(block):
        flat = block.transpose(1, 0, 2).reshape(P, -1)
        out[at[0], :, :flat.shape[1]] = flat
        at[0] += 1

    def cut(m, c0, width, kk=2):
        m = rows(m[:, c0:c0 + width])
        for k in range(0, m.shape[0], kk):
            put(m[k:k + kk])

    w_in = w["w_in"][0]
    put(rows(w_in[:, 1536:1536 + P]))
    for c in (0, 512, 1544, 2056, 1024, 2568):
        cut(w_in, c, 512)
    for g in range(2):
        cut(w_in, 3080 + 512 * g, 512)
        cut(w["w_br_fox"][0], 512 * g, 512)
        cut(w_in, 4104 + 512 * g, 512)
        cut(w["w_br_chunk"][0], 512 * g, 512)
    for g in range(2):
        cut(w["w_out"][0], 512 * g, 512)

    def ffn(up, down):
        a, b = (up[:, i * FF:(i + 1) * FF].reshape(D, KF, P) for i in range(2))
        both = np.stack([a, b], 2).reshape(D, 2 * FF)
        for g in range(11):
            cut(both, 512 * g, 512)
        for g in range(2):
            m, k = rows(down[:, 512 * g:512 * (g + 1)]), 0
            for n in DOWN_ROWS:
                put(m[k:k + n])
                k += n

    ffn(w["w_up"][0], w["w_down"][0])
    m = w["mla_w_dqkv_2"][0]
    cut(m, 0, 512)
    z = np.zeros((D, ROPE), np.float32)
    rope = m[:, RQ + RKV:]
    cut(np.concatenate([m[:, 512:640], z, rope, rope, z], 1), 0, 256, 4)
    m = w["mla_w_uq_2"][0].reshape(RQ, H2, NOPE + ROPE)
    z = np.zeros((RQ, ROPE), np.float32)
    for h in range(0, H2, 2):
        cut(np.concatenate([m[:, h], z, z, m[:, h + 1, NOPE:], m[:, h + 1, :NOPE]], 1), 0, 256, 3)
    m = w["mla_w_ukv_2"][0].reshape(RKV, H2, 2, NOPE)
    for part in range(2):
        for g in range(2):
            cut(m[:, 8 * g:8 * g + 8, part].reshape(RKV, 512), 0, 512)
    for g in range(2):
        cut(w["mla_w_o_2"][0], 512 * g, 512)
    ffn(w["ffn_w_up_2"][0], w["ffn_w_down_2"][0])
    m = w["pool_w_group_2"][0]
    for g in range(0, 4, 2):
        put(rows(m[g:g + 2].reshape(512, 256)))
    ffn(w["ffn_w_up_2"][1], w["ffn_w_down_2"][1])
    assert at[0] == NBLK, (at[0], NBLK)
    return out


def vector_table(np, w):
    t = np.zeros((P, NVEC), np.float32)

    def put(name, cols):
        t[:, VEC[name]:VEC[name] + cols.shape[1]] = cols

    put("c", columns(w["c"]))
    for name in ("b_ada", "ln1_g", "ln1_b", "ln2_g", "ln2_b"):
        put(name, columns(w[name]))
    t[0:8, VEC["b_f"]] = w["b_f"][0]
    put("qk_scale", np.broadcast_to(np.array([[0.125, 1.0, 0.125, 1.0]], np.float32), (P, 4)))
    put("rel_far", np.broadcast_to(w["rel_bias"][0][:, 256][None], (P, 8)))
    r = np.arange(P)[:, None]
    put("sel", ((r < 96) & (r % 32 == np.arange(8)[None])).astype(np.float32))
    for name, src in (("mix_pre", "norm_mix_pre_2"), ("mix_post", "norm_mix_post_2"),
                      ("ffn_pre", "norm_ffn_pre_2"), ("ffn_post", "norm_ffn_post_2"),
                      ("q_norm", "mla_q_norm_2"), ("kv_norm", "mla_kv_norm_2"), ("pool_scale", "pool_scale_2")):
        put(name, columns(w[src]))
    put("eps", np.broadcast_to(np.array([[LN_EPS, RMS_EPS]], np.float32), (P, 2)))
    put("cnt", np.broadcast_to(np.concatenate(
        [1.0 / np.minimum(np.arange(16) + 1, n) for n in POOLS]).astype(np.float32)[None], (P, 64)))
    layers = [(w["conv_w"][0], w["conv_b"][0])]
    layers += [(w["ffn_conv_w_2"][i], w["ffn_conv_b_2"][i]) for i in range(2)]
    conv = []
    for taps, bias in layers:
        a = np.concatenate([taps, bias[None]], 0).reshape(4, 2, KF, P)
        conv.append(a.transpose(3, 2, 1, 0).reshape(P, -1))
    put("conv", np.concatenate(conv, 1))
    return t


def kernel(**inputs):
    import numpy as np
    import concourse.bacc as bacc
    from concourse.bass_utils import run_bass_kernel_spmd

    w = {k: np.asarray(v) for k, v in inputs.items()}
    q, s = np.arange(P)[:, None], np.arange(P)[None]
    neg = np.float32(-3e38)
    consts = np.concatenate([np.eye(P), np.where(s <= q, 0, neg), np.where((q < 64) & (s >= 64), neg, 0)], 1)
    far = np.clip(P + q - np.arange(2 * P)[None], -P, P) + P
    period = 10000.0 ** (np.arange(0, ROPE, 2, dtype=np.float32) / ROPE)
    pos = np.arange(S2, dtype=np.float32)[None] / period[:, None]
    turn = np.zeros((2, P, S2), np.float32)
    for r in (32, 64):
        turn[0, r:r + ROPE] = np.concatenate([np.cos(pos), np.cos(pos)])
        turn[1, r:r + ROPE] = np.concatenate([-np.sin(pos), np.sin(pos)])
    arrays = {
        "xT": np.ascontiguousarray(w["x"][0].T).reshape(KD, P, S1),
        "meta": np.ascontiguousarray(w["meta_tokens_2"].T).reshape(KD, P, META),
        "stream": weight_stream(np, w),
        "ada": np.concatenate([rows(w["w_ada"][0][:, part * D:(part + 1) * D]) for part in ADA_ORDER]),
        "vecs": vector_table(np, w),
        "consts": consts.astype(np.float32),
        "rel": np.ascontiguousarray(w["rel_bias"][0][:, far]),
        "rope": turn,
    }
    nc = bacc.Bacc("TRN2", target_bir_lowering=False, num_devices=1)
    args = {n: nc.dram_tensor(n, a.shape, mybir.dt.from_np(a.dtype), kind="ExternalInput").ap()
            for n, a in arrays.items()}
    yT = nc.dram_tensor("yT", (KD, P, S1), F32, kind="ExternalOutput").ap()
    program(nc, yT=yT, **args)
    got = run_bass_kernel_spmd(nc, [arrays], core_ids=[0]).results[0]["yT"]
    return np.ascontiguousarray(got.reshape(D, S1).T)[None]
```
